# Optimizing a Trainium2 kernel written in Bass

```python
import jax, jax.numpy as jnp
from jax import lax
import numpy as np

D_MODEL = 1024
BATCH = 1
SEQ = 1024
DEPTH = 1

MIX_WIDTH = D_MODEL
ATTN_HEADS = 8
HEAD_DIM = 64
ATTN_WIDTH = ATTN_HEADS * HEAD_DIM
CONV_WIDTH = MIX_WIDTH - ATTN_WIDTH
CONV_KERNEL = 31
IN_COLS = 3 * ATTN_WIDTH + 2 * CONV_WIDTH
Q_BLOCK = 128

PEER_HEADS = 8
PEER_KEY_DIM = 128
PEER_HALF = PEER_KEY_DIM // 2
N_KEYS = 128
N_EXPERTS = N_KEYS * N_KEYS
PEER_TOPK = 16
PEER_CHUNK = 128

EPS = 1e-6

kernel_name = "hymba_sbattn_conformer_peer"

def rms_norm(x, g):
    xf = x.astype(jnp.float32)
    y = xf * lax.rsqrt(jnp.mean(xf * xf, axis=-1, keepdims=True) + EPS)
    return (y * g.astype(jnp.float32)).astype(x.dtype)

def layer_norm(x, g, b):
    xf = x.astype(jnp.float32)
    mu = jnp.mean(xf, axis=-1, keepdims=True)
    xc = xf - mu
    var = jnp.mean(xc * xc, axis=-1, keepdims=True)
    y = xc * lax.rsqrt(var + EPS) * g.astype(jnp.float32) + b.astype(jnp.float32)
    return y.astype(x.dtype)

def stick_breaking_attention(q, k, v):
    B, H, S, hd = q.shape
    qf, kf, vf = q.astype(jnp.float32), k.astype(jnp.float32), v.astype(jnp.float32)
    scale = hd ** -0.5
    key_pos = jnp.arange(S)
    n_blocks = S // Q_BLOCK

    def block(i):
        start = i * Q_BLOCK
        qb = lax.dynamic_slice_in_dim(qf, start, Q_BLOCK, axis=2)
        z = jnp.einsum('bhqd,bhkd->bhqk', qb, kf) * scale
        q_pos = start + jnp.arange(Q_BLOCK)
        mask = key_pos[None, :] < q_pos[:, None]
        log_keep = jnp.where(mask, jax.nn.log_sigmoid(-z), 0.0)
        later = lax.cumsum(log_keep, axis=3, reverse=True) - log_keep
        att = jnp.where(mask, jnp.exp(jax.nn.log_sigmoid(z) + later), 0.0)
        return jnp.einsum('bhqk,bhkd->bhqd', att, vf)

    out = lax.map(block, jnp.arange(n_blocks))
    out = out.transpose(1, 2, 0, 3, 4).reshape(B, H, S, hd)
    return out.astype(q.dtype)

def conformer_conv(u, conv_w, conv_b, ln_g, ln_b):
    a, gate = jnp.split(u, 2, axis=-1)
    h = a * jax.nn.sigmoid(gate)
    h = lax.conv_general_dilated(
        h, conv_w[:, None, :], window_strides=(1,),
        padding=[(CONV_KERNEL - 1, 0)],
        dimension_numbers=('NWC', 'WIO', 'NWC'),
        feature_group_count=CONV_WIDTH) + conv_b
    h = layer_norm(h, ln_g, ln_b)
    return jax.nn.silu(h)

def hybrid_mixer(x, norm_g, w_in, q_norm_g, k_norm_g, attn_out_g, conv_w, conv_b,
                 conv_ln_g, conv_ln_b, w_out):
    B, S, _ = x.shape
    xn = rms_norm(x, norm_g)
    proj = jnp.einsum('bsd,de->bse', xn, w_in)
    q, k, v, c = jnp.split(proj, [ATTN_WIDTH, 2 * ATTN_WIDTH, 3 * ATTN_WIDTH], axis=-1)
    q = rms_norm(q.reshape(B, S, ATTN_HEADS, HEAD_DIM), q_norm_g).transpose(0, 2, 1, 3)
    k = rms_norm(k.reshape(B, S, ATTN_HEADS, HEAD_DIM), k_norm_g).transpose(0, 2, 1, 3)
    v = v.reshape(B, S, ATTN_HEADS, HEAD_DIM).transpose(0, 2, 1, 3)
    o_attn = stick_breaking_attention(q, k, v).transpose(0, 2, 1, 3).reshape(B, S, ATTN_WIDTH)
    o_attn = rms_norm(o_attn, attn_out_g)
    o_conv = conformer_conv(c, conv_w, conv_b, conv_ln_g, conv_ln_b)
    mixed = jnp.concatenate([o_attn, o_conv], axis=-1)
    return x + jnp.einsum('bse,ed->bsd', mixed, w_out)

def peer_ffn(xn, wq, sub_k1, sub_k2, u_tab, v_tab):
    B, S, D = xn.shape
    xt = xn.reshape(-1, PEER_CHUNK, D)
    k1 = sub_k1.astype(jnp.float32)
    k2 = sub_k2.astype(jnp.float32)

    def chunk(xc):
        qh = jnp.einsum('cd,de->ce', xc, wq).reshape(-1, PEER_HEADS, PEER_KEY_DIM).astype(jnp.float32)
        s1 = jnp.einsum('chd,hnd->chn', qh[..., :PEER_HALF], k1)
        s2 = jnp.einsum('chd,hnd->chn', qh[..., PEER_HALF:], k2)
        v1, i1 = lax.top_k(s1, PEER_TOPK)
        v2, i2 = lax.top_k(s2, PEER_TOPK)
        cand = (v1[..., :, None] + v2[..., None, :]).reshape(-1, PEER_HEADS, PEER_TOPK * PEER_TOPK)
        cidx = (i1[..., :, None] * N_KEYS + i2[..., None, :]).reshape(-1, PEER_HEADS, PEER_TOPK * PEER_TOPK)
        top_s, pos = lax.top_k(cand, PEER_TOPK)
        experts = jnp.take_along_axis(cidx, pos, axis=-1)
        gates = jax.nn.softmax(top_s, axis=-1)
        u_sel = u_tab[experts]
        act = jax.nn.gelu(jnp.einsum('chkd,cd->chk', u_sel, xc).astype(jnp.float32), approximate=False)
        w = (gates * act).astype(xc.dtype)
        v_sel = v_tab[experts]
        return jnp.einsum('chk,chkd->cd', w, v_sel)

    y = lax.map(chunk, xt)
    return y.reshape(B, S, D)

def setup_inputs(seed: int = 0) -> dict:
    key = jax.random.key(seed)
    ks = jax.random.split(key, 16)
    f32 = jnp.float32
    n = lambda k, shape, s: (jax.random.normal(k, shape, f32) * s)
    gain = lambda k, shape: 1.0 + 0.01 * jax.random.normal(k, shape, f32)
    return {
        "x": jax.random.normal(ks[0], (BATCH, SEQ, D_MODEL), f32),
        "norm_mix_g": gain(ks[1], (DEPTH, D_MODEL)),
        "w_in": n(ks[2], (DEPTH, D_MODEL, IN_COLS), D_MODEL ** -0.5),
        "q_norm_g": gain(ks[3], (DEPTH, HEAD_DIM)),
        "k_norm_g": gain(ks[4], (DEPTH, HEAD_DIM)),
        "attn_out_g": gain(ks[5], (DEPTH, ATTN_WIDTH)),
        "conv_w": n(ks[6], (DEPTH, CONV_KERNEL, CONV_WIDTH), CONV_KERNEL ** -0.5),
        "conv_b": n(ks[7], (DEPTH, CONV_WIDTH), 0.01),
        "conv_ln_g": gain(ks[8], (DEPTH, CONV_WIDTH)),
        "conv_ln_b": n(ks[9], (DEPTH, CONV_WIDTH), 0.01),
        "w_out": n(ks[10], (DEPTH, MIX_WIDTH, D_MODEL), MIX_WIDTH ** -0.5),
        "norm_ffn_g": gain(ks[11], (DEPTH, D_MODEL)),
        "peer_wq": n(ks[12], (DEPTH, D_MODEL, PEER_HEADS * PEER_KEY_DIM), D_MODEL ** -0.5),
        "peer_k1": n(ks[13], (DEPTH, PEER_HEADS, N_KEYS, PEER_HALF), PEER_HALF ** -0.5),
        "peer_k2": n(ks[14], (DEPTH, PEER_HEADS, N_KEYS, PEER_HALF), PEER_HALF ** -0.5),
        "peer_u": n(jax.random.fold_in(ks[15], 0), (DEPTH, N_EXPERTS, D_MODEL), D_MODEL ** -0.5),
        "peer_v": n(jax.random.fold_in(ks[15], 1), (DEPTH, N_EXPERTS, D_MODEL), PEER_HEADS ** -0.5),
    }

def reference(x, norm_mix_g, w_in, q_norm_g, k_norm_g, attn_out_g, conv_w, conv_b,
              conv_ln_g, conv_ln_b, w_out, norm_ffn_g, peer_wq, peer_k1, peer_k2,
              peer_u, peer_v):
    h = x
    for l in range(DEPTH):
        h = hybrid_mixer(h, norm_mix_g[l], w_in[l], q_norm_g[l], k_norm_g[l], attn_out_g[l],
                         conv_w[l], conv_b[l], conv_ln_g[l], conv_ln_b[l], w_out[l])
        h = h + peer_ffn(rms_norm(h, norm_ffn_g[l]), peer_wq[l], peer_k1[l], peer_k2[l],
                         peer_u[l], peer_v[l])
    return h


_drawn_inputs = setup_inputs


def setup_inputs(seed=0):
    import zlib

    import numpy as np

    out = dict(_drawn_inputs(seed))
    spreads = {}
    factors = {'norm_mix_g': 3.718,
     'q_norm_g': 6.516,
     'k_norm_g': 7.229,
     'attn_out_g': 23.767,
     'conv_b': 13.901,
     'conv_ln_g': 33.823,
     'conv_ln_b': 34.447,
     'norm_ffn_g': 21.361}
    for name, (base, spread) in spreads.items():
        noise = np.random.default_rng([zlib.crc32(name.encode()), seed]).standard_normal(out[name].shape)
        drawn = base * np.exp(spread * noise) if base else spread * noise
        out[name] = __import__('jax').numpy.asarray(drawn.astype(out[name].dtype))
    for name, factor in factors.items():
        out[name] = (out[name] * factor).astype(out[name].dtype)
    return out
```

```python
import numpy as np
import concourse.bass as bass
from concourse import mybir

F32 = mybir.dt.float32
BF16 = mybir.dt.bfloat16
I32 = mybir.dt.int32
U32 = mybir.dt.uint32
ALU = mybir.AluOpType
ACT = mybir.ActivationFunctionType
AXX = mybir.AxisListType.X

P = 128
SEQ, D = 1024, 1024
CHUNKS = SEQ // P
KT_D = D // P
HEADS, HD = 8, 64
AW = HEADS * HD
CW = D - AW
AB = AW // P
CB = CW // P
TAPS = 31
HALO = TAPS - 1
COLS = 3 * AW + 2 * CW
BANK = 512
PH, TOPK, NKEYS = 8, 16, 128
HALF = 64
ROWS = PH * TOPK
EPS = 1e-6
NEG = -1.0e30
LOWEST = -3.0e38
RING = 8
MASK_SPAN = SEQ - P


def spread(view, dims):
    return bass.AP(view.tensor, view.offset, [list(view.ap[0])] + [list(d) for d in dims])


def hold(eng, sem, value, passed):
    eng.wait_ge(sem, value)
    eng.sem_inc(passed, 1)


class Map:

    def __init__(self, nc, start):
        self.nc, self.at = nc, (start + 31) // 32 * 32

    def tile(self, name, shape, dt):
        size = int(np.prod(shape[1:])) * (2 if dt == BF16 else 4)
        t = self.nc.alloc_sbuf_tensor_at(name, list(shape), dt, offset=self.at)
        self.at += (size + 31) // 32 * 32
        return t


def build(nc, x, norm_mix_g, w_in, q_norm_g, k_norm_g, attn_out_g, conv_w, conv_b, conv_ln_g,
          conv_ln_b, w_out, norm_ffn_g, peer_wq, peer_k1, peer_k2, peer_u, peer_v, out):
    keep = Map(nc, nc.sbuf_base)
    ident = keep.tile("ident", [P, P], F32)
    ident_b = keep.tile("ident_b", [P, P], BF16)
    mask_band = keep.tile("mask_band", [P, MASK_SPAN + SEQ], BF16)
    kT = keep.tile("kT", [P, AB, SEQ], F32)
    vals = keep.tile("vals", [P, CHUNKS, AW], F32)
    keys_bd = keep.tile("keys_bd", [P, PH, 2 * NKEYS], F32)
    NVEC = KT_D + 4 * CB + 2
    vec = keep.tile("vec", [P, NVEC], F32)
    iota16 = keep.tile("iota16", [P, TOPK], F32)
    g_mix = vec[:, 0:KT_D]
    g_attn = vec[:, KT_D:KT_D + AB]
    b_conv = vec[:, KT_D + AB:KT_D + 2 * AB]
    g_ln = vec[:, KT_D + 2 * AB:KT_D + 3 * AB]
    b_ln = vec[:, KT_D + 3 * AB:KT_D + 4 * AB]
    g_q = vec[:, NVEC - 2:NVEC - 1]
    g_k = vec[:, NVEC - 1:NVEC]

    qT_spill = nc.dram_tensor("qT_spill", [CHUNKS, P, AW], F32, kind="Internal").ap()
    cT_spill = nc.dram_tensor("cT_spill", [CHUNKS, P, CW], F32, kind="Internal").ap()
    psum = nc.alloc_psum_tensor("psum", [P, 8, BANK], F32)

    phase0(nc, keep.at, psum, ident, ident_b, mask_band, kT, vals, keys_bd, vec, iota16, g_mix,
           b_conv, g_ln, b_ln, g_q, g_k, qT_spill, cT_spill, x, norm_mix_g, w_in, q_norm_g,
           k_norm_g, attn_out_g, conv_w, conv_b, conv_ln_g, conv_ln_b, peer_k1, peer_k2)
    phase1(nc, keep.at, psum, ident, ident_b, mask_band, kT, vals, keys_bd, iota16, g_attn,
           qT_spill, cT_spill, x, w_out, norm_ffn_g, peer_wq, peer_u, peer_v, out)


def phase0(nc, base, psum, ident, ident_b, mask_band, kT, vals, keys_bd, vec, iota16, g_mix,
           b_conv, g_ln, b_ln, g_q, g_k, qT_spill, cT_spill, x, norm_mix_g, w_in, q_norm_g,
           k_norm_g, attn_out_g, conv_w, conv_b, conv_ln_g, conv_ln_b, peer_k1, peer_k2):
    m = Map(nc, base)
    GROUPS = COLS // BANK
    Q, K, V, A, G = range(GROUPS)
    ORDER = (Q, K, A, G, V)
    w_sb = m.tile("w_sb", [P, GROUPS, KT_D, BANK], F32)
    x_in = m.tile("x_in", [P, D], F32)
    xn = m.tile("xn", [P, D], F32)
    xnT = m.tile("xnT", [P, KT_D, P], F32)
    squares = m.tile("squares", [P, 2 * AW], F32)
    qn = m.tile("qn", [P, AW], F32)
    kn = m.tile("kn", [P, AW], F32)
    qT_out = m.tile("qT_out", [P, AW], F32)
    sig = m.tile("sig", [P, CW], F32)
    glu = m.tile("glu", [P, CW], F32)
    conv_in = m.tile("conv_in", [P, CB, HALO + P], F32)
    acc = m.tile("acc", [P, CB, P], F32)
    cn = m.tile("cn", [P, CW], F32)
    cT_out = m.tile("cT_out", [P, CW], F32)
    rows = m.tile("rows", [P, P], F32)
    taps_row = m.tile("taps_row", [TAPS, CW], F32)
    taps = m.tile("taps", [P, CB, TAPS], F32)
    keys = m.tile("keys", [P, PH, 2, HALF], F32)
    x_stat = m.tile("x_stat", [P, 4], F32)
    qk_stat = m.tile("qk_stat", [P, 4, 2 * HEADS], F32)
    bn = m.tile("bn", [P, 6], F32)
    ln_stat = m.tile("ln_stat", [P, 8], F32)
    assert m.at <= nc.sbuf_usable_end
    NVEC = vec.shape[1]

    ps = [psum[:, g, :] for g in range(GROUPS)]
    tA, tB, tC = psum[:, 5, :], psum[:, 6, :], psum[:, 7, :]

    sem = nc.alloc_semaphore
    small_in, w_loaded = sem("small_in"), [sem(f"w_loaded{g}") for g in range(GROUPS)]
    x_loaded, consts, zeroed, setup_T, setup_copied = (
        sem("x_loaded"), sem("consts"), sem("zeroed"), sem("setup_T"), sem("setup_copied"))
    x_squared, x_meaned, x_rooted, x_recip, x_normed = (
        sem("x_squared"), sem("x_meaned"), sem("x_rooted"), sem("x_recip"), sem("x_normed"))
    xT_ready, xT_copied = sem("xT_ready"), sem("xT_copied")
    projected = [sem(f"projected{g}") for g in range(GROUPS)]
    qk_squared, qk_summed, qk_meaned, qk_rooted, qk_recip, q_normed, k_normed = (
        sem("qk_squared"), sem("qk_summed"), sem("qk_meaned"), sem("qk_rooted"), sem("qk_recip"),
        sem("q_normed"), sem("k_normed"))
    qT_ready, kT_ready, hT_ready = sem("qT_ready"), sem("kT_ready"), sem("hT_ready")
    qT_copied, kT_copied, hT_copied, v_copied = (
        sem("qT_copied"), sem("kT_copied"), sem("hT_copied"), sem("v_copied"))
    gated, glu_done, tapped, halo_moved = (
        sem("gated"), sem("glu_done"), sem("tapped"), sem("halo_moved"))
    conv_T, bn_done, ln_done, ln_eps, ln_rooted, ln_recip, cn_done, cT_ready, swished = (
        sem("conv_T"), sem("bn_done"), sem("ln_done"), sem("ln_eps"), sem("ln_rooted"),
        sem("ln_recip"), sem("cn_done"), sem("cT_ready"), sem("swished"))
    qT_stored, cT_stored, dve_passed = sem("qT_stored"), sem("cT_stored"), sem("dve_passed0")
    NSMALL = 10
    TAP_OPS = TAPS * CB

    with nc.Block() as block:

        @block.sync
        def _(sp):
            r = 0
            for v, n in ((norm_mix_g, KT_D), (attn_out_g, AB), (conv_b, CB), (conv_ln_g, CB),
                         (conv_ln_b, CB)):
                sp.dma_start(rows[r:r + n, :], v[0, :].rearrange("(n p) -> n p", p=P)).then_inc(small_in, 16)
                r += n
            for v in (q_norm_g, k_norm_g):
                sp.dma_start(rows[r:r + 1, :].rearrange("o (two d) -> o two d", two=2),
                             v[0:1, :].unsqueeze(1).to_broadcast([1, 2, HD])).then_inc(small_in, 16)
                r += 1
            sp.dma_start(taps_row[:, :], conv_w[0, :, :]).then_inc(small_in, 16)
            for n, k in enumerate((peer_k1, peer_k2)):
                sp.dma_start(keys[:, :, n, :], k[0].rearrange("h n d -> n h d")).then_inc(small_in, 16)
            sp.dma_start(x_in[:, :], x[0, 0:P, :]).then_inc(x_loaded, 16)
            for g in ORDER:
                sp.dma_start(w_sb[:, g, :, :], w_in[0, :, g * BANK:(g + 1) * BANK]
                             .rearrange("(k p) n -> p k n", p=P)).then_inc(w_loaded[g], 16)

            def next_x(i):
                sp.wait_ge(x_normed, i + 1)
                sp.dma_start(x_in[:, :], x[0, bass.ds((i + 1) * P, P), :]).then_inc(x_loaded, 16)

            def store_q(i):
                sp.wait_ge(qT_copied, i + 1)
                sp.dma_start(qT_spill[bass.ds(i, 1), :, :].rearrange("o p n -> (o p) n"),
                             qT_out[:, :]).then_inc(qT_stored, 16)

            def store_c(i):
                sp.wait_ge(swished, CB * (i + 1))
                sp.dma_start(cT_spill[bass.ds(i, 1), :, :].rearrange("o p n -> (o p) n"),
                             cT_out[:, :]).then_inc(cT_stored, 16)

            next_x(0)
            store_q(0)
            with sp.Fori(1, CHUNKS - 1) as i:
                next_x(i)
                store_c(i - 1)
                store_q(i)
            store_c(CHUNKS - 2)
            store_q(CHUNKS - 1)
            store_c(CHUNKS - 1)
            sp.wait_ge(qT_stored, 16 * CHUNKS)
            sp.wait_ge(cT_stored, 16 * CHUNKS)

        @block.gpsimd
        def _(pool):
            nc.gpsimd.memset(ident[:, :], 0.0).then_inc(zeroed, 1)
            nc.gpsimd.memset(mask_band[:, :], 0.0).then_inc(zeroed, 1)
            pool.wait_ge(zeroed, 2)
            nc.gpsimd.affine_select(out=ident[:, :], in_=ident[:, :], compare_op=ALU.not_equal, fill=1.0,
                                    base=0, pattern=[[-1, P]], channel_multiplier=1).then_inc(consts, 1)
            nc.gpsimd.affine_select(out=mask_band[:, :], in_=mask_band[:, :], compare_op=ALU.is_gt, fill=NEG,
                                    base=MASK_SPAN, pattern=[[-1, MASK_SPAN + SEQ]],
                                    channel_multiplier=1).then_inc(consts, 1)
            nc.gpsimd.iota(iota16[:, :], pattern=[[1, TOPK]], base=0, channel_multiplier=0,
                           allow_small_or_imprecise_dtypes=True).then_inc(consts, 1)
            pool.wait_ge(consts, 3)
            nc.gpsimd.tensor_copy(ident_b[:, :], ident[:, :]).then_inc(consts, 1)
            nc.gpsimd.memset(kT[:, :, :], 0.0).then_inc(zeroed, 1)
            nc.gpsimd.memset(vals[:, :, :], 0.0).then_inc(zeroed, 1)
            nc.gpsimd.memset(keys_bd[:, :, :], 0.0).then_inc(zeroed, 1)
            nc.gpsimd.memset(conv_in[:, :, :], 0.0).then_inc(zeroed, 1)

        @block.tensor
        def _(pe):
            pe.wait_ge(consts, 4)
            pe.wait_ge(small_in, 16 * NSMALL)
            nc.tensor.transpose(tC[:, 0:NVEC], rows[0:NVEC, :], ident[0:NVEC, 0:NVEC])
            for c in range(CB):
                last = nc.tensor.transpose(tC[:, P + c * 32:P + c * 32 + TAPS],
                                           taps_row[:, c * P:(c + 1) * P], ident[0:TAPS, 0:TAPS])
            for h in range(PH):
                t = (tA, tB)[h // 4]
                last = nc.tensor.transpose(t[:, (h % 4) * P:(h % 4 + 1) * P],
                                           keys[:, h, :, :].rearrange("p a d -> p (a d)"), ident[:, :])
            last.then_inc(setup_T, 1)

            def transpose_x(i):
                pe.wait_ge(x_normed, i + 1)
                pe.wait_ge(setup_copied, 4)
                if not isinstance(i, int) or i:
                    pe.wait_ge(hT_copied, i)
                    pe.wait_ge(kT_copied, i)
                for k in range(KT_D):
                    last = nc.tensor.transpose((tA, tB)[k // 4][:, (k % 4) * P:(k % 4 + 1) * P],
                                               xn[:, k * P:(k + 1) * P], ident[:, :])
                    if k % 4 == 3:
                        last.then_inc(xT_ready, 1)

            def project(i, g):
                if isinstance(i, int) and i == 0:
                    pe.wait_ge(w_loaded[g], 16)
                else:
                    readers = {Q: (q_normed, i), K: (k_normed, i), V: (v_copied, i),
                               A: (glu_done, i), G: (gated, i)}
                    pe.wait_ge(*readers[g])
                for k in range(KT_D):
                    if g == Q:
                        pe.wait_ge(xT_copied, KT_D * i + k + 1)
                    last = nc.tensor.matmul(ps[g], xnT[:, k, :], w_sb[:, g, k, :],
                                            start=k == 0, stop=k == KT_D - 1)
                last.then_inc(projected[g], 1)

            def transpose_conv(i):
                pe.wait_ge(tapped, TAP_OPS * (i + 1))
                if not isinstance(i, int) or i:
                    pe.wait_ge(swished, CB * i)
                for c in range(CB):
                    last = nc.tensor.transpose(tC[:, c * P:(c + 1) * P], acc[:, c, :], ident[:, :])
                last.then_inc(conv_T, 1)

            def transpose_back(i):
                pe.wait_ge(cn_done, i + 1)
                for c in range(CB):
                    last = nc.tensor.transpose(tC[:, c * P:(c + 1) * P], cn[:, c * P:(c + 1) * P], ident[:, :])
                last.then_inc(cT_ready, 1)

            def transpose_qkh(i):
                pe.wait_ge(xT_copied, KT_D * (i + 1))
                pe.wait_ge(q_normed, i + 1)
                for b in range(AB):
                    last = nc.tensor.transpose(tA[:, b * P:(b + 1) * P], qn[:, b * P:(b + 1) * P], ident[:, :])
                last.then_inc(qT_ready, 1)
                pe.wait_ge(k_normed, i + 1)
                for b in range(AB):
                    last = nc.tensor.transpose(tB[:, b * P:(b + 1) * P], kn[:, b * P:(b + 1) * P], ident[:, :])
                last.then_inc(kT_ready, 1)
                pe.wait_ge(qT_copied, i + 1)
                pe.wait_ge(glu_done, i + 1)
                for c in range(CB):
                    last = nc.tensor.transpose(tA[:, c * P:(c + 1) * P], glu[:, c * P:(c + 1) * P], ident[:, :])
                last.then_inc(hT_ready, 1)

            def chunk(i, first=False):
                transpose_x(i)
                for g in (Q, K, A, G):
                    project(i, g)
                if not first:
                    transpose_conv(i - 1)
                project(i, V)
                if not first:
                    transpose_back(i - 1)
                transpose_qkh(i)

            chunk(0, first=True)
            with pe.Fori(1, CHUNKS) as i:
                chunk(i)
            transpose_conv(CHUNKS - 1)
            transpose_back(CHUNKS - 1)

        @block.scalar
        def _(act):
            def square_x(i):
                act.wait_ge(x_loaded, 16 * (i + 1))
                if not isinstance(i, int) or i:
                    act.wait_ge(xT_ready, 2 * i)
                    act.wait_ge(x_meaned, i)
                nc.scalar.activation(xn[:, :], x_in[:, :], ACT.Square, accum_out=x_stat[:, 0:1]).then_inc(x_squared, 1)

            def root_x(i):
                act.wait_ge(x_meaned, i + 1)
                if not isinstance(i, int) or i:
                    act.wait_ge(x_recip, i)
                nc.scalar.activation(x_stat[:, 2:3], x_stat[:, 1:2], ACT.Sqrt).then_inc(x_rooted, 1)

            def copy_xT(i):
                act.wait_ge(setup_copied, 1)
                if not isinstance(i, int) or i:
                    act.wait_ge(projected[V], i)
                for k in range(KT_D):
                    if k % 4 == 0:
                        act.wait_ge(xT_ready, 2 * i + k // 4 + 1)
                    nc.scalar.activation(xnT[:, k, :], (tA, tB)[k // 4][:, (k % 4) * P:(k % 4 + 1) * P],
                                         ACT.Copy, scale=g_mix[:, k:k + 1]).then_inc(xT_copied, 1)

            def square_qk(i):
                if not isinstance(i, int) or i:
                    act.wait_ge(qk_summed, i)
                for n, g in enumerate((Q, K)):
                    act.wait_ge(projected[g], i + 1)
                    nc.scalar.activation(squares[:, n * AW:(n + 1) * AW], ps[g], ACT.Square).then_inc(qk_squared, 1)

            def gate(i):
                act.wait_ge(projected[G], i + 1)
                if not isinstance(i, int) or i:
                    act.wait_ge(glu_done, i)
                nc.scalar.activation(sig[:, :], ps[G], ACT.Sigmoid).then_inc(gated, 1)

            def root_qk(i):
                act.wait_ge(qk_meaned, 2 * (i + 1))
                if not isinstance(i, int) or i:
                    act.wait_ge(qk_recip, i)
                nc.scalar.activation(qk_stat[:, 2, :], qk_stat[:, 1, :], ACT.Sqrt).then_inc(qk_rooted, 1)

            def copy_v(i):
                act.wait_ge(projected[V], i + 1)
                act.wait_ge(zeroed, 6)
                nc.scalar.activation(vals[:, bass.ds(i, 1), :].rearrange("p o n -> p (o n)"), ps[V],
                                     ACT.Copy).then_inc(v_copied, 1)

            def copy_qkh(i):
                act.wait_ge(qT_ready, i + 1)
                if not isinstance(i, int) or i:
                    act.wait_ge(qT_stored, 16 * i)
                nc.scalar.activation(qT_out[:, :], tA, ACT.Copy, scale=g_q).then_inc(qT_copied, 1)
                act.wait_ge(kT_ready, i + 1)
                nc.scalar.activation(kT[:, :, bass.ds(i * P, P)], tB.rearrange("p (b t) -> p b t", b=AB),
                                     ACT.Copy, scale=g_k).then_inc(kT_copied, 1)
                act.wait_ge(hT_ready, i + 1)
                if not isinstance(i, int) or i:
                    act.wait_ge(halo_moved, i)
                else:
                    act.wait_ge(zeroed, 6)
                nc.scalar.activation(conv_in[:, :, HALO:], tA.rearrange("p (b t) -> p b t", b=CB),
                                     ACT.Copy).then_inc(hT_copied, 1)

            def root_ln(i):
                act.wait_ge(ln_eps, i + 1)
                if not isinstance(i, int) or i:
                    act.wait_ge(ln_recip, i)
                nc.scalar.activation(ln_stat[:, 3:4], ln_stat[:, 2:3], ACT.Sqrt).then_inc(ln_rooted, 1)

            def swish(i):
                act.wait_ge(cT_ready, i + 1)
                if not isinstance(i, int) or i:
                    act.wait_ge(cT_stored, 16 * i)
                for c in range(CB):
                    nc.scalar.activation(cT_out[:, c * P:(c + 1) * P], tC[:, c * P:(c + 1) * P], ACT.Silu,
                                         bias=b_ln[:, c:c + 1], scale=g_ln[:, c:c + 1]).then_inc(swished, 1)

            def chunk(i, first=False, last=False):
                copy_xT(i)
                square_qk(i)
                gate(i)
                root_qk(i)
                if not first:
                    root_ln(i - 1)
                copy_v(i)
                if not last:
                    square_x(i + 1)
                    root_x(i + 1)
                if not first:
                    swish(i - 1)
                copy_qkh(i)

            square_x(0)
            root_x(0)
            chunk(0, first=True)
            with act.Fori(1, CHUNKS - 1) as i:
                chunk(i)
            chunk(CHUNKS - 1, last=True)
            root_ln(CHUNKS - 1)
            swish(CHUNKS - 1)

        @block.vector
        def _(dve):
            def norm_x(i):
                dve.wait_ge(x_squared, i + 1)
                if not isinstance(i, int) or i:
                    dve.wait_ge(x_rooted, i)
                nc.vector.tensor_scalar(x_stat[:, 1:2], x_stat[:, 0:1], 1.0 / D, EPS, ALU.mult, ALU.add).then_inc(x_meaned, 1)
                dve.wait_ge(x_rooted, i + 1)
                if not isinstance(i, int) or i:
                    dve.wait_ge(x_normed, i)
                nc.vector.reciprocal(x_stat[:, 3:4], x_stat[:, 2:3]).then_inc(x_recip, 1)
                dve.wait_ge(x_recip, i + 1)
                nc.vector.tensor_scalar(xn[:, :], x_in[:, :], x_stat[:, 3:4], None, ALU.mult).then_inc(x_normed, 1)

            def convolve(i):
                dve.wait_ge(hT_copied, i + 1)
                if not isinstance(i, int) or i:
                    dve.wait_ge(conv_T, i)
                for t in range(TAPS):
                    for c in range(CB):
                        if t == 0:
                            nc.vector.tensor_scalar(acc[:, c, :], conv_in[:, c, 0:P], taps[:, c, 0:1],
                                                    b_conv[:, c:c + 1], ALU.mult, ALU.add).then_inc(tapped, 1)
                        else:
                            dve.wait_ge(tapped, TAP_OPS * i + (t - 1) * CB + c + 1)
                            nc.vector.scalar_tensor_tensor(out=acc[:, c, :], in0=conv_in[:, c, t:t + P],
                                                           scalar=taps[:, c, t:t + 1], in1=acc[:, c, :],
                                                           op0=ALU.mult, op1=ALU.add).then_inc(tapped, 1)
                dve.wait_ge(tapped, TAP_OPS * (i + 1))
                nc.vector.tensor_copy(conv_in[:, :, 0:HALO], conv_in[:, :, P:P + HALO]).then_inc(halo_moved, 1)

            def norm_qk(i):
                dve.wait_ge(qk_squared, 2 * (i + 1))
                if not isinstance(i, int) or i:
                    dve.wait_ge(qk_meaned, 2 * i)
                nc.vector.reduce_sum(qk_stat[:, 0, :], squares[:, :].rearrange("p (h d) -> p h d", d=HD),
                                     AXX).then_inc(qk_summed, 1)
                dve.wait_ge(qk_summed, i + 1)
                if not isinstance(i, int) or i:
                    dve.wait_ge(qk_rooted, i)
                nc.vector.tensor_scalar(qk_stat[:, 1, 0:HEADS], qk_stat[:, 0, 0:HEADS], 1.0, HD * EPS,
                                        ALU.mult, ALU.add).then_inc(qk_meaned, 1)
                nc.vector.tensor_scalar(qk_stat[:, 1, HEADS:], qk_stat[:, 0, HEADS:], 1.0 / HD, EPS,
                                        ALU.mult, ALU.add).then_inc(qk_meaned, 1)

            def scale_qk(i):
                dve.wait_ge(qk_rooted, i + 1)
                if not isinstance(i, int) or i:
                    dve.wait_ge(k_normed, i)
                nc.vector.reciprocal(qk_stat[:, 3, :], qk_stat[:, 2, :]).then_inc(qk_recip, 1)
                dve.wait_ge(qk_recip, i + 1)
                for n, (g, to, done, used) in enumerate(((Q, qn, q_normed, qT_ready), (K, kn, k_normed, kT_ready))):
                    if not isinstance(i, int) or i:
                        dve.wait_ge(used, i)
                    nc.vector.tensor_tensor(to[:, :].rearrange("p (h d) -> p h d", d=HD),
                                            ps[g].rearrange("p (h d) -> p h d", d=HD),
                                            spread(qk_stat[:, 3, n * HEADS:], [[1, HEADS], [0, HD]]),
                                            ALU.mult).then_inc(done, 1)

            def ln_stats(i):
                dve.wait_ge(conv_T, i + 1)
                if not isinstance(i, int) or i:
                    dve.wait_ge(ln_done, i)
                nc.vector.bn_stats(bn[:, :], tC).then_inc(bn_done, 1)
                if not isinstance(i, int) or i:
                    hold(dve, cn_done, i, dve_passed)
                hold(dve, bn_done, i + 1, dve_passed)
                nc.vector.bn_aggr(ln_stat[:, 0:2], bn[:, :]).then_inc(ln_done, 1)
                dve.wait_ge(ln_done, i + 1)
                if not isinstance(i, int) or i:
                    dve.wait_ge(ln_rooted, i)
                nc.vector.tensor_scalar(ln_stat[:, 2:3], ln_stat[:, 1:2], 1.0, EPS, ALU.mult, ALU.add).then_inc(ln_eps, 1)

            def ln_scale(i):
                dve.wait_ge(ln_rooted, i + 1)
                nc.vector.reciprocal(ln_stat[:, 4:5], ln_stat[:, 3:4]).then_inc(ln_recip, 1)
                dve.wait_ge(ln_recip, i + 1)
                if not isinstance(i, int) or i:
                    dve.wait_ge(cT_ready, i)
                nc.vector.tensor_scalar(cn[:, :], tC, ln_stat[:, 0:1], ln_stat[:, 4:5],
                                        ALU.subtract, ALU.mult).then_inc(cn_done, 1)

            def glu_(i):
                dve.wait_ge(gated, i + 1)
                dve.wait_ge(projected[A], i + 1)
                if not isinstance(i, int) or i:
                    dve.wait_ge(hT_ready, i)
                nc.vector.tensor_tensor(glu[:, :], ps[A], sig[:, :], ALU.mult).then_inc(glu_done, 1)

            def chunk(i, first=False, last=False):
                if not first:
                    convolve(i - 1)
                norm_qk(i)
                if not first:
                    ln_stats(i - 1)
                scale_qk(i)
                glu_(i)
                if not first:
                    ln_scale(i - 1)
                if not last:
                    norm_x(i + 1)

            norm_x(0)
            dve.wait_ge(setup_T, 1)
            dve.wait_ge(zeroed, 6)
            nc.vector.tensor_copy(vec[:, :], tC[:, 0:NVEC]).then_inc(setup_copied, 1)
            nc.vector.tensor_copy(taps[:, :, :], tC[:, P:P + CB * 32].rearrange("p (c t) -> p c t", t=32)[:, :, 0:TAPS]).then_inc(setup_copied, 1)
            for half, (lo, hi) in enumerate(((0, HALF), (HALF, P))):
                for t, bank in enumerate((tA, tB)):
                    copied = nc.vector.tensor_copy(
                        keys_bd[lo:hi, 4 * t:4 * t + 4, half * NKEYS:(half + 1) * NKEYS],
                        bank[lo:hi, :].rearrange("p (h n) -> p h n", n=NKEYS))
            copied.then_inc(setup_copied, 2)
            dve.wait_ge(setup_copied, 4)

            chunk(0, first=True)
            with dve.Fori(1, CHUNKS - 1) as i:
                chunk(i)
            chunk(CHUNKS - 1, last=True)
            convolve(CHUNKS - 1)
            ln_stats(CHUNKS - 1)
            ln_scale(CHUNKS - 1)


def phase1(nc, base, psum, ident, ident_b, mask_band, kT, vals, keys_bd, iota16, g_attn,
           qT_spill, cT_spill, x, w_out, norm_ffn_g, peer_wq, peer_u, peer_v, out):
    m = Map(nc, base)
    wo_sb = m.tile("wo_sb", [P, KT_D, D], F32)
    wq_sb = m.tile("wq_sb", [P, KT_D, D], F32)
    ring = m.tile("ring", [P, RING, D], F32)
    h_res = m.tile("h_res", [P, D], F32)
    g_ffn = m.tile("g_ffn", [P, D], F32)
    hn_next = m.tile("hn_next", [P, D], F32)
    hn = m.tile("hn", [P, D], F32)
    y_out = m.tile("y_out", [P, D], F32)
    actT = m.tile("actT", [P, KT_D, P], F32)
    qT = m.tile("qT", [P, AB, P], F32)
    diag = m.tile("diag", [P, TOPK, P], F32)
    log_keep = [m.tile(f"log_keep{n}", [P, SEQ], F32) for n in range(2)]
    relu_z = [m.tile(f"relu_z{n}", [P, SEQ], F32) for n in range(2)]
    attT = m.tile("attT", [P, CHUNKS, P], F32)
    small = Map(nc, m.at)
    experts_next = small.tile("experts_next", [P, ROWS], I32)
    experts = small.tile("experts", [P, ROWS], I32)
    gates_next = small.tile("gates_next", [P, ROWS], F32)
    gates = small.tile("gates", [P, ROWS], F32)
    dots = small.tile("dots", [P, ROWS], F32)
    geld = small.tile("geld", [P, ROWS], F32)
    weights = small.tile("weights", [P, ROWS], F32)
    top_v = small.tile("top_v", [P, PH, 2, TOPK], F32)
    top_i = small.tile("top_i", [P, PH, 2, TOPK], U32)
    best_v = small.tile("best_v", [P, PH, TOPK], F32)
    best_i = small.tile("best_i", [P, PH, TOPK], U32)
    stat = small.tile("stat", [P, 8], F32)
    gate_sum = small.tile("gate_sum", [P, 2, PH], F32)
    assert small.at <= nc.sbuf_usable_end

    o_norm = log_keep[0][:, 0:AW]
    qhT = log_keep[1][:, :].rearrange("p (h t) -> p h t", t=P)
    at_of = lambda t: t[:, :].offset
    left1 = relu_z[0]
    left2 = relu_z[1]
    top_f = attT

    y_ps = psum[:, 0:2, :].rearrange("p b n -> p (b n)")
    z_ps = [psum[:, 2 + 2 * n:4 + 2 * n, :].rearrange("p b n -> p (b n)") for n in range(2)]
    t_ps, o_ps = psum[:, 6, :], psum[:, 7, :]

    def score(h, half):
        at = (h % 4) * 2 * NKEYS + half * NKEYS
        return z_ps[h // 4][:, at:at + NKEYS]

    def left(h, half):
        n = 2 * h + half
        return (left1 if n < 8 else left2)[:, (n % 8) * NKEYS:(n % 8 + 1) * NKEYS]

    cand = [log_keep[n][:, :].rearrange("p (h c) -> p h c", c=TOPK * TOPK) for n in range(2)]

    sem = nc.alloc_semaphore
    wo_loaded, wq_loaded, g_loaded = sem("wo_loaded"), sem("wq_loaded"), sem("g_loaded")
    x_in, q_in, c_in, y_stored = sem("x_in"), sem("q_in"), sem("c_in"), sem("y_stored")
    z_ready, abs_done, exp_done, ln_done1, relu_done = (
        sem("z_ready"), sem("abs_done"), sem("exp_done"), sem("ln_done1"), sem("relu_done"))
    summed, stick, att_done, att_T, att_copied, attended = (
        sem("summed"), sem("stick"), sem("att_done"), sem("att_T"), sem("att_copied"), sem("attended"))
    o_squared, o_meaned, o_rooted, o_recip, o_normed, o_T, o_copied = (
        sem("o_squared"), sem("o_meaned"), sem("o_rooted"), sem("o_recip"), sem("o_normed"),
        sem("o_T"), sem("o_copied"))
    mixed, h_done, h_squared, h_meaned, h_rooted, h_recip, h_normed = (
        sem("mixed"), sem("h_done"), sem("h_squared"), sem("h_meaned"), sem("h_rooted"),
        sem("h_recip"), sem("h_normed"))
    h_T, h_copied, queried, queries_copied, scored = (
        sem("h_T"), sem("h_copied"), sem("queried"), sem("queries_copied"), sem("scored"))
    top8, index8, replaced, top16, index16 = (
        sem("top8"), sem("index8"), sem("replaced"), sem("top16"), sem("index16"))
    top_floated, cand_done = sem("top_floated"), sem("cand_done")
    best8, bindex8, breplaced, best16, bindex16 = (
        sem("best8"), sem("bindex8"), sem("breplaced"), sem("best16"), sem("bindex16"))
    split, split_f, matched, picked, looked, experts_done = (
        sem("split"), sem("split_f"), sem("matched"), sem("picked"), sem("looked"), sem("experts_done"))
    g_shifted, g_exped, g_summed, g_recip, gates_done = (
        sem("g_shifted"), sem("g_exped"), sem("g_summed"), sem("g_recip"), sem("gates_done"))
    taken, experts_live, gates_live = sem("taken"), sem("experts_live"), sem("gates_live")
    row_in = [sem(f"row_in{n}") for n in range(RING)]
    dotted, gelued, weighted, diagonal, y_begun, row_added, y_copied = (
        sem("dotted"), sem("gelued"), sem("weighted"), sem("diagonal"), sem("y_begun"),
        sem("row_added"), sem("y_copied"))

    dve_passed, pool_passed = sem("dve_passed1"), sem("pool_passed")
    later = lambda i: not isinstance(i, int) or i > 0
    PIECES = 2 * TOPK
    FILLS = PH * PIECES // RING
    WAITS_TOP = 2 * PH

    SPANS = ((0, 1, 2 * P), (1, 2, 2 * P), (2, 4, 4 * P), (4, CHUNKS, SEQ))

    def over_chunks(eng, step):
        step(None, 0, SPANS[0][2])
        for lo, hi, keys in SPANS[1:]:
            if hi - lo == 1:
                step(lo - 1, lo, keys)
            else:
                with eng.Fori(lo, hi) as f:
                    step(f - 1, f, keys)
        step(CHUNKS - 1, None, 0)

    with nc.Block() as block:

        @block.sync
        def _(sp):
            sp.dma_start(g_ffn[:, :], norm_ffn_g[0:1, :].to_broadcast([P, D])).then_inc(g_loaded, 16)

            def load_front(f):
                if later(f):
                    sp.wait_ge(z_ready, HEADS * f)
                sp.dma_start(qT[:, :, :].rearrange("p b t -> p (b t)"),
                             qT_spill[bass.ds(f, 1), :, :].rearrange("o p n -> (o p) n")).then_inc(q_in, 16)
                if later(f):
                    sp.wait_ge(queried, f)
                sp.dma_start(actT[:, AB:, :].rearrange("p b t -> p (b t)"),
                             cT_spill[bass.ds(f, 1), :, :].rearrange("o p n -> (o p) n")).then_inc(c_in, 16)
                if later(f):
                    sp.wait_ge(y_begun, f)
                sp.dma_start(h_res[:, :], x[0, bass.ds(f * P, P), :]).then_inc(x_in, 16)

            def store(c):
                sp.wait_ge(y_copied, c + 1)
                sp.dma_start(out[0, bass.ds(c * P, P), :], y_out[:, :]).then_inc(y_stored, 16)

            def step(c, f, keys):
                if f is not None:
                    load_front(f)
                if c is None:
                    for w, to, loaded in ((w_out, wo_sb, wo_loaded), (peer_wq, wq_sb, wq_loaded)):
                        sp.dma_start(to[:, :, :], w[0].rearrange("(k p) n -> p k n", p=P)).then_inc(loaded, 16)
                else:
                    store(c)

            over_chunks(sp, step)
            sp.wait_ge(y_stored, 16 * CHUNKS)

        @block.gpsimd
        def _(pool):
            def step(c, f, keys):
                if c is None:
                    return
                for w in range(PH):
                    if w == 0:
                        hold(pool, experts_live, 2 * c + 1, pool_passed)
                    if w == PH - 1:
                        hold(pool, experts_live, 2 * c + 2, pool_passed)
                    for piece in range(PIECES):
                        n = w * PIECES + piece
                        before = n - RING
                        if before < 0 and not later(c):
                            pass
                        elif piece < TOPK and piece >= RING:
                            hold(pool, dotted, ROWS * c + w * TOPK + piece - RING + 1, pool_passed)
                        elif piece < RING:
                            hold(pool, row_added, ROWS * c + w * TOPK + piece - RING + 1, pool_passed)
                        elif piece < TOPK + RING:
                            hold(pool, dotted, ROWS * c + w * TOPK + piece - RING + 1, pool_passed)
                        else:
                            hold(pool, row_added, ROWS * c + w * TOPK + piece - TOPK - RING + 1, pool_passed)
                        table = peer_u if piece < TOPK else peer_v
                        e = w * TOPK + piece % TOPK
                        nc.gpsimd.indirect_dma_start(
                            ring[:, n % RING, :], None, table[0],
                            bass.IndirectOffsetOnAxis(experts[:, e:e + 1], 0)).then_inc(row_in[n % RING], 16)

            over_chunks(pool, step)

        @block.tensor
        def _(pe):
            def scores(f, a, keys):
                z = z_ps[a % 2]
                if a == 0:
                    pe.wait_ge(q_in, 16 * (f + 1))
                if a < 2:
                    if later(f):
                        pe.wait_ge(replaced, WAITS_TOP * f)
                        pe.wait_ge(index8, WAITS_TOP * f)
                else:
                    pe.wait_ge(stick, HEADS * f + a - 1)
                lo = HD * (a % 2)
                for s in range(0, keys, BANK):
                    n = min(BANK, keys - s)
                    nc.tensor.matmul(z[:, s:s + n], qT[lo:lo + HD, a // 2, :], kT[lo:lo + HD, a // 2, s:s + n],
                                     start=True, stop=False)
                    last = nc.tensor.matmul(z[:, s:s + n], ident_b[:, :],
                                            mask_band[:, bass.ds(s + MASK_SPAN - f * P, n)],
                                            start=False, stop=True)
                last.then_inc(z_ready, 1)

            def attend(f, a, keys):
                blocks = keys // P
                if a == 0 and later(f):
                    pe.wait_ge(h_copied, 2 * f)
                pe.wait_ge(att_done, HEADS * f + a + 1)
                for half in range(2):
                    g = 2 * HEADS * f + 2 * a + half
                    if a or half:
                        pe.wait_ge(att_copied, g)
                    elif later(f):
                        pe.wait_ge(o_copied, AB * f)
                    for b in range(blocks // 2):
                        s = (half * blocks // 2 + b) * P
                        last = nc.tensor.transpose(t_ps[:, b * P:(b + 1) * P],
                                                   log_keep[a % 2][:, s:s + P], ident[:, :])
                    last.then_inc(att_T, 1)
                if a == 0 and later(f):
                    pe.wait_ge(o_normed, f)
                for b in range(blocks):
                    if b in (0, blocks // 2):
                        pe.wait_ge(att_copied, 2 * HEADS * f + 2 * a + 1 + (b > 0))
                    last = nc.tensor.matmul(o_ps[:, a * HD:(a + 1) * HD], attT[:, b, :],
                                            vals[:, b, a * HD:(a + 1) * HD], start=b == 0, stop=b == blocks - 1)
                last.then_inc(attended, 1)

            def mix(f):
                pe.wait_ge(o_normed, f + 1)
                pe.wait_ge(att_copied, 2 * HEADS * (f + 1))
                for b in range(AB):
                    last = nc.tensor.transpose(t_ps[:, b * P:(b + 1) * P], o_norm[:, b * P:(b + 1) * P], ident[:, :])
                last.then_inc(o_T, 1)
                pe.wait_ge(c_in, 16 * (f + 1))
                if not later(f):
                    pe.wait_ge(wo_loaded, 16)
                pe.wait_ge(stick, HEADS * (f + 1))
                for j in range(2):
                    for n, k in enumerate((*range(AB, KT_D), *range(AB))):
                        if j == 0 and k < AB:
                            pe.wait_ge(o_copied, AB * f + k + 1)
                        last = nc.tensor.matmul(z_ps[0][:, j * BANK:(j + 1) * BANK], actT[:, k, :],
                                                wo_sb[:, k, j * BANK:(j + 1) * BANK], start=n == 0, stop=n == KT_D - 1)
                last.then_inc(mixed, 1)

            def query(f):
                pe.wait_ge(h_normed, f + 1)
                for k in range(KT_D):
                    last = nc.tensor.transpose(z_ps[1][:, k * P:(k + 1) * P], hn_next[:, k * P:(k + 1) * P], ident[:, :])
                    if k % 4 == 3:
                        last.then_inc(h_T, 1)
                pe.wait_ge(h_copied, 2 * (f + 1))
                pe.wait_ge(h_done, f + 1)
                if not later(f):
                    pe.wait_ge(wq_loaded, 16)
                for h in range(PH):
                    for k in range(KT_D):
                        last = nc.tensor.matmul(z_ps[0][:, h * P:(h + 1) * P], wq_sb[:, k, h * P:(h + 1) * P],
                                                actT[:, k, :], start=k == 0, stop=k == KT_D - 1)
                last.then_inc(queried, 1)
                pe.wait_ge(queries_copied, f + 1)
                for h in range(PH):
                    last = nc.tensor.matmul(z_ps[h // 4][:, (h % 4) * 2 * NKEYS:(h % 4 + 1) * 2 * NKEYS],
                                            qhT[:, h, :], keys_bd[:, h, :], start=True, stop=True)
                last.then_inc(scored, 1)

            def begin_y(c):
                pe.wait_ge(h_done, c + 1)
                if later(c):
                    pe.wait_ge(y_copied, c)
                for j in range(2):
                    last = nc.tensor.matmul(y_ps[:, j * BANK:(j + 1) * BANK], ident[:, :],
                                            h_res[:, j * BANK:(j + 1) * BANK], start=True, stop=False)
                last.then_inc(y_begun, 1)

            def add_rows(c, w):
                pe.wait_ge(diagonal, PH * c + w + 1)
                for k in range(TOPK):
                    n = w * PIECES + TOPK + k
                    pe.wait_ge(row_in[n % RING], 16 * (FILLS * c + n // RING + 1))
                    for j in range(2):
                        last = nc.tensor.matmul(y_ps[:, j * BANK:(j + 1) * BANK], diag[:, k, :],
                                                ring[:, n % RING, j * BANK:(j + 1) * BANK], start=False,
                                                stop=w == PH - 1 and k == TOPK - 1)
                    last.then_inc(row_added, 1)

            def step(c, f, keys):
                if c is not None:
                    begin_y(c)
                for w in range(PH):
                    if f is not None and w < HEADS // 2:
                        scores(f, 2 * w, keys)
                        scores(f, 2 * w + 1, keys)
                    if c is not None:
                        add_rows(c, w)
                    if f is not None:
                        if w < HEADS // 2:
                            attend(f, 2 * w, keys)
                            attend(f, 2 * w + 1, keys)
                        elif w == HEADS // 2:
                            mix(f)
                        elif w == HEADS // 2 + 1:
                            query(f)

            over_chunks(pe, step)

        @block.scalar
        def _(act):
            def soften(f, a, keys):
                z, l, r = z_ps[a % 2][:, 0:keys], log_keep[a % 2][:, 0:keys], relu_z[a % 2][:, 0:keys]
                act.wait_ge(z_ready, HEADS * f + a + 1)
                if a >= 2:
                    act.wait_ge(att_T, 2 * (HEADS * f + a - 1))
                    act.wait_ge(summed, HEADS * f + a - 1)
                elif later(f):
                    act.wait_ge(looked, 4 * f)
                    act.wait_ge(bindex16, PH * f)
                nc.scalar.activation(l, z, ACT.Abs).then_inc(abs_done, 1)
                nc.scalar.activation(r, z, ACT.Relu).then_inc(relu_done, 1)
                act.wait_ge(abs_done, HEADS * f + a + 1)
                nc.scalar.activation(l, l, ACT.Exp, scale=-1.0).then_inc(exp_done, 1)
                act.wait_ge(exp_done, HEADS * f + a + 1)
                nc.scalar.activation(l, l, ACT.Ln, bias=1.0).then_inc(ln_done1, 1)

            def weigh(f, a, keys):
                act.wait_ge(stick, HEADS * f + a + 1)
                l = log_keep[a % 2][:, 0:keys]
                nc.scalar.activation(l, l, ACT.Exp).then_inc(att_done, 1)

            def copy_att(f, a, keys):
                blocks = keys // P // 2
                if a or later(f):
                    act.wait_ge(attended, HEADS * f + a)
                if a == 0 and later(f):
                    act.wait_ge(experts_done, f)
                for half in range(2):
                    act.wait_ge(att_T, 2 * (HEADS * f + a) + half + 1)
                    nc.scalar.activation(attT[:, half * blocks:(half + 1) * blocks, :],
                                         t_ps[:, 0:blocks * P].rearrange("p (b t) -> p b t", t=P),
                                         ACT.Copy).then_inc(att_copied, 1)

            def square_o(f):
                act.wait_ge(attended, HEADS * (f + 1))
                act.wait_ge(att_T, 2 * HEADS * (f + 1))
                if later(f):
                    act.wait_ge(o_meaned, f)
                nc.scalar.activation(o_norm, o_ps, ACT.Square, accum_out=stat[:, 0:1]).then_inc(o_squared, 1)

            def root_o(f):
                act.wait_ge(o_meaned, f + 1)
                if later(f):
                    act.wait_ge(o_recip, f)
                nc.scalar.activation(stat[:, 2:3], stat[:, 1:2], ACT.Sqrt).then_inc(o_rooted, 1)

            def copy_o(f):
                act.wait_ge(o_T, f + 1)
                if later(f):
                    act.wait_ge(queried, f)
                for b in range(AB):
                    nc.scalar.activation(actT[:, b, :], t_ps[:, b * P:(b + 1) * P], ACT.Copy,
                                         scale=g_attn[:, b:b + 1]).then_inc(o_copied, 1)

            def square_h(f):
                act.wait_ge(h_done, f + 1)
                if later(f):
                    act.wait_ge(taken, 2 * f)
                    act.wait_ge(h_meaned, f)
                    act.wait_ge(h_T, 2 * f)
                nc.scalar.activation(hn_next[:, :], h_res[:, :], ACT.Square, accum_out=stat[:, 4:5]).then_inc(h_squared, 1)

            def root_h(f):
                act.wait_ge(h_meaned, f + 1)
                if later(f):
                    act.wait_ge(h_recip, f)
                nc.scalar.activation(stat[:, 6:7], stat[:, 5:6], ACT.Sqrt).then_inc(h_rooted, 1)

            def copy_h(f):
                act.wait_ge(mixed, f + 1)
                for j in range(2):
                    act.wait_ge(h_T, 2 * f + j + 1)
                    nc.scalar.activation(actT[:, 4 * j:4 * j + 4, :],
                                         z_ps[1][:, j * BANK:(j + 1) * BANK].rearrange("p (b t) -> p b t", t=P),
                                         ACT.Copy).then_inc(h_copied, 1)
                act.wait_ge(queried, f + 1)
                nc.scalar.activation(qhT[:, :, :], z_ps[0].rearrange("p (h t) -> p h t", t=P),
                                     ACT.Copy).then_inc(queries_copied, 1)

            def exp_gates(f):
                act.wait_ge(g_shifted, f + 1)
                nc.scalar.activation(gates_next[:, :], gates_next[:, :], ACT.Exp).then_inc(g_exped, 1)

            def gelu(c, w):
                act.wait_ge(dotted, ROWS * c + TOPK * (w + 1))
                if later(c):
                    act.wait_ge(weighted, PH * (c - 1) + w + 1)
                nc.scalar.activation(geld[:, w * TOPK:(w + 1) * TOPK], dots[:, w * TOPK:(w + 1) * TOPK],
                                     ACT.Gelu).then_inc(gelued, 1)

            def copy_y(c):
                act.wait_ge(row_added, ROWS * (c + 1))
                if later(c):
                    act.wait_ge(y_stored, 16 * c)
                nc.scalar.activation(y_out[:, :], y_ps, ACT.Copy).then_inc(y_copied, 1)

            def step(c, f, keys):
                for w in range(PH):
                    if f is not None and w < HEADS // 2:
                        soften(f, 2 * w, keys)
                        soften(f, 2 * w + 1, keys)
                    if c is not None:
                        if w == HEADS // 2 + 0 and f is not None:
                            pass
                        gelu(c, w)
                    if f is not None:
                        if w < HEADS // 2:
                            weigh(f, 2 * w, keys)
                            weigh(f, 2 * w + 1, keys)
                            copy_att(f, 2 * w, keys)
                            copy_att(f, 2 * w + 1, keys)
                        if w == HEADS // 2 - 1:
                            square_o(f)
                            root_o(f)
                        elif w == HEADS // 2:
                            copy_o(f)
                        elif w == HEADS // 2 + 1:
                            square_h(f)
                            root_h(f)
                            copy_h(f)
                        elif w == PH - 1:
                            exp_gates(f)
                if c is not None:
                    copy_y(c)

            over_chunks(act, step)

        @block.vector
        def _(dve):
            def accumulate(f, a, keys):
                l, r = log_keep[a % 2], relu_z[a % 2]
                dve.wait_ge(ln_done1, HEADS * f + a + 1)
                dve.wait_ge(relu_done, HEADS * f + a + 1)
                back = slice(keys - 1, None, -1) if keys == SEQ else slice(keys - 1, None, -1)
                nc.vector.tensor_tensor_scan(l[:, back], l[:, back], r[:, back], 0.0, ALU.add, ALU.add).then_inc(summed, 1)
                dve.wait_ge(summed, HEADS * f + a + 1)
                nc.vector.tensor_tensor(l[:, 0:keys], z_ps[a % 2][:, 0:keys], l[:, 0:keys], ALU.subtract).then_inc(stick, 1)

            def mean_o(f):
                dve.wait_ge(o_squared, f + 1)
                if later(f):
                    dve.wait_ge(o_rooted, f)
                nc.vector.tensor_scalar(stat[:, 1:2], stat[:, 0:1], 1.0 / AW, EPS, ALU.mult, ALU.add).then_inc(o_meaned, 1)

            def norm_o(f):
                dve.wait_ge(o_rooted, f + 1)
                if later(f):
                    dve.wait_ge(o_normed, f)
                nc.vector.reciprocal(stat[:, 3:4], stat[:, 2:3]).then_inc(o_recip, 1)
                dve.wait_ge(o_recip, f + 1)
                nc.vector.tensor_scalar(o_norm, o_ps, stat[:, 3:4], None, ALU.mult).then_inc(o_normed, 1)

            def add_residual(f):
                dve.wait_ge(mixed, f + 1)
                dve.wait_ge(x_in, 16 * (f + 1))
                nc.vector.tensor_tensor(h_res[:, :], z_ps[0], h_res[:, :], ALU.add).then_inc(h_done, 1)
                dve.wait_ge(h_squared, f + 1)
                if later(f):
                    dve.wait_ge(h_rooted, f)
                nc.vector.tensor_scalar(stat[:, 5:6], stat[:, 4:5], 1.0 / D, EPS, ALU.mult, ALU.add).then_inc(h_meaned, 1)
                dve.wait_ge(h_rooted, f + 1)
                if later(f):
                    dve.wait_ge(h_normed, f)
                else:
                    dve.wait_ge(g_loaded, 16)
                nc.vector.reciprocal(stat[:, 7:8], stat[:, 6:7]).then_inc(h_recip, 1)
                dve.wait_ge(h_recip, f + 1)
                nc.vector.scalar_tensor_tensor(out=hn_next[:, :], in0=h_res[:, :], scalar=stat[:, 7:8],
                                               in1=g_ffn[:, :], op0=ALU.mult, op1=ALU.mult).then_inc(h_normed, 1)

            def search_keys(f):
                halves = [(h, half) for h in range(PH) for half in range(2)]
                if later(f):
                    hold(dve, cand_done, 2 * f, dve_passed)
                    hold(dve, top_floated, f, dve_passed)
                hold(dve, scored, f + 1, dve_passed)
                for h, half in halves:
                    nc.vector.max(top_v[:, h, half, 0:8], score(h, half)).then_inc(top8, 1)
                hold(dve, top8, WAITS_TOP * (f + 1), dve_passed)
                for h, half in halves:
                    nc.vector.max_index(top_i[:, h, half, 0:8], top_v[:, h, half, 0:8], score(h, half)).then_inc(index8, 1)
                for h, half in halves:
                    nc.vector.match_replace(left(h, half), top_v[:, h, half, 0:8], score(h, half), LOWEST).then_inc(replaced, 1)
                hold(dve, replaced, WAITS_TOP * (f + 1), dve_passed)
                for h, half in halves:
                    nc.vector.max(top_v[:, h, half, 8:16], left(h, half)).then_inc(top16, 1)
                hold(dve, top16, WAITS_TOP * (f + 1), dve_passed)
                for h, half in halves:
                    nc.vector.max_index(top_i[:, h, half, 8:16], top_v[:, h, half, 8:16], left(h, half)).then_inc(index16, 1)

            tf = attT[:, 0:2, :].rearrange("p b t -> p (b t)").rearrange("p (h two k) -> p h two k", two=2, k=TOPK)
            parts_i = attT[:, 2:4, :].bitcast(U32).rearrange("p b t -> p (b t)")
            parts = attT[:, 4:6, :].rearrange("p b t -> p (b t)")
            looks = attT[:, 6:8, :].rearrange("p b t -> p (b t)")

            def add_candidates(f):
                dve.wait_ge(index16, WAITS_TOP * (f + 1))
                nc.vector.tensor_copy(tf, top_i[:, :, :, :]).then_inc(top_floated, 1)
                dve.wait_ge(top16, WAITS_TOP * (f + 1))
                for j in range(2):
                    first = top_v[:, 4 * j, 0, :]
                    second = top_v[:, 4 * j, 1, :]
                    nc.vector.tensor_tensor(
                        spread(cand[j], [[256, 4], [TOPK, TOPK], [1, TOPK]]),
                        spread(first, [[2 * TOPK, 4], [1, TOPK], [0, TOPK]]),
                        spread(second, [[2 * TOPK, 4], [0, TOPK], [1, TOPK]]), ALU.add).then_inc(cand_done, 1)

            def search_candidates(f, heads):
                if heads[0] == 0 and later(f):
                    hold(dve, split, 2 * f, dve_passed)
                    hold(dve, g_shifted, f, dve_passed)
                done = PH * f + heads[-1] + 1
                hold(dve, cand_done, 2 * f + heads[-1] // 4 + 1, dve_passed)
                for h in heads:
                    nc.vector.max(best_v[:, h, 0:8], cand[h // 4][:, h % 4, :]).then_inc(best8, 1)
                hold(dve, best8, done, dve_passed)
                for h in heads:
                    nc.vector.max_index(best_i[:, h, 0:8], best_v[:, h, 0:8], cand[h // 4][:, h % 4, :]).then_inc(bindex8, 1)
                hold(dve, bindex8, done, dve_passed)
                for h in heads:
                    nc.vector.match_replace(cand[h // 4][:, h % 4, :], best_v[:, h, 0:8], cand[h // 4][:, h % 4, :],
                                            LOWEST).then_inc(breplaced, 1)
                hold(dve, breplaced, done, dve_passed)
                for h in heads:
                    nc.vector.max(best_v[:, h, 8:16], cand[h // 4][:, h % 4, :]).then_inc(best16, 1)
                hold(dve, best16, done, dve_passed)
                for h in heads:
                    nc.vector.max_index(best_i[:, h, 8:16], best_v[:, h, 8:16], cand[h // 4][:, h % 4, :]).then_inc(bindex16, 1)

            def shift_gates(f):
                dve.wait_ge(best16, PH * (f + 1))
                if later(f):
                    dve.wait_ge(gates_live, f)
                nc.vector.tensor_tensor(gates_next[:, :].rearrange("p (h k) -> p h k", k=TOPK), best_v[:, :, :],
                                        spread(best_v[:, 0, 0:1], [[TOPK, PH], [0, TOPK]]), ALU.subtract).then_inc(g_shifted, 1)

            def look_up(f):
                dve.wait_ge(bindex16, PH * (f + 1))
                pos = best_i[:, :, :].rearrange("p h k -> p (h k)")
                nc.vector.tensor_single_scalar(parts_i[:, 0:ROWS], pos, 4, ALU.logical_shift_right).then_inc(split, 1)
                nc.vector.tensor_single_scalar(parts_i[:, ROWS:], pos, TOPK - 1, ALU.bitwise_and).then_inc(split, 1)
                dve.wait_ge(split, 2 * (f + 1))
                nc.vector.tensor_copy(parts, parts_i).then_inc(split_f, 1)
                dve.wait_ge(split_f, f + 1)
                eq = [relu_z[0], relu_z[1]]
                for half in range(2):
                    for j in range(2):
                        nc.vector.tensor_tensor(
                            spread(eq[j][:, :], [[256, 4], [TOPK, TOPK], [1, TOPK]]),
                            spread(parts[:, half * ROWS + 4 * j * TOPK:], [[TOPK, 4], [1, TOPK], [0, TOPK]]),
                            spread(iota16[:, :], [[0, 4], [0, TOPK], [1, TOPK]]), ALU.is_equal).then_inc(matched, 1)
                    for j in range(2):
                        dve.wait_ge(matched, 4 * f + 2 * half + j + 1)
                        nc.vector.tensor_tensor(
                            spread(eq[j][:, :], [[256, 4], [TOPK, TOPK], [1, TOPK]]),
                            spread(eq[j][:, :], [[256, 4], [TOPK, TOPK], [1, TOPK]]),
                            spread(tf[:, 4 * j, half, :], [[2 * TOPK, 4], [0, TOPK], [1, TOPK]]),
                            ALU.mult).then_inc(picked, 1)
                    for j in range(2):
                        dve.wait_ge(picked, 4 * f + 2 * half + j + 1)
                        nc.vector.reduce_sum(looks[:, half * ROWS + 64 * j:half * ROWS + 64 * j + 64],
                                             eq[j][:, :].rearrange("p (r s) -> p r s", s=TOPK), AXX).then_inc(looked, 1)
                    dve.wait_ge(looked, 4 * f + 2 * half + 2)
                if later(f):
                    dve.wait_ge(experts_live, 2 * f)
                nc.vector.scalar_tensor_tensor(out=experts_next[:, :], in0=looks[:, 0:ROWS], scalar=float(NKEYS),
                                               in1=looks[:, ROWS:], op0=ALU.mult, op1=ALU.add).then_inc(experts_done, 1)

            def finish_gates(f):
                g = gates_next[:, :].rearrange("p (h k) -> p h k", k=TOPK)
                dve.wait_ge(g_exped, f + 1)
                nc.vector.reduce_sum(gate_sum[:, 0, :], g, AXX).then_inc(g_summed, 1)
                dve.wait_ge(g_summed, f + 1)
                nc.vector.reciprocal(gate_sum[:, 1, :], gate_sum[:, 0, :]).then_inc(g_recip, 1)
                dve.wait_ge(g_recip, f + 1)
                nc.vector.tensor_tensor(g, g, spread(gate_sum[:, 1, :], [[1, PH], [0, TOPK]]), ALU.mult).then_inc(gates_done, 1)

            LAST = (PH - 1) * TOPK

            def go_live(c):
                dve.wait_ge(experts_done, c + 1)
                if later(c):
                    dve.wait_ge(row_in[RING - 1], 16 * (FILLS * c - PIECES // RING))
                nc.vector.tensor_copy(experts[:, 0:LAST], experts_next[:, 0:LAST]).then_inc(experts_live, 1)
                dve.wait_ge(gates_done, c + 1)
                nc.vector.tensor_copy(gates[:, :], gates_next[:, :]).then_inc(gates_live, 1)
                dve.wait_ge(h_normed, c + 1)
                nc.vector.tensor_copy(hn[:, :], hn_next[:, :]).then_inc(taken, 2)
                if later(c):
                    for n in range(RING):
                        dve.wait_ge(row_in[n], 16 * FILLS * c)
                nc.vector.tensor_copy(experts[:, LAST:], experts_next[:, LAST:]).then_inc(experts_live, 1)

            def dot_rows(c, w, between):
                if w == 0:
                    dve.wait_ge(taken, 2 * (c + 1))
                    if later(c):
                        dve.wait_ge(gelued, PH * c)
                for k in range(TOPK):
                    if k in between:
                        between[k]()
                    n = w * PIECES + k
                    e = w * TOPK + k
                    dve.wait_ge(row_in[n % RING], 16 * (FILLS * c + n // RING + 1))
                    nc.vector.tensor_tensor_reduce(out=ring[:, n % RING, :], in0=ring[:, n % RING, :], in1=hn[:, :],
                                                   scale=1.0, scalar=0.0, op0=ALU.mult, op1=ALU.add,
                                                   accum_out=dots[:, e:e + 1]).then_inc(dotted, 1)

            def weigh_rows(c, w):
                dve.wait_ge(gelued, PH * c + w + 1)
                if w == 0:
                    dve.wait_ge(gates_live, c + 1)
                if later(c):
                    dve.wait_ge(diagonal, PH * (c - 1) + w + 1)
                at = slice(w * TOPK, (w + 1) * TOPK)
                nc.vector.tensor_tensor(weights[:, at], geld[:, at], gates[:, at], ALU.mult).then_inc(weighted, 1)
                dve.wait_ge(weighted, PH * c + w + 1)
                if w or later(c):
                    dve.wait_ge(row_added, ROWS * c + w * TOPK)
                nc.vector.tensor_tensor(diag[:, :, :], spread(ident[:, :], [[0, TOPK], [1, P]]),
                                        spread(weights[:, at], [[1, TOPK], [0, P]]), ALU.mult).then_inc(diagonal, 1)

            def step(c, f, keys):
                if c is not None:
                    go_live(c)
                for w in range(PH):
                    between = {}
                    if f is not None and w == HEADS // 2:
                        between = {10: lambda: mean_o(f), 12: lambda: norm_o(f)}
                    if c is not None:
                        dot_rows(c, w, between)
                        weigh_rows(c, w)
                    else:
                        for fn in between.values():
                            fn()
                    if f is None:
                        continue
                    if w < HEADS // 2:
                        accumulate(f, 2 * w, keys)
                        accumulate(f, 2 * w + 1, keys)
                    elif w == HEADS // 2 + 1:
                        add_residual(f)
                    elif w == HEADS // 2 + 2:
                        search_keys(f)
                        add_candidates(f)
                        search_candidates(f, range(0, 4))
                    elif w == HEADS // 2 + 3:
                        search_candidates(f, range(4, PH))
                        shift_gates(f)
                        look_up(f)
                        finish_gates(f)

            over_chunks(dve, step)


_INS = ["x", "norm_mix_g", "w_in", "q_norm_g", "k_norm_g", "attn_out_g", "conv_w", "conv_b", "conv_ln_g",
        "conv_ln_b", "w_out", "norm_ffn_g", "peer_wq", "peer_k1", "peer_k2", "peer_u", "peer_v"]


def kernel(**inputs):
    import concourse.bacc as _bacc
    from concourse.bass_utils import run_bass_kernel_spmd as _run

    nc = _bacc.Bacc("TRN2", target_bir_lowering=False, num_devices=1)
    arrays, args = {}, []
    for name in _INS:
        a = np.ascontiguousarray(inputs[name])
        arrays[f"in_{name}"] = a
        args.append(nc.dram_tensor(f"in_{name}", a.shape, mybir.dt.from_np(a.dtype), kind="ExternalInput").ap())
    args.append(nc.dram_tensor("out_0", [1, SEQ, D], F32, kind="ExternalOutput").ap())
    build(nc, *args)
    r = _run(nc, [arrays], core_ids=[0])
    return r.results[0]["out_0"]
```

```python
import numpy as np
import concourse.bass as bass
from concourse import mybir

F32 = mybir.dt.float32
BF16 = mybir.dt.bfloat16
I32 = mybir.dt.int32
U32 = mybir.dt.uint32
ALU = mybir.AluOpType
ACT = mybir.ActivationFunctionType
AXX = mybir.AxisListType.X

P = 128
SEQ, D = 1024, 1024
CHUNKS = SEQ // P
KT_D = D // P
HEADS, HD = 8, 64
AW = HEADS * HD
CW = D - AW
AB = AW // P
CB = CW // P
TAPS = 31
HALO = TAPS - 1
COLS = 3 * AW + 2 * CW
BANK = 512
PH, TOPK, NKEYS = 8, 16, 128
HALF = 64
ROWS = PH * TOPK
EPS = 1e-6
NEG = -1.0e30
LOWEST = -3.0e38
RING = 4
FILLS = ROWS // RING
LAG = 20
SLOTS = ROWS
TABLE_PART = 96
TABLE_SLOT = 28
assert LAG % RING == 0 and TABLE_PART <= ROWS - LAG and TABLE_SLOT > LAG

MASK_SPAN = SEQ - P

ATT0, ATT_STEP = 0, 5
ATT_SOFT, ATT_SUM, ATT_EXP = 2, 4, 5
ATT_T0, ATT_T1, ATT_USE = 6, 7, 8
TAP0 = 8
ATT_END = ATT0 + ATT_STEP * (HEADS - 1) + ATT_USE
CONV_T, LN_STAT, LN_SCALE, CONV_BACK = (ATT_END + n for n in (-1, 0, 2, 3))
O_MEAN, O_NORM, O_T = (ATT_END + n for n in (1, 2, 3))
MIX, MIX_SLOTS = ATT_END + 6, 14
H_ADD, H_MEAN, H_NORM, H_T = (MIX + MIX_SLOTS + n for n in (0, 1, 3, 4))
QUERY, QUERY_SLOTS = H_T + 2, 14
SCORE = QUERY + QUERY_SLOTS + 1
SEARCH = SCORE + 3
CAND = SEARCH + 10
BEST = CAND + 3
SHIFT, SPLIT, LOOK = BEST + 10, BEST + 10, BEST + 11
EXPERTS, GATES = LOOK + 8, LOOK + 9
TABLE_NEXT = GATES + 1
assert TAP0 + TAPS <= CONV_T and TABLE_PART + LAG < TABLE_NEXT < SLOTS


def spread(view, dims):
    return bass.AP(view.tensor, view.offset, [list(view.ap[0])] + [list(d) for d in dims])


def hold(eng, sem, value, passed):
    eng.wait_ge(sem, value)
    eng.sem_inc(passed, 1)


class Map:

    def __init__(self, nc, start):
        self.nc, self.at = nc, (start + 31) // 32 * 32

    def tile(self, name, shape, dt):
        size = int(np.prod(shape[1:])) * (2 if dt == BF16 else 4)
        t = self.nc.alloc_sbuf_tensor_at(name, list(shape), dt, offset=self.at)
        self.at += (size + 31) // 32 * 32
        return t


def build(nc, x, norm_mix_g, w_in, q_norm_g, k_norm_g, attn_out_g, conv_w, conv_b, conv_ln_g,
          conv_ln_b, w_out, norm_ffn_g, peer_wq, peer_k1, peer_k2, peer_u, peer_v, out):
    keep = Map(nc, nc.sbuf_base)
    ident = keep.tile("ident", [P, P], F32)
    ident_b = keep.tile("ident_b", [P, P], BF16)
    mask_band = keep.tile("mask_band", [P, MASK_SPAN + SEQ], BF16)
    kT = keep.tile("kT", [P, AB, SEQ], F32)
    vals = keep.tile("vals", [P, CHUNKS, AW], F32)
    keys_bd = keep.tile("keys_bd", [P, PH, 2 * NKEYS], F32)
    NVEC = KT_D + 4 * CB + 2
    vec = keep.tile("vec", [P, NVEC], F32)
    iota16 = keep.tile("iota16", [P, TOPK], F32)
    taps = keep.tile("taps", [P, CB, TAPS], F32)
    g_mix = vec[:, 0:KT_D]
    g_attn = vec[:, KT_D:KT_D + AB]
    b_conv = vec[:, KT_D + AB:KT_D + 2 * AB]
    g_ln = vec[:, KT_D + 2 * AB:KT_D + 3 * AB]
    b_ln = vec[:, KT_D + 3 * AB:KT_D + 4 * AB]
    g_q = vec[:, NVEC - 2:NVEC - 1]
    g_k = vec[:, NVEC - 1:NVEC]

    qT_spill = nc.dram_tensor("qT_spill", [CHUNKS, P, AW], F32, kind="Internal").ap()
    hT_spill = nc.dram_tensor("hT_spill", [P, CB, HALO + SEQ], F32, kind="Internal").ap()
    psum = nc.alloc_psum_tensor("psum", [P, 8, BANK], F32)

    phase0(nc, keep.at, psum, ident, ident_b, mask_band, kT, vals, keys_bd, vec, iota16, taps, g_mix,
           g_q, g_k, qT_spill, hT_spill, x, norm_mix_g, w_in, q_norm_g,
           k_norm_g, attn_out_g, conv_w, conv_b, conv_ln_g, conv_ln_b, peer_k1, peer_k2)
    phase1(nc, keep.at, psum, ident, ident_b, mask_band, kT, vals, keys_bd, iota16, taps, g_attn,
           b_conv, g_ln, b_ln, qT_spill, hT_spill, x, w_out, norm_ffn_g, peer_wq, peer_u, peer_v, out)


def phase0(nc, base, psum, ident, ident_b, mask_band, kT, vals, keys_bd, vec, iota16, taps, g_mix,
           g_q, g_k, qT_spill, hT_spill, x, norm_mix_g, w_in, q_norm_g,
           k_norm_g, attn_out_g, conv_w, conv_b, conv_ln_g, conv_ln_b, peer_k1, peer_k2):
    m = Map(nc, base)
    GROUPS = COLS // BANK
    Q, K, V, A, G = range(GROUPS)
    ORDER = (Q, K, A, G, V)
    w_sb = m.tile("w_sb", [P, GROUPS, KT_D, BANK], F32)
    x_in = m.tile("x_in", [P, D], F32)
    xn = m.tile("xn", [P, D], F32)
    xnT = m.tile("xnT", [P, KT_D, P], F32)
    squares = m.tile("squares", [P, 2 * AW], F32)
    qn = m.tile("qn", [P, AW], F32)
    kn = m.tile("kn", [P, AW], F32)
    qT_out = m.tile("qT_out", [P, AW], F32)
    sig = m.tile("sig", [P, CW], F32)
    glu = m.tile("glu", [P, CW], F32)
    hT_out = m.tile("hT_out", [P, CB, P], F32)
    before = m.tile("before", [P, CB, HALO], F32)
    rows = m.tile("rows", [P, P], F32)
    taps_row = m.tile("taps_row", [TAPS, CW], F32)
    keys = m.tile("keys", [P, PH, 2, HALF], F32)
    x_stat = m.tile("x_stat", [P, 4], F32)
    qk_stat = m.tile("qk_stat", [P, 4, 2 * HEADS], F32)
    assert m.at <= nc.sbuf_usable_end
    NVEC = vec.shape[1]

    ps = [psum[:, g, :] for g in range(GROUPS)]
    tA, tB, tC = psum[:, 5, :], psum[:, 6, :], psum[:, 7, :]

    sem = nc.alloc_semaphore
    small_in, w_loaded = sem("small_in"), [sem(f"w_loaded{g}") for g in range(GROUPS)]
    x_loaded, consts, zeroed, setup_T, setup_copied = (
        sem("x_loaded"), sem("consts"), sem("zeroed"), sem("setup_T"), sem("setup_copied"))
    x_squared, x_meaned, x_rooted, x_recip, x_normed = (
        sem("x_squared"), sem("x_meaned"), sem("x_rooted"), sem("x_recip"), sem("x_normed"))
    xT_ready, xT_copied = sem("xT_ready"), sem("xT_copied")
    projected = [sem(f"projected{g}") for g in range(GROUPS)]
    qk_squared, qk_summed, qk_meaned, qk_rooted, qk_recip, q_normed, k_normed = (
        sem("qk_squared"), sem("qk_summed"), sem("qk_meaned"), sem("qk_rooted"), sem("qk_recip"),
        sem("q_normed"), sem("k_normed"))
    qT_ready, kT_ready, hT_ready = sem("qT_ready"), sem("kT_ready"), sem("hT_ready")
    qT_copied, kT_copied, hT_copied, v_copied = (
        sem("qT_copied"), sem("kT_copied"), sem("hT_copied"), sem("v_copied"))
    gated, glu_done = sem("gated"), sem("glu_done")
    qT_stored, hT_stored, zeros_stored = sem("qT_stored"), sem("hT_stored"), sem("zeros_stored")
    NSMALL = 10

    with nc.Block() as block:

        @block.sync
        def _(sp):
            r = 0
            for v, n in ((norm_mix_g, KT_D), (attn_out_g, AB), (conv_b, CB), (conv_ln_g, CB),
                         (conv_ln_b, CB)):
                sp.dma_start(rows[r:r + n, :], v[0, :].rearrange("(n p) -> n p", p=P)).then_inc(small_in, 16)
                r += n
            for v in (q_norm_g, k_norm_g):
                sp.dma_start(rows[r:r + 1, :].rearrange("o (two d) -> o two d", two=2),
                             v[0:1, :].unsqueeze(1).to_broadcast([1, 2, HD])).then_inc(small_in, 16)
                r += 1
            sp.dma_start(taps_row[:, :], conv_w[0, :, :]).then_inc(small_in, 16)
            for n, k in enumerate((peer_k1, peer_k2)):
                sp.dma_start(keys[:, :, n, :], k[0].rearrange("h n d -> n h d")).then_inc(small_in, 16)
            sp.dma_start(x_in[:, :], x[0, 0:P, :]).then_inc(x_loaded, 16)
            for g in ORDER:
                sp.dma_start(w_sb[:, g, :, :], w_in[0, :, g * BANK:(g + 1) * BANK]
                             .rearrange("(k p) n -> p k n", p=P)).then_inc(w_loaded[g], 16)

            def next_x(i):
                sp.wait_ge(x_normed, i + 1)
                sp.dma_start(x_in[:, :], x[0, bass.ds((i + 1) * P, P), :]).then_inc(x_loaded, 16)

            def store_q(i):
                sp.wait_ge(qT_copied, i + 1)
                sp.dma_start(qT_spill[bass.ds(i, 1), :, :].rearrange("o p n -> (o p) n"),
                             qT_out[:, :]).then_inc(qT_stored, 16)

            def store_h(i):
                sp.wait_ge(hT_copied, i + 1)
                sp.dma_start(hT_spill[:, :, bass.ds(i * P + HALO, P)], hT_out[:, :, :]).then_inc(hT_stored, 16)

            next_x(0)
            sp.wait_ge(zeroed, 6)
            sp.dma_start(hT_spill[:, :, 0:HALO], before[:, :, :]).then_inc(zeros_stored, 16)
            store_q(0)
            store_h(0)
            with sp.Fori(1, CHUNKS - 1) as i:
                next_x(i)
                store_q(i)
                store_h(i)
            store_q(CHUNKS - 1)
            store_h(CHUNKS - 1)
            sp.wait_ge(zeros_stored, 16)
            sp.wait_ge(qT_stored, 16 * CHUNKS)
            sp.wait_ge(hT_stored, 16 * CHUNKS)

        @block.gpsimd
        def _(pool):
            nc.gpsimd.memset(ident[:, :], 0.0).then_inc(zeroed, 1)
            nc.gpsimd.memset(mask_band[:, :], 0.0).then_inc(zeroed, 1)
            pool.wait_ge(zeroed, 2)
            nc.gpsimd.affine_select(out=ident[:, :], in_=ident[:, :], compare_op=ALU.not_equal, fill=1.0,
                                    base=0, pattern=[[-1, P]], channel_multiplier=1).then_inc(consts, 1)
            nc.gpsimd.affine_select(out=mask_band[:, :], in_=mask_band[:, :], compare_op=ALU.is_gt, fill=NEG,
                                    base=MASK_SPAN, pattern=[[-1, MASK_SPAN + SEQ]],
                                    channel_multiplier=1).then_inc(consts, 1)
            nc.gpsimd.iota(iota16[:, :], pattern=[[1, TOPK]], base=0, channel_multiplier=0,
                           allow_small_or_imprecise_dtypes=True).then_inc(consts, 1)
            pool.wait_ge(consts, 3)
            nc.gpsimd.tensor_copy(ident_b[:, :], ident[:, :]).then_inc(consts, 1)
            nc.gpsimd.memset(kT[:, :, :], 0.0).then_inc(zeroed, 1)
            nc.gpsimd.memset(vals[:, :, :], 0.0).then_inc(zeroed, 1)
            nc.gpsimd.memset(keys_bd[:, :, :], 0.0).then_inc(zeroed, 1)
            nc.gpsimd.memset(before[:, :, :], 0.0).then_inc(zeroed, 1)

        @block.tensor
        def _(pe):
            pe.wait_ge(consts, 4)
            pe.wait_ge(small_in, 16 * NSMALL)
            nc.tensor.transpose(tC[:, 0:NVEC], rows[0:NVEC, :], ident[0:NVEC, 0:NVEC])
            for c in range(CB):
                last = nc.tensor.transpose(tC[:, P + c * 32:P + c * 32 + TAPS],
                                           taps_row[:, c * P:(c + 1) * P], ident[0:TAPS, 0:TAPS])
            for h in range(PH):
                t = (tA, tB)[h // 4]
                last = nc.tensor.transpose(t[:, (h % 4) * P:(h % 4 + 1) * P],
                                           keys[:, h, :, :].rearrange("p a d -> p (a d)"), ident[:, :])
            last.then_inc(setup_T, 1)

            def transpose_x(i):
                pe.wait_ge(x_normed, i + 1)
                pe.wait_ge(setup_copied, 4)
                if not isinstance(i, int) or i:
                    pe.wait_ge(hT_copied, i)
                    pe.wait_ge(kT_copied, i)
                for k in range(KT_D):
                    last = nc.tensor.transpose((tA, tB)[k // 4][:, (k % 4) * P:(k % 4 + 1) * P],
                                               xn[:, k * P:(k + 1) * P], ident[:, :])
                    if k % 4 == 3:
                        last.then_inc(xT_ready, 1)

            def project(i, g):
                if isinstance(i, int) and i == 0:
                    pe.wait_ge(w_loaded[g], 16)
                else:
                    readers = {Q: (q_normed, i), K: (k_normed, i), V: (v_copied, i),
                               A: (glu_done, i), G: (gated, i)}
                    pe.wait_ge(*readers[g])
                for k in range(KT_D):
                    if g == Q:
                        pe.wait_ge(xT_copied, KT_D * i + k + 1)
                    last = nc.tensor.matmul(ps[g], xnT[:, k, :], w_sb[:, g, k, :],
                                            start=k == 0, stop=k == KT_D - 1)
                last.then_inc(projected[g], 1)

            def transpose_qkh(i):
                pe.wait_ge(xT_copied, KT_D * (i + 1))
                pe.wait_ge(q_normed, i + 1)
                for b in range(AB):
                    last = nc.tensor.transpose(tA[:, b * P:(b + 1) * P], qn[:, b * P:(b + 1) * P], ident[:, :])
                last.then_inc(qT_ready, 1)
                pe.wait_ge(k_normed, i + 1)
                for b in range(AB):
                    last = nc.tensor.transpose(tB[:, b * P:(b + 1) * P], kn[:, b * P:(b + 1) * P], ident[:, :])
                last.then_inc(kT_ready, 1)
                pe.wait_ge(qT_copied, i + 1)
                pe.wait_ge(glu_done, i + 1)
                for c in range(CB):
                    last = nc.tensor.transpose(tA[:, c * P:(c + 1) * P], glu[:, c * P:(c + 1) * P], ident[:, :])
                last.then_inc(hT_ready, 1)

            def chunk(i):
                transpose_x(i)
                for g in ORDER:
                    project(i, g)
                transpose_qkh(i)

            chunk(0)
            with pe.Fori(1, CHUNKS) as i:
                chunk(i)

        @block.scalar
        def _(act):
            def square_x(i):
                act.wait_ge(x_loaded, 16 * (i + 1))
                if not isinstance(i, int) or i:
                    act.wait_ge(xT_ready, 2 * i)
                    act.wait_ge(x_meaned, i)
                nc.scalar.activation(xn[:, :], x_in[:, :], ACT.Square, accum_out=x_stat[:, 0:1]).then_inc(x_squared, 1)

            def root_x(i):
                act.wait_ge(x_meaned, i + 1)
                if not isinstance(i, int) or i:
                    act.wait_ge(x_recip, i)
                nc.scalar.activation(x_stat[:, 2:3], x_stat[:, 1:2], ACT.Sqrt).then_inc(x_rooted, 1)

            def copy_xT(i):
                act.wait_ge(setup_copied, 1)
                if not isinstance(i, int) or i:
                    act.wait_ge(projected[V], i)
                for k in range(KT_D):
                    if k % 4 == 0:
                        act.wait_ge(xT_ready, 2 * i + k // 4 + 1)
                    nc.scalar.activation(xnT[:, k, :], (tA, tB)[k // 4][:, (k % 4) * P:(k % 4 + 1) * P],
                                         ACT.Copy, scale=g_mix[:, k:k + 1]).then_inc(xT_copied, 1)

            def square_qk(i):
                if not isinstance(i, int) or i:
                    act.wait_ge(qk_summed, i)
                for n, g in enumerate((Q, K)):
                    act.wait_ge(projected[g], i + 1)
                    nc.scalar.activation(squares[:, n * AW:(n + 1) * AW], ps[g], ACT.Square).then_inc(qk_squared, 1)

            def gate(i):
                act.wait_ge(projected[G], i + 1)
                if not isinstance(i, int) or i:
                    act.wait_ge(glu_done, i)
                nc.scalar.activation(sig[:, :], ps[G], ACT.Sigmoid).then_inc(gated, 1)

            def root_qk(i):
                act.wait_ge(qk_meaned, 2 * (i + 1))
                if not isinstance(i, int) or i:
                    act.wait_ge(qk_recip, i)
                nc.scalar.activation(qk_stat[:, 2, :], qk_stat[:, 1, :], ACT.Sqrt).then_inc(qk_rooted, 1)

            def copy_v(i):
                act.wait_ge(projected[V], i + 1)
                act.wait_ge(zeroed, 6)
                nc.scalar.activation(vals[:, bass.ds(i, 1), :].rearrange("p o n -> p (o n)"), ps[V],
                                     ACT.Copy).then_inc(v_copied, 1)

            def copy_qkh(i):
                act.wait_ge(qT_ready, i + 1)
                if not isinstance(i, int) or i:
                    act.wait_ge(qT_stored, 16 * i)
                nc.scalar.activation(qT_out[:, :], tA, ACT.Copy, scale=g_q).then_inc(qT_copied, 1)
                act.wait_ge(kT_ready, i + 1)
                nc.scalar.activation(kT[:, :, bass.ds(i * P, P)], tB.rearrange("p (b t) -> p b t", b=AB),
                                     ACT.Copy, scale=g_k).then_inc(kT_copied, 1)
                act.wait_ge(hT_ready, i + 1)
                if not isinstance(i, int) or i:
                    act.wait_ge(hT_stored, 16 * i)
                nc.scalar.activation(hT_out[:, :, :], tA.rearrange("p (b t) -> p b t", b=CB),
                                     ACT.Copy).then_inc(hT_copied, 1)

            def chunk(i, last=False):
                copy_xT(i)
                square_qk(i)
                gate(i)
                root_qk(i)
                if not last:
                    square_x(i + 1)
                    root_x(i + 1)
                copy_v(i)
                copy_qkh(i)

            square_x(0)
            root_x(0)
            chunk(0)
            with act.Fori(1, CHUNKS - 1) as i:
                chunk(i)
            chunk(CHUNKS - 1, last=True)

        @block.vector
        def _(dve):
            def norm_x(i):
                dve.wait_ge(x_squared, i + 1)
                if not isinstance(i, int) or i:
                    dve.wait_ge(x_rooted, i)
                nc.vector.tensor_scalar(x_stat[:, 1:2], x_stat[:, 0:1], 1.0 / D, EPS, ALU.mult, ALU.add).then_inc(x_meaned, 1)
                dve.wait_ge(x_rooted, i + 1)
                if not isinstance(i, int) or i:
                    dve.wait_ge(x_normed, i)
                nc.vector.reciprocal(x_stat[:, 3:4], x_stat[:, 2:3]).then_inc(x_recip, 1)
                dve.wait_ge(x_recip, i + 1)
                nc.vector.tensor_scalar(xn[:, :], x_in[:, :], x_stat[:, 3:4], None, ALU.mult).then_inc(x_normed, 1)

            def norm_qk(i):
                dve.wait_ge(qk_squared, 2 * (i + 1))
                if not isinstance(i, int) or i:
                    dve.wait_ge(qk_meaned, 2 * i)
                nc.vector.reduce_sum(qk_stat[:, 0, :], squares[:, :].rearrange("p (h d) -> p h d", d=HD),
                                     AXX).then_inc(qk_summed, 1)
                dve.wait_ge(qk_summed, i + 1)
                if not isinstance(i, int) or i:
                    dve.wait_ge(qk_rooted, i)
                nc.vector.tensor_scalar(qk_stat[:, 1, 0:HEADS], qk_stat[:, 0, 0:HEADS], 1.0, HD * EPS,
                                        ALU.mult, ALU.add).then_inc(qk_meaned, 1)
                nc.vector.tensor_scalar(qk_stat[:, 1, HEADS:], qk_stat[:, 0, HEADS:], 1.0 / HD, EPS,
                                        ALU.mult, ALU.add).then_inc(qk_meaned, 1)

            def scale_qk(i):
                dve.wait_ge(qk_rooted, i + 1)
                if not isinstance(i, int) or i:
                    dve.wait_ge(k_normed, i)
                nc.vector.reciprocal(qk_stat[:, 3, :], qk_stat[:, 2, :]).then_inc(qk_recip, 1)
                dve.wait_ge(qk_recip, i + 1)
                for n, (g, to, done, used) in enumerate(((Q, qn, q_normed, qT_ready), (K, kn, k_normed, kT_ready))):
                    if not isinstance(i, int) or i:
                        dve.wait_ge(used, i)
                    nc.vector.tensor_tensor(to[:, :].rearrange("p (h d) -> p h d", d=HD),
                                            ps[g].rearrange("p (h d) -> p h d", d=HD),
                                            spread(qk_stat[:, 3, n * HEADS:], [[1, HEADS], [0, HD]]),
                                            ALU.mult).then_inc(done, 1)

            def glu_(i):
                dve.wait_ge(gated, i + 1)
                dve.wait_ge(projected[A], i + 1)
                if not isinstance(i, int) or i:
                    dve.wait_ge(hT_ready, i)
                nc.vector.tensor_tensor(glu[:, :], ps[A], sig[:, :], ALU.mult).then_inc(glu_done, 1)

            def chunk(i, last=False):
                norm_qk(i)
                scale_qk(i)
                glu_(i)
                if not last:
                    norm_x(i + 1)

            norm_x(0)
            dve.wait_ge(setup_T, 1)
            dve.wait_ge(zeroed, 6)
            nc.vector.tensor_copy(vec[:, :], tC[:, 0:NVEC]).then_inc(setup_copied, 1)
            nc.vector.tensor_copy(taps[:, :, :], tC[:, P:P + CB * 32].rearrange("p (c t) -> p c t", t=32)[:, :, 0:TAPS]).then_inc(setup_copied, 1)
            for half, (lo, hi) in enumerate(((0, HALF), (HALF, P))):
                for t, bank in enumerate((tA, tB)):
                    copied = nc.vector.tensor_copy(
                        keys_bd[lo:hi, 4 * t:4 * t + 4, half * NKEYS:(half + 1) * NKEYS],
                        bank[lo:hi, :].rearrange("p (h n) -> p h n", n=NKEYS))
            copied.then_inc(setup_copied, 2)
            dve.wait_ge(setup_copied, 4)

            chunk(0)
            with dve.Fori(1, CHUNKS - 1) as i:
                chunk(i)
            chunk(CHUNKS - 1, last=True)


def phase1(nc, base, psum, ident, ident_b, mask_band, kT, vals, keys_bd, iota16, taps, g_attn,
           b_conv, g_ln, b_ln, qT_spill, hT_spill, x, w_out, norm_ffn_g, peer_wq, peer_u, peer_v, out):
    m = Map(nc, base)
    wo_sb = m.tile("wo_sb", [P, KT_D, D], F32)
    wq_sb = m.tile("wq_sb", [P, KT_D, D], F32)
    ring = {kind: m.tile(f"ring_{kind}", [P, RING, D], F32) for kind in "uv"}
    h_res = m.tile("h_res", [P, D], F32)
    g_ffn = m.tile("g_ffn", [P, D], F32)
    hn_next = m.tile("hn_next", [P, D], F32)
    hn = m.tile("hn", [P, D], F32)
    y_out = m.tile("y_out", [P, D], F32)
    actT = m.tile("actT", [P, KT_D, P], F32)
    qT = m.tile("qT", [P, AB, P], F32)
    diag = m.tile("diag", [P, TOPK, P], F32)
    log_keep = [m.tile(f"log_keep{n}", [P, SEQ], F32) for n in range(2)]
    relu_z = [m.tile(f"relu_z{n}", [P, SEQ], F32) for n in range(2)]
    attT = m.tile("attT", [P, CHUNKS, P], F32)
    conv_in = m.tile("conv_in", [P, CB, HALO + P], F32)
    acc = m.tile("acc", [P, CB, P], F32)
    small = Map(nc, m.at)
    bn = small.tile("bn", [P, 6], F32)
    ln_stat = small.tile("ln_stat", [P, 8], F32)
    experts_next = small.tile("experts_next", [P, ROWS], I32)
    experts = small.tile("experts", [P, ROWS], I32)
    gates_next = small.tile("gates_next", [P, ROWS], F32)
    gates = small.tile("gates", [P, ROWS], F32)
    dots = small.tile("dots", [P, ROWS], F32)
    geld = small.tile("geld", [P, ROWS], F32)
    weights = small.tile("weights", [P, ROWS], F32)
    top_v = small.tile("top_v", [P, PH, 2, TOPK], F32)
    top_i = small.tile("top_i", [P, PH, 2, TOPK], U32)
    best_v = small.tile("best_v", [P, PH, TOPK], F32)
    best_i = small.tile("best_i", [P, PH, TOPK], U32)
    stat = small.tile("stat", [P, 8], F32)
    gate_sum = small.tile("gate_sum", [P, 2, PH], F32)
    assert small.at <= nc.sbuf_usable_end

    o_norm = log_keep[0][:, 0:AW]
    qhT = log_keep[1][:, :].rearrange("p (h t) -> p h t", t=P)
    cn = hn_next[:, 0:CW]
    left1 = relu_z[0]
    left2 = relu_z[1]

    y_ps = psum[:, 0:2, :].rearrange("p b n -> p (b n)")
    z_ps = [psum[:, 2 + 2 * n:4 + 2 * n, :].rearrange("p b n -> p (b n)") for n in range(2)]
    t_ps, o_ps = psum[:, 6, :], psum[:, 7, :]

    def score(h, half):
        at = (h % 4) * 2 * NKEYS + half * NKEYS
        return z_ps[h // 4][:, at:at + NKEYS]

    def left(h, half):
        n = 2 * h + half
        return (left1 if n < 8 else left2)[:, (n % 8) * NKEYS:(n % 8 + 1) * NKEYS]

    cand = [log_keep[n][:, :].rearrange("p (h c) -> p h c", c=TOPK * TOPK) for n in range(2)]

    sem = nc.alloc_semaphore
    wo_loaded, wq_loaded, g_loaded = sem("wo_loaded"), sem("wq_loaded"), sem("g_loaded")
    x_in, q_in, c_in, y_stored = sem("x_in"), sem("q_in"), sem("c_in"), sem("y_stored")
    tapped, conv_T, bn_done, ln_done, ln_eps, ln_rooted, ln_recip, cn_done, cT_ready, swished = (
        sem("tapped"), sem("conv_T"), sem("bn_done"), sem("ln_done"), sem("ln_eps"), sem("ln_rooted"),
        sem("ln_recip"), sem("cn_done"), sem("cT_ready"), sem("swished"))
    TAP_OPS = TAPS * CB
    z_ready, abs_done, exp_done, ln_done1, relu_done = (
        sem("z_ready"), sem("abs_done"), sem("exp_done"), sem("ln_done1"), sem("relu_done"))
    summed, stick, att_done, att_T, att_copied, attended = (
        sem("summed"), sem("stick"), sem("att_done"), sem("att_T"), sem("att_copied"), sem("attended"))
    o_squared, o_meaned, o_rooted, o_recip, o_normed, o_T, o_copied = (
        sem("o_squared"), sem("o_meaned"), sem("o_rooted"), sem("o_recip"), sem("o_normed"),
        sem("o_T"), sem("o_copied"))
    mixed, h_done, h_squared, h_meaned, h_rooted, h_recip, h_normed = (
        sem("mixed"), sem("h_done"), sem("h_squared"), sem("h_meaned"), sem("h_rooted"),
        sem("h_recip"), sem("h_normed"))
    h_T, h_copied, queried, queries_copied, scored = (
        sem("h_T"), sem("h_copied"), sem("queried"), sem("queries_copied"), sem("scored"))
    top8, index8, replaced, top16, index16 = (
        sem("top8"), sem("index8"), sem("replaced"), sem("top16"), sem("index16"))
    top_floated, cand_done = sem("top_floated"), sem("cand_done")
    best8, bindex8, breplaced, best16, bindex16 = (
        sem("best8"), sem("bindex8"), sem("breplaced"), sem("best16"), sem("bindex16"))
    split, split_f, matched, picked, looked, experts_done = (
        sem("split"), sem("split_f"), sem("matched"), sem("picked"), sem("looked"), sem("experts_done"))
    g_shifted, g_exped, g_summed, g_recip, gates_done = (
        sem("g_shifted"), sem("g_exped"), sem("g_summed"), sem("g_recip"), sem("gates_done"))
    taken, experts_live, gates_live = sem("taken"), sem("experts_live"), sem("gates_live")
    row_in = {kind: [sem(f"{kind}_in{n}") for n in range(RING)] for kind in "uv"}
    dotted, gelued, weighted, diagonal, y_begun, row_added, y_copied = (
        sem("dotted"), sem("gelued"), sem("weighted"), sem("diagonal"), sem("y_begun"),
        sem("row_added"), sem("y_copied"))

    dve_passed, pool_passed = sem("dve_passed1"), sem("pool_passed")
    HALF_ROWS = TOPK // 2
    later = lambda i: not isinstance(i, int) or i > 0
    WAITS_TOP = 2 * PH

    SPANS = ((0, 1, 2 * P), (1, 2, 2 * P), (2, 3, 4 * P), (3, CHUNKS, SEQ))

    def over_chunks(eng, step):
        step(None, 0, SPANS[0][2])
        for lo, hi, keys in SPANS[1:]:
            if hi - lo == 1:
                step(lo - 1, lo, keys)
            else:
                with eng.Fori(lo, hi) as f:
                    step(f - 1, f, keys)
        step(CHUNKS - 1, None, 0)

    with nc.Block() as block:

        @block.sync
        def _(sp):
            sp.dma_start(g_ffn[:, :], norm_ffn_g[0:1, :].to_broadcast([P, D])).then_inc(g_loaded, 16)

            def load_front(f):
                if later(f):
                    sp.wait_ge(z_ready, HEADS * f)
                sp.dma_start(qT[:, :, :].rearrange("p b t -> p (b t)"),
                             qT_spill[bass.ds(f, 1), :, :].rearrange("o p n -> (o p) n")).then_inc(q_in, 16)
                if later(f):
                    sp.wait_ge(tapped, TAP_OPS * f)
                sp.dma_start(conv_in[:, :, :], hT_spill[:, :, bass.ds(f * P, HALO + P)]).then_inc(c_in, 16)
                if later(f):
                    sp.wait_ge(y_begun, f)
                sp.dma_start(h_res[:, :], x[0, bass.ds(f * P, P), :]).then_inc(x_in, 16)

            def store(c):
                sp.wait_ge(y_copied, c + 1)
                sp.dma_start(out[0, bass.ds(c * P, P), :], y_out[:, :]).then_inc(y_stored, 16)

            def step(c, f, keys):
                if f is not None:
                    load_front(f)
                if c is None:
                    for w, to, loaded in ((w_out, wo_sb, wo_loaded), (peer_wq, wq_sb, wq_loaded)):
                        sp.dma_start(to[:, :, :], w[0].rearrange("(k p) n -> p k n", p=P)).then_inc(loaded, 16)
                elif later(c):
                    store(c - 1)

            over_chunks(sp, step)
            store(CHUNKS - 1)
            sp.wait_ge(y_stored, 16 * CHUNKS)

        @block.gpsimd
        def _(pool):
            def step(c, f, keys):
                if c is None:
                    return
                hold(pool, experts_live, 2 * c + 1, pool_passed)
                for s in range(SLOTS):
                    if s == TABLE_PART:
                        hold(pool, experts_live, 2 * c + 2, pool_passed)
                    gather("u", c, s)
                    if s >= LAG:
                        gather("v", c, s - LAG)
                    elif later(c):
                        gather("v", c - 1, s - LAG + ROWS)

            def gather(kind, c, e):
                if e >= RING or later(c):
                    hold(pool, dotted if kind == "u" else row_added, ROWS * c + e - RING + 1, pool_passed)
                nc.gpsimd.indirect_dma_start(
                    ring[kind][:, e % RING, :], None, peer_u[0] if kind == "u" else peer_v[0],
                    bass.IndirectOffsetOnAxis(experts[:, e:e + 1], 0)).then_inc(row_in[kind][e % RING], 16)

            def tail():
                for e in range(ROWS - LAG, ROWS):
                    gather("v", CHUNKS - 1, e)

            over_chunks(pool, step)
            tail()

        @block.tensor
        def _(pe):
            def scores(f, a, keys):
                z = z_ps[a % 2]
                if a == 0:
                    pe.wait_ge(q_in, 16 * (f + 1))
                if a < 2:
                    if later(f):
                        pe.wait_ge(replaced, WAITS_TOP * f)
                        pe.wait_ge(index8, WAITS_TOP * f)
                else:
                    pe.wait_ge(stick, HEADS * f + a - 1)
                lo = HD * (a % 2)
                for s in range(0, keys, BANK):
                    n = min(BANK, keys - s)
                    nc.tensor.matmul(z[:, s:s + n], qT[lo:lo + HD, a // 2, :], kT[lo:lo + HD, a // 2, s:s + n],
                                     start=True, stop=False)
                    last = nc.tensor.matmul(z[:, s:s + n], ident_b[:, :],
                                            mask_band[:, bass.ds(s + MASK_SPAN - f * P, n)],
                                            start=False, stop=True)
                last.then_inc(z_ready, 1)

            def transpose_weights(f, a, half, keys):
                blocks = keys // P
                pe.wait_ge(att_done, HEADS * f + a + 1)
                if a or half:
                    pe.wait_ge(att_copied, 2 * HEADS * f + 2 * a + half)
                elif later(f):
                    pe.wait_ge(o_copied, AB * f)
                for b in range(blocks // 2):
                    s = (half * blocks // 2 + b) * P
                    last = nc.tensor.transpose(t_ps[:, b * P:(b + 1) * P],
                                               log_keep[a % 2][:, s:s + P], ident[:, :])
                last.then_inc(att_T, 1)

            def attend(f, a, keys):
                blocks = keys // P
                if a == 0 and later(f):
                    pe.wait_ge(o_normed, f)
                for b in range(blocks):
                    if b in (0, blocks // 2):
                        pe.wait_ge(att_copied, 2 * HEADS * f + 2 * a + 1 + (b > 0))
                    last = nc.tensor.matmul(o_ps[:, a * HD:(a + 1) * HD], attT[:, b, :],
                                            vals[:, b, a * HD:(a + 1) * HD], start=b == 0, stop=b == blocks - 1)
                last.then_inc(attended, 1)

            def transpose_conv(f):
                pe.wait_ge(tapped, TAP_OPS * (f + 1))
                pe.wait_ge(stick, HEADS * (f + 1))
                for c in range(CB):
                    last = nc.tensor.transpose(z_ps[1][:, c * P:(c + 1) * P], acc[:, c, :], ident[:, :])
                last.then_inc(conv_T, 1)

            def transpose_conv_back(f):
                pe.wait_ge(cn_done, f + 1)
                for c in range(CB):
                    last = nc.tensor.transpose(z_ps[1][:, BANK + c * P:BANK + (c + 1) * P], cn[:, c * P:(c + 1) * P],
                                               ident[:, :])
                last.then_inc(cT_ready, 1)

            def transpose_o(f):
                pe.wait_ge(o_normed, f + 1)
                pe.wait_ge(att_copied, 2 * HEADS * (f + 1))
                for b in range(AB):
                    last = nc.tensor.transpose(t_ps[:, b * P:(b + 1) * P], o_norm[:, b * P:(b + 1) * P], ident[:, :])
                last.then_inc(o_T, 1)

            def mix(f, n):
                if n == 0:
                    pe.wait_ge(stick, HEADS * (f + 1))
                    pe.wait_ge(o_copied, AB * (f + 1))
                    pe.wait_ge(swished, CB * (f + 1))
                    if not later(f):
                        pe.wait_ge(wo_loaded, 16)
                total = 2 * KT_D
                for m in range(total * n // MIX_SLOTS, total * (n + 1) // MIX_SLOTS):
                    j, k = m // KT_D, m % KT_D
                    product = nc.tensor.matmul(z_ps[0][:, j * BANK:(j + 1) * BANK], actT[:, k, :],
                                               wo_sb[:, k, j * BANK:(j + 1) * BANK], start=k == 0, stop=k == KT_D - 1)
                    if m == total - 1:
                        product.then_inc(mixed, 1)

            def transpose_h(f):
                pe.wait_ge(h_normed, f + 1)
                for k in range(KT_D):
                    last = nc.tensor.transpose(z_ps[1][:, k * P:(k + 1) * P], hn_next[:, k * P:(k + 1) * P], ident[:, :])
                    if k % 4 == 3:
                        last.then_inc(h_T, 1)

            def query(f, n):
                if n == 0:
                    pe.wait_ge(h_copied, 2 * (f + 1))
                    pe.wait_ge(h_done, f + 1)
                    if not later(f):
                        pe.wait_ge(wq_loaded, 16)
                total = PH * KT_D
                for m in range(total * n // QUERY_SLOTS, total * (n + 1) // QUERY_SLOTS):
                    h, k = m // KT_D, m % KT_D
                    product = nc.tensor.matmul(z_ps[0][:, h * P:(h + 1) * P], wq_sb[:, k, h * P:(h + 1) * P],
                                               actT[:, k, :], start=k == 0, stop=k == KT_D - 1)
                    if m == total - 1:
                        product.then_inc(queried, 1)

            def score_keys(f, pair):
                pe.wait_ge(queries_copied, f + 1)
                for h in (2 * pair, 2 * pair + 1):
                    last = nc.tensor.matmul(z_ps[h // 4][:, (h % 4) * 2 * NKEYS:(h % 4 + 1) * 2 * NKEYS],
                                            qhT[:, h, :], keys_bd[:, h, :], start=True, stop=True)
                last.then_inc(scored, 1)

            def begin_y(c):
                pe.wait_ge(h_done, c + 1)
                if later(c):
                    pe.wait_ge(y_copied, c)
                for j in range(2):
                    last = nc.tensor.matmul(y_ps[:, j * BANK:(j + 1) * BANK], ident[:, :],
                                            h_res[:, j * BANK:(j + 1) * BANK], start=True, stop=False)
                last.then_inc(y_begun, 1)

            def add_row(c, e):
                if e % HALF_ROWS == 0:
                    pe.wait_ge(diagonal, 2 * PH * c + e // HALF_ROWS + 1)
                pe.wait_ge(row_in["v"][e % RING], 16 * (FILLS * c + e // RING + 1))
                for j in range(2):
                    last = nc.tensor.matmul(y_ps[:, j * BANK:(j + 1) * BANK], diag[:, e % TOPK, :],
                                            ring["v"][:, e % RING, j * BANK:(j + 1) * BANK], start=False,
                                            stop=e == ROWS - 1)
                last.then_inc(row_added, 1)

            def front(f, s, keys):
                for piece, at in ((lambda a: scores(f, a, keys), 0),
                                  (lambda a: transpose_weights(f, a, 0, keys), ATT_T0),
                                  (lambda a: transpose_weights(f, a, 1, keys), ATT_T1),
                                  (lambda a: attend(f, a, keys), ATT_USE)):
                    a, after = divmod(s - ATT0 - at, ATT_STEP)
                    if 0 <= a < HEADS and after == 0:
                        piece(a)
                if s == CONV_T:
                    transpose_conv(f)
                if s == O_T:
                    transpose_o(f)
                if s == CONV_BACK:
                    transpose_conv_back(f)
                if MIX <= s < MIX + MIX_SLOTS:
                    mix(f, s - MIX)
                if s == H_T:
                    transpose_h(f)
                if QUERY <= s < QUERY + QUERY_SLOTS:
                    query(f, s - QUERY)
                if SCORE <= s < SCORE + 4:
                    score_keys(f, s - SCORE)

            def step(c, f, keys):
                for s in range(SLOTS):
                    if c is not None:
                        if s < LAG and later(c):
                            add_row(c - 1, s - LAG + ROWS)
                        if s == LAG:
                            begin_y(c)
                        if s >= LAG:
                            add_row(c, s - LAG)
                    if f is not None:
                        front(f, s, keys)

            over_chunks(pe, step)
            for e in range(ROWS - LAG, ROWS):
                add_row(CHUNKS - 1, e)

        @block.scalar
        def _(act):
            def soften(f, a, keys):
                z, l, r = z_ps[a % 2][:, 0:keys], log_keep[a % 2][:, 0:keys], relu_z[a % 2][:, 0:keys]
                act.wait_ge(z_ready, HEADS * f + a + 1)
                if a >= 2:
                    act.wait_ge(att_T, 2 * (HEADS * f + a - 1))
                    act.wait_ge(summed, HEADS * f + a - 1)
                elif later(f):
                    act.wait_ge(looked, 4 * f)
                    act.wait_ge(bindex16, PH * f)
                nc.scalar.activation(l, z, ACT.Abs).then_inc(abs_done, 1)
                nc.scalar.activation(r, z, ACT.Relu).then_inc(relu_done, 1)
                act.wait_ge(abs_done, HEADS * f + a + 1)
                nc.scalar.activation(l, l, ACT.Exp, scale=-1.0).then_inc(exp_done, 1)
                act.wait_ge(exp_done, HEADS * f + a + 1)
                nc.scalar.activation(l, l, ACT.Ln, bias=1.0).then_inc(ln_done1, 1)

            def weigh(f, a, keys):
                act.wait_ge(stick, HEADS * f + a + 1)
                l = log_keep[a % 2][:, 0:keys]
                nc.scalar.activation(l, l, ACT.Exp).then_inc(att_done, 1)

            def copy_weights(f, a, half, keys):
                blocks = keys // P // 2
                if half == 0 and (a or later(f)):
                    act.wait_ge(attended, HEADS * f + a)
                if half == 0 and a == 0 and later(f):
                    act.wait_ge(experts_done, f)
                act.wait_ge(att_T, 2 * (HEADS * f + a) + half + 1)
                nc.scalar.activation(attT[:, half * blocks:(half + 1) * blocks, :],
                                     t_ps[:, 0:blocks * P].rearrange("p (b t) -> p b t", t=P),
                                     ACT.Copy).then_inc(att_copied, 1)

            def square_o(f):
                act.wait_ge(attended, HEADS * (f + 1))
                act.wait_ge(att_T, 2 * HEADS * (f + 1))
                if later(f):
                    act.wait_ge(o_meaned, f)
                nc.scalar.activation(o_norm, o_ps, ACT.Square, accum_out=stat[:, 0:1]).then_inc(o_squared, 1)

            def root_o(f):
                act.wait_ge(o_meaned, f + 1)
                if later(f):
                    act.wait_ge(o_recip, f)
                nc.scalar.activation(stat[:, 2:3], stat[:, 1:2], ACT.Sqrt).then_inc(o_rooted, 1)

            def copy_o(f):
                act.wait_ge(o_T, f + 1)
                if later(f):
                    act.wait_ge(queried, f)
                for b in range(AB):
                    nc.scalar.activation(actT[:, b, :], t_ps[:, b * P:(b + 1) * P], ACT.Copy,
                                         scale=g_attn[:, b:b + 1]).then_inc(o_copied, 1)

            def root_ln(f):
                act.wait_ge(ln_eps, f + 1)
                if later(f):
                    act.wait_ge(ln_recip, f)
                nc.scalar.activation(ln_stat[:, 3:4], ln_stat[:, 2:3], ACT.Sqrt).then_inc(ln_rooted, 1)

            def swish(f):
                act.wait_ge(cT_ready, f + 1)
                if later(f):
                    act.wait_ge(queried, f)
                for c in range(CB):
                    nc.scalar.activation(actT[:, AB + c, :], z_ps[1][:, BANK + c * P:BANK + (c + 1) * P], ACT.Silu,
                                         bias=b_ln[:, c:c + 1], scale=g_ln[:, c:c + 1]).then_inc(swished, 1)

            def square_h(f):
                act.wait_ge(h_done, f + 1)
                act.wait_ge(cT_ready, f + 1)
                if later(f):
                    act.wait_ge(taken, f)
                    act.wait_ge(h_meaned, f)
                nc.scalar.activation(hn_next[:, :], h_res[:, :], ACT.Square, accum_out=stat[:, 4:5]).then_inc(h_squared, 1)

            def root_h(f):
                act.wait_ge(h_meaned, f + 1)
                if later(f):
                    act.wait_ge(h_recip, f)
                nc.scalar.activation(stat[:, 6:7], stat[:, 5:6], ACT.Sqrt).then_inc(h_rooted, 1)

            def copy_h(f):
                act.wait_ge(mixed, f + 1)
                for j in range(2):
                    act.wait_ge(h_T, 2 * f + j + 1)
                    nc.scalar.activation(actT[:, 4 * j:4 * j + 4, :],
                                         z_ps[1][:, j * BANK:(j + 1) * BANK].rearrange("p (b t) -> p b t", t=P),
                                         ACT.Copy).then_inc(h_copied, 1)

            def copy_queries(f):
                act.wait_ge(queried, f + 1)
                nc.scalar.activation(qhT[:, :, :], z_ps[0].rearrange("p (h t) -> p h t", t=P),
                                     ACT.Copy).then_inc(queries_copied, 1)

            def exp_gates(f):
                act.wait_ge(g_shifted, f + 1)
                nc.scalar.activation(gates_next[:, :], gates_next[:, :], ACT.Exp).then_inc(g_exped, 1)

            def gelu(c, w):
                act.wait_ge(dotted, ROWS * c + TOPK * (w + 1))
                if w or later(c):
                    act.wait_ge(weighted, PH * c + w)
                nc.scalar.activation(geld[:, w * TOPK:(w + 1) * TOPK], dots[:, w * TOPK:(w + 1) * TOPK],
                                     ACT.Gelu).then_inc(gelued, 1)

            def copy_y(c):
                act.wait_ge(row_added, ROWS * (c + 1))
                if later(c):
                    act.wait_ge(y_stored, 16 * c)
                nc.scalar.activation(y_out[:, :], y_ps, ACT.Copy).then_inc(y_copied, 1)

            def front(f, s, keys):
                for piece, at in ((lambda a: copy_weights(f, a, 0, keys), ATT_T0),
                                  (lambda a: copy_weights(f, a, 1, keys), ATT_T1),
                                  (lambda a: soften(f, a, keys), ATT_SOFT),
                                  (lambda a: weigh(f, a, keys), ATT_EXP)):
                    a, after = divmod(s - ATT0 - at, ATT_STEP)
                    if 0 <= a < HEADS and after == 0:
                        piece(a)
                if s == ATT_END:
                    square_o(f)
                if s == O_MEAN:
                    root_o(f)
                if s == LN_STAT + 1:
                    root_ln(f)
                if s == O_T:
                    copy_o(f)
                if s == CONV_BACK:
                    swish(f)
                if s == H_ADD:
                    square_h(f)
                if s == H_MEAN:
                    root_h(f)
                if s == H_T:
                    copy_h(f)
                if s == QUERY + QUERY_SLOTS:
                    copy_queries(f)
                if s == SHIFT:
                    exp_gates(f)

            def step(c, f, keys):
                for s in range(SLOTS):
                    if c is not None:
                        if s == 0 and later(c):
                            gelu(c - 1, PH - 1)
                        if s % TOPK == 0 and s > 0:
                            gelu(c, s // TOPK - 1)
                        if s == LAG and later(c):
                            copy_y(c - 1)
                    if f is not None:
                        if s % TOPK == 0 and s < ATT_END:
                            nc.scalar.preload_act_table_set("natural_log_exp_and_others")
                        front(f, s, keys)

            over_chunks(act, step)
            gelu(CHUNKS - 1, PH - 1)
            copy_y(CHUNKS - 1)

        @block.vector
        def _(dve):
            def accumulate(f, a, keys):
                l, r = log_keep[a % 2], relu_z[a % 2]
                dve.wait_ge(ln_done1, HEADS * f + a + 1)
                dve.wait_ge(relu_done, HEADS * f + a + 1)
                back = slice(keys - 1, None, -1) if keys == SEQ else slice(keys - 1, None, -1)
                nc.vector.tensor_tensor_scan(l[:, back], l[:, back], r[:, back], 0.0, ALU.add, ALU.add).then_inc(summed, 1)
                dve.wait_ge(summed, HEADS * f + a + 1)
                nc.vector.tensor_tensor(l[:, 0:keys], z_ps[a % 2][:, 0:keys], l[:, 0:keys], ALU.subtract).then_inc(stick, 1)

            def mean_o(f):
                dve.wait_ge(o_squared, f + 1)
                if later(f):
                    dve.wait_ge(o_rooted, f)
                nc.vector.tensor_scalar(stat[:, 1:2], stat[:, 0:1], 1.0 / AW, EPS, ALU.mult, ALU.add).then_inc(o_meaned, 1)

            def norm_o(f):
                dve.wait_ge(o_rooted, f + 1)
                if later(f):
                    dve.wait_ge(o_normed, f)
                nc.vector.reciprocal(stat[:, 3:4], stat[:, 2:3]).then_inc(o_recip, 1)
                dve.wait_ge(o_recip, f + 1)
                nc.vector.tensor_scalar(o_norm, o_ps, stat[:, 3:4], None, ALU.mult).then_inc(o_normed, 1)

            def convolve(f, t):
                if t == 0:
                    dve.wait_ge(c_in, 16 * (f + 1))
                    if later(f):
                        dve.wait_ge(conv_T, f)
                else:
                    dve.wait_ge(tapped, TAP_OPS * f + t * CB)
                for c in range(CB):
                    if t == 0:
                        nc.vector.tensor_scalar(acc[:, c, :], conv_in[:, c, 0:P], taps[:, c, 0:1],
                                                b_conv[:, c:c + 1], ALU.mult, ALU.add).then_inc(tapped, 1)
                    else:
                        nc.vector.scalar_tensor_tensor(out=acc[:, c, :], in0=conv_in[:, c, t:t + P],
                                                       scalar=taps[:, c, t:t + 1], in1=acc[:, c, :],
                                                       op0=ALU.mult, op1=ALU.add).then_inc(tapped, 1)

            def ln_stats(f):
                dve.wait_ge(conv_T, f + 1)
                if later(f):
                    dve.wait_ge(ln_done, f)
                nc.vector.bn_stats(bn[:, :], z_ps[1][:, 0:CW]).then_inc(bn_done, 1)
                if later(f):
                    hold(dve, cn_done, f, dve_passed)
                hold(dve, bn_done, f + 1, dve_passed)
                nc.vector.bn_aggr(ln_stat[:, 0:2], bn[:, :]).then_inc(ln_done, 1)
                dve.wait_ge(ln_done, f + 1)
                if later(f):
                    dve.wait_ge(ln_rooted, f)
                nc.vector.tensor_scalar(ln_stat[:, 2:3], ln_stat[:, 1:2], 1.0, EPS, ALU.mult, ALU.add).then_inc(ln_eps, 1)

            def ln_scale(f):
                dve.wait_ge(ln_rooted, f + 1)
                nc.vector.reciprocal(ln_stat[:, 4:5], ln_stat[:, 3:4]).then_inc(ln_recip, 1)
                dve.wait_ge(ln_recip, f + 1)
                if later(f):
                    dve.wait_ge(taken, f)
                    dve.wait_ge(h_T, 2 * f)
                nc.vector.tensor_scalar(cn, z_ps[1][:, 0:CW], ln_stat[:, 0:1], ln_stat[:, 4:5],
                                        ALU.subtract, ALU.mult).then_inc(cn_done, 1)

            def add_residual(f):
                dve.wait_ge(mixed, f + 1)
                dve.wait_ge(x_in, 16 * (f + 1))
                nc.vector.tensor_tensor(h_res[:, :], z_ps[0], h_res[:, :], ALU.add).then_inc(h_done, 1)

            def mean_h(f):
                dve.wait_ge(h_squared, f + 1)
                if later(f):
                    dve.wait_ge(h_rooted, f)
                nc.vector.tensor_scalar(stat[:, 5:6], stat[:, 4:5], 1.0 / D, EPS, ALU.mult, ALU.add).then_inc(h_meaned, 1)

            def norm_h(f):
                dve.wait_ge(h_rooted, f + 1)
                if later(f):
                    dve.wait_ge(h_normed, f)
                else:
                    dve.wait_ge(g_loaded, 16)
                nc.vector.reciprocal(stat[:, 7:8], stat[:, 6:7]).then_inc(h_recip, 1)
                dve.wait_ge(h_recip, f + 1)
                nc.vector.scalar_tensor_tensor(out=hn_next[:, :], in0=h_res[:, :], scalar=stat[:, 7:8],
                                               in1=g_ffn[:, :], op0=ALU.mult, op1=ALU.mult).then_inc(h_normed, 1)

            def search_keys(f, n):
                stage, part = n // 2, n % 2
                halves = [(h, half) for h in range(4 * part, 4 * part + 4) for half in range(2)]
                ended = WAITS_TOP * f + PH * (part + 1)
                if stage == 0:
                    if later(f):
                        hold(dve, cand_done, 2 * f, dve_passed)
                        hold(dve, top_floated, f, dve_passed)
                    hold(dve, scored, 4 * f + 2 * part + 2, dve_passed)
                    for h, half in halves:
                        nc.vector.max(top_v[:, h, half, 0:8], score(h, half)).then_inc(top8, 1)
                elif stage == 1:
                    hold(dve, top8, ended, dve_passed)
                    for h, half in halves:
                        nc.vector.max_index(top_i[:, h, half, 0:8], top_v[:, h, half, 0:8], score(h, half)).then_inc(index8, 1)
                elif stage == 2:
                    for h, half in halves:
                        nc.vector.match_replace(left(h, half), top_v[:, h, half, 0:8], score(h, half), LOWEST).then_inc(replaced, 1)
                elif stage == 3:
                    hold(dve, replaced, ended, dve_passed)
                    for h, half in halves:
                        nc.vector.max(top_v[:, h, half, 8:16], left(h, half)).then_inc(top16, 1)
                else:
                    hold(dve, top16, ended, dve_passed)
                    for h, half in halves:
                        nc.vector.max_index(top_i[:, h, half, 8:16], top_v[:, h, half, 8:16], left(h, half)).then_inc(index16, 1)

            tf = attT[:, 0:2, :].rearrange("p b t -> p (b t)").rearrange("p (h two k) -> p h two k", two=2, k=TOPK)
            parts_i = attT[:, 2:4, :].bitcast(U32).rearrange("p b t -> p (b t)")
            parts = attT[:, 4:6, :].rearrange("p b t -> p (b t)")
            looks = attT[:, 6:8, :].rearrange("p b t -> p (b t)")

            def add_candidates(f, n):
                if n == 0:
                    dve.wait_ge(index16, WAITS_TOP * (f + 1))
                    nc.vector.tensor_copy(tf, top_i[:, :, :, :]).then_inc(top_floated, 1)
                    return
                j = n - 1
                dve.wait_ge(top16, WAITS_TOP * (f + 1))
                nc.vector.tensor_tensor(
                    spread(cand[j], [[256, 4], [TOPK, TOPK], [1, TOPK]]),
                    spread(top_v[:, 4 * j, 0, :], [[2 * TOPK, 4], [1, TOPK], [0, TOPK]]),
                    spread(top_v[:, 4 * j, 1, :], [[2 * TOPK, 4], [0, TOPK], [1, TOPK]]), ALU.add).then_inc(cand_done, 1)

            def search_candidates(f, n):
                stage, part = n // 2, n % 2
                heads = range(4 * part, 4 * part + 4)
                ended = PH * f + 4 * (part + 1)
                if stage == 0:
                    if part == 0 and later(f):
                        hold(dve, split, 2 * f, dve_passed)
                        hold(dve, g_shifted, f, dve_passed)
                    hold(dve, cand_done, 2 * f + part + 1, dve_passed)
                else:
                    hold(dve, (best8, bindex8, breplaced, best16)[stage - 1], ended, dve_passed)
                for h in heads:
                    c = cand[h // 4][:, h % 4, :]
                    if stage == 0:
                        nc.vector.max(best_v[:, h, 0:8], c).then_inc(best8, 1)
                    elif stage == 1:
                        nc.vector.max_index(best_i[:, h, 0:8], best_v[:, h, 0:8], c).then_inc(bindex8, 1)
                    elif stage == 2:
                        nc.vector.match_replace(c, best_v[:, h, 0:8], c, LOWEST).then_inc(breplaced, 1)
                    elif stage == 3:
                        nc.vector.max(best_v[:, h, 8:16], c).then_inc(best16, 1)
                    else:
                        nc.vector.max_index(best_i[:, h, 8:16], best_v[:, h, 8:16], c).then_inc(bindex16, 1)

            def shift_gates(f):
                dve.wait_ge(best16, PH * (f + 1))
                if later(f):
                    dve.wait_ge(gates_live, f)
                nc.vector.tensor_tensor(gates_next[:, :].rearrange("p (h k) -> p h k", k=TOPK), best_v[:, :, :],
                                        spread(best_v[:, 0, 0:1], [[TOPK, PH], [0, TOPK]]), ALU.subtract).then_inc(g_shifted, 1)

            def split_positions(f):
                dve.wait_ge(bindex16, PH * (f + 1))
                pos = best_i[:, :, :].rearrange("p h k -> p (h k)")
                nc.vector.tensor_single_scalar(parts_i[:, 0:ROWS], pos, 4, ALU.logical_shift_right).then_inc(split, 1)
                nc.vector.tensor_single_scalar(parts_i[:, ROWS:], pos, TOPK - 1, ALU.bitwise_and).then_inc(split, 1)
                dve.wait_ge(split, 2 * (f + 1))
                nc.vector.tensor_copy(parts, parts_i).then_inc(split_f, 1)

            def look_up(f, n):
                half, j = n // 2, n % 2
                grid = spread(relu_z[j][:, :], [[256, 4], [TOPK, TOPK], [1, TOPK]])
                dve.wait_ge(split_f, f + 1)
                if half:
                    dve.wait_ge(looked, 4 * f + j + 1)
                nc.vector.tensor_tensor(
                    grid, spread(parts[:, half * ROWS + 4 * j * TOPK:], [[TOPK, 4], [1, TOPK], [0, TOPK]]),
                    spread(iota16[:, :], [[0, 4], [0, TOPK], [1, TOPK]]), ALU.is_equal).then_inc(matched, 1)
                dve.wait_ge(matched, 4 * f + n + 1)
                nc.vector.tensor_tensor(
                    grid, grid, spread(tf[:, 4 * j, half, :], [[2 * TOPK, 4], [0, TOPK], [1, TOPK]]),
                    ALU.mult).then_inc(picked, 1)
                dve.wait_ge(picked, 4 * f + n + 1)
                at = half * ROWS + 4 * j * TOPK
                nc.vector.reduce_sum(looks[:, at:at + 4 * TOPK],
                                     relu_z[j][:, :].rearrange("p (r s) -> p r s", s=TOPK), AXX).then_inc(looked, 1)

            def number_experts(f):
                dve.wait_ge(looked, 4 * (f + 1))
                if later(f):
                    dve.wait_ge(experts_live, 2 * f)
                nc.vector.scalar_tensor_tensor(out=experts_next[:, :], in0=looks[:, 0:ROWS], scalar=float(NKEYS),
                                               in1=looks[:, ROWS:], op0=ALU.mult, op1=ALU.add).then_inc(experts_done, 1)

            def finish_gates(f):
                g = gates_next[:, :].rearrange("p (h k) -> p h k", k=TOPK)
                dve.wait_ge(g_exped, f + 1)
                nc.vector.reduce_sum(gate_sum[:, 0, :], g, AXX).then_inc(g_summed, 1)
                dve.wait_ge(g_summed, f + 1)
                nc.vector.reciprocal(gate_sum[:, 1, :], gate_sum[:, 0, :]).then_inc(g_recip, 1)
                dve.wait_ge(g_recip, f + 1)
                nc.vector.tensor_tensor(g, g, spread(gate_sum[:, 1, :], [[1, PH], [0, TOPK]]), ALU.mult).then_inc(gates_done, 1)

            def table_go_live(c):
                dve.wait_ge(experts_done, c + 1)
                if later(c):
                    dve.wait_ge(dotted, ROWS * (c - 1) + TABLE_PART)
                    dve.wait_ge(row_added, ROWS * (c - 1) + TABLE_PART)
                nc.vector.tensor_copy(experts[:, 0:TABLE_PART], experts_next[:, 0:TABLE_PART]).then_inc(experts_live, 1)

            def hn_go_live(c):
                dve.wait_ge(h_normed, c + 1)
                if later(c):
                    dve.wait_ge(dotted, ROWS * c)
                nc.vector.tensor_copy(hn[:, :], hn_next[:, :]).then_inc(taken, 1)

            def gates_go_live(c):
                dve.wait_ge(gates_done, c + 1)
                if later(c):
                    dve.wait_ge(weighted, PH * c)
                nc.vector.tensor_copy(gates[:, :], gates_next[:, :]).then_inc(gates_live, 1)

            def rest_go_live(c):
                if later(c):
                    dve.wait_ge(row_added, ROWS * c)
                nc.vector.tensor_copy(experts[:, TABLE_PART:], experts_next[:, TABLE_PART:]).then_inc(experts_live, 1)

            def dot_row(c, e):
                if e == 0:
                    dve.wait_ge(taken, c + 1)
                if e % TOPK == 0 and later(c):
                    dve.wait_ge(gelued, PH * (c - 1) + e // TOPK + 1)
                dve.wait_ge(row_in["u"][e % RING], 16 * (FILLS * c + e // RING + 1))
                row = ring["u"][:, e % RING, :]
                nc.vector.tensor_tensor_reduce(out=row, in0=row, in1=hn[:, :],
                                               scale=1.0, scalar=0.0, op0=ALU.mult, op1=ALU.add,
                                               accum_out=dots[:, e:e + 1]).then_inc(dotted, 1)

            def weigh_rows(c, h):
                dve.wait_ge(gelued, PH * c + h + 1)
                if h == 0:
                    dve.wait_ge(gates_live, c + 1)
                if h or later(c):
                    dve.wait_ge(diagonal, 2 * (PH * c + h))
                at = slice(h * TOPK, (h + 1) * TOPK)
                nc.vector.tensor_tensor(weights[:, at], geld[:, at], gates[:, at], ALU.mult).then_inc(weighted, 1)

            def spread_weights(c, e):
                dve.wait_ge(weighted, PH * c + e // TOPK + 1)
                if e >= TOPK or later(c):
                    dve.wait_ge(row_added, ROWS * c + e - TOPK + HALF_ROWS)
                at = e % TOPK
                nc.vector.tensor_tensor(diag[:, at:at + HALF_ROWS, :], spread(ident[:, :], [[0, HALF_ROWS], [1, P]]),
                                        spread(weights[:, e:e + HALF_ROWS], [[1, HALF_ROWS], [0, P]]),
                                        ALU.mult).then_inc(diagonal, 1)

            def front(f, s, keys):
                a, after = divmod(s - ATT0 - ATT_SUM, ATT_STEP)
                if 0 <= a < HEADS and after == 0:
                    accumulate(f, a, keys)
                if TAP0 <= s < TAP0 + TAPS:
                    convolve(f, s - TAP0)
                if s == O_MEAN:
                    mean_o(f)
                if s == O_NORM:
                    norm_o(f)
                if s == LN_STAT:
                    ln_stats(f)
                if s == LN_SCALE:
                    ln_scale(f)
                if s == H_ADD:
                    add_residual(f)
                if s == H_MEAN:
                    mean_h(f)
                if s == H_NORM:
                    norm_h(f)
                if SEARCH <= s < SEARCH + 10:
                    search_keys(f, s - SEARCH)
                if CAND <= s < CAND + 3:
                    add_candidates(f, s - CAND)
                if BEST <= s < BEST + 10:
                    search_candidates(f, s - BEST)
                if s == SHIFT:
                    shift_gates(f)
                if s == SPLIT:
                    split_positions(f)
                if LOOK <= s < EXPERTS and (s - LOOK) % 2 == 0:
                    look_up(f, (s - LOOK) // 2)
                if s == EXPERTS:
                    number_experts(f)
                if s == GATES:
                    finish_gates(f)
                if s == TABLE_NEXT:
                    table_go_live(f)

            def step(c, f, keys):
                if c is not None:
                    hn_go_live(c)
                for s in range(SLOTS):
                    if c is not None:
                        dot_row(c, s)
                        h, after = divmod(s, TOPK)
                        h -= 1
                        if h >= 0 or later(c):
                            ch, h = (c, h) if h >= 0 else (c - 1, PH - 1)
                            if after == 1:
                                weigh_rows(ch, h)
                                spread_weights(ch, h * TOPK)
                            if after == HALF_ROWS:
                                spread_weights(ch, h * TOPK + HALF_ROWS)
                        if s == TOPK // 2 + 2:
                            gates_go_live(c)
                        if s == TABLE_SLOT:
                            rest_go_live(c)
                    if f is not None:
                        front(f, s, keys)

            over_chunks(dve, step)
            weigh_rows(CHUNKS - 1, PH - 1)
            spread_weights(CHUNKS - 1, ROWS - TOPK)
            spread_weights(CHUNKS - 1, ROWS - HALF_ROWS)


_INS = ["x", "norm_mix_g", "w_in", "q_norm_g", "k_norm_g", "attn_out_g", "conv_w", "conv_b", "conv_ln_g",
        "conv_ln_b", "w_out", "norm_ffn_g", "peer_wq", "peer_k1", "peer_k2", "peer_u", "peer_v"]


def kernel(**inputs):
    import concourse.bacc as _bacc
    from concourse.bass_utils import run_bass_kernel_spmd as _run

    nc = _bacc.Bacc("TRN2", target_bir_lowering=False, num_devices=1)
    arrays, args = {}, []
    for name in _INS:
        a = np.ascontiguousarray(inputs[name])
        arrays[f"in_{name}"] = a
        args.append(nc.dram_tensor(f"in_{name}", a.shape, mybir.dt.from_np(a.dtype), kind="ExternalInput").ap())
    args.append(nc.dram_tensor("out_0", [1, SEQ, D], F32, kind="ExternalOutput").ap())
    build(nc, *args)
    r = _run(nc, [arrays], core_ids=[0])
    return r.results[0]["out_0"]
```

```python
import numpy as np
import concourse.bass as bass
from concourse import mybir

F32 = mybir.dt.float32
BF16 = mybir.dt.bfloat16
I32 = mybir.dt.int32
U32 = mybir.dt.uint32
ALU = mybir.AluOpType
ACT = mybir.ActivationFunctionType
AXX = mybir.AxisListType.X

P = 128
SEQ, D = 1024, 1024
CHUNKS = SEQ // P
KT_D = D // P
HEADS, HD = 8, 64
AW = HEADS * HD
CW = D - AW
AB = AW // P
CB = CW // P
TAPS = 31
HALO = TAPS - 1
COLS = 3 * AW + 2 * CW
BANK = 512
PH, TOPK, NKEYS = 8, 16, 128
HALF = 64
ROWS = PH * TOPK
EPS = 1e-6
NEG = -1.0e30
LOWEST = -3.0e38
RING = 4
FILLS = ROWS // RING
LAG = 20
SLOTS = ROWS
TABLE_PART = 96
TABLE_SLOT = 28
assert LAG % RING == 0 and TABLE_PART <= ROWS - LAG and TABLE_SLOT > LAG

MASK_SPAN = SEQ - P

ATT0, ATT_STEP = 0, 5
ATT_SOFT, ATT_SUM, ATT_EXP = 2, 4, 5
ATT_T0, ATT_T1, ATT_USE = 6, 7, 8
ATT_END = ATT0 + ATT_STEP * (HEADS - 1) + ATT_USE
TAP_SLOTS = [s for s in range(ATT_END) if (s - ATT0 - ATT_SUM) % ATT_STEP][:TAPS]
FIRST_TAP_SLOTS = [LAG + t * (ATT_END - 1 - LAG) // TAPS for t in range(TAPS)]
CONV_T, LN_STAT, LN_SCALE, CONV_BACK = (ATT_END + n for n in (-1, 0, 2, 3))
O_MEAN, O_NORM, O_T = (ATT_END + n for n in (1, 2, 3))
MIX, MIX_SLOTS = ATT_END + 6, 14
H_ADD, H_MEAN, H_NORM, H_T = (MIX + MIX_SLOTS + n for n in (0, 1, 3, 4))
QUERY, QUERY_SLOTS = H_T + 2, 14
SCORE = QUERY + QUERY_SLOTS + 1
SEARCH = SCORE + 3
CAND = SEARCH + 10
BEST = CAND + 3
SHIFT, SPLIT, LOOK = BEST + 10, BEST + 10, BEST + 11
EXPERTS, GATES = LOOK + 8, LOOK + 9
TABLE_NEXT = GATES + 1
KEY_HALVES = 2 * PH
assert len(TAP_SLOTS) == TAPS and TAP_SLOTS[-1] < CONV_T and TABLE_PART + LAG < TABLE_NEXT < SLOTS


def spread(view, dims):
    return bass.AP(view.tensor, view.offset, [list(view.ap[0])] + [list(d) for d in dims])


def hold(eng, sem, value, passed):
    eng.wait_ge(sem, value)
    eng.sem_inc(passed, 1)


def heads_at(s, after):
    a, rest = divmod(s - ATT0 - after, ATT_STEP)
    return [a] if rest == 0 and 0 <= a < HEADS else []


def later(i):
    return not isinstance(i, int) or i > 0


class Shared:
    pass


class Map:

    def __init__(self, nc, start):
        self.nc, self.at = nc, (start + 31) // 32 * 32

    def tile(self, name, shape, dt):
        size = int(np.prod(shape[1:])) * (2 if dt == BF16 else 4)
        t = self.nc.alloc_sbuf_tensor_at(name, list(shape), dt, offset=self.at)
        self.at += (size + 31) // 32 * 32
        return t


def build(nc, x, norm_mix_g, w_in, q_norm_g, k_norm_g, attn_out_g, conv_w, conv_b, conv_ln_g,
          conv_ln_b, w_out, norm_ffn_g, peer_wq, peer_k1, peer_k2, peer_u, peer_v, out):
    keep = Map(nc, nc.sbuf_base)
    ident = keep.tile("ident", [P, P], F32)
    ident_b = keep.tile("ident_b", [P, P], BF16)
    mask_band = keep.tile("mask_band", [P, MASK_SPAN + SEQ], BF16)
    kT = keep.tile("kT", [P, AB, SEQ], F32)
    vals = keep.tile("vals", [P, CHUNKS, AW], F32)
    keys_bd = keep.tile("keys_bd", [P, PH, 2 * NKEYS], F32)
    NVEC = KT_D + 4 * CB + 2
    vec = keep.tile("vec", [P, NVEC], F32)
    iota16 = keep.tile("iota16", [P, TOPK], F32)
    taps = keep.tile("taps", [P, CB, TAPS], F32)
    w_kept = keep.tile("w_kept", [P, KT_D, D], F32)
    actT = keep.tile("actT", [P, KT_D, P], F32)
    qT = keep.tile("qT", [P, AB, P], F32)
    conv_in = keep.tile("conv_in", [P, CB, HALO + P], F32)
    acc = keep.tile("acc", [P, CB, P], F32)
    h_res = keep.tile("h_res", [P, D], F32)
    g_ffn = keep.tile("g_ffn", [P, D], F32)
    hn_next = keep.tile("hn_next", [P, D], F32)
    stat = keep.tile("stat", [P, 8], F32)
    gate_sum = keep.tile("gate_sum", [P, 2, PH], F32)
    late = Map(nc, keep.at)
    log_keep = [late.tile(f"log_keep{n}", [P, SEQ], F32) for n in range(2)]
    relu_z = [late.tile(f"relu_z{n}", [P, SEQ], F32) for n in range(2)]
    attT = late.tile("attT", [P, CHUNKS, P], F32)
    experts_next = late.tile("experts_next", [P, ROWS], I32)
    gates_next = late.tile("gates_next", [P, ROWS], F32)
    top_v = late.tile("top_v", [P, PH, 2, TOPK], F32)
    top_i = late.tile("top_i", [P, PH, 2, TOPK], U32)
    best_v = late.tile("best_v", [P, PH, TOPK], F32)
    best_i = late.tile("best_i", [P, PH, TOPK], U32)
    assert late.at - keep.at <= 2 * KT_D * BANK * 4
    wo_sb = late.tile("wo_sb", [P, KT_D, D], F32)
    g_mix = vec[:, 0:KT_D]
    g_attn = vec[:, KT_D:KT_D + AB]
    b_conv = vec[:, KT_D + AB:KT_D + 2 * AB]
    g_ln = vec[:, KT_D + 2 * AB:KT_D + 3 * AB]
    b_ln = vec[:, KT_D + 3 * AB:KT_D + 4 * AB]
    g_q = vec[:, NVEC - 2:NVEC - 1]
    g_k = vec[:, NVEC - 1:NVEC]

    qT_spill = nc.dram_tensor("qT_spill", [CHUNKS, P, AW], F32, kind="Internal").ap()
    hT_spill = nc.dram_tensor("hT_spill", [P, CB, HALO + SEQ], F32, kind="Internal").ap()
    psum = nc.alloc_psum_tensor("psum", [P, 8, BANK], F32)
    S = Shared()
    S.ident = ident
    S.actT = actT
    S.keys_bd = keys_bd
    S.iota16 = iota16
    S.h_res = h_res
    S.g_ffn = g_ffn
    S.hn_next = hn_next
    S.stat = stat
    S.gate_sum = gate_sum
    S.log_keep = log_keep
    S.relu_z = relu_z
    S.attT = attT
    S.experts_next = experts_next
    S.gates_next = gates_next
    S.top_v = top_v
    S.top_i = top_i
    S.best_v = best_v
    S.best_i = best_i
    S.qhT = log_keep[1][:, :].rearrange("p (h t) -> p h t", t=P)
    S.q_in = nc.alloc_semaphore("q_in")
    S.c_in = nc.alloc_semaphore("c_in")
    S.wo_loaded = nc.alloc_semaphore("wo_loaded")
    S.tapped = nc.alloc_semaphore("tapped")
    S.conv_T = nc.alloc_semaphore("conv_T")
    S.bn_done = nc.alloc_semaphore("bn_done")
    S.ln_done = nc.alloc_semaphore("ln_done")
    S.ln_eps = nc.alloc_semaphore("ln_eps")
    S.ln_rooted = nc.alloc_semaphore("ln_rooted")
    S.ln_recip = nc.alloc_semaphore("ln_recip")
    S.cn_done = nc.alloc_semaphore("cn_done")
    S.cT_ready = nc.alloc_semaphore("cT_ready")
    S.swished = nc.alloc_semaphore("swished")
    S.z_ready = nc.alloc_semaphore("z_ready")
    S.abs_done = nc.alloc_semaphore("abs_done")
    S.exp_done = nc.alloc_semaphore("exp_done")
    S.ln_done1 = nc.alloc_semaphore("ln_done1")
    S.relu_done = nc.alloc_semaphore("relu_done")
    S.summed = nc.alloc_semaphore("summed")
    S.stick = nc.alloc_semaphore("stick")
    S.att_done = nc.alloc_semaphore("att_done")
    S.att_T = nc.alloc_semaphore("att_T")
    S.att_copied = nc.alloc_semaphore("att_copied")
    S.attended = nc.alloc_semaphore("attended")
    S.o_squared = nc.alloc_semaphore("o_squared")
    S.o_meaned = nc.alloc_semaphore("o_meaned")
    S.o_rooted = nc.alloc_semaphore("o_rooted")
    S.o_recip = nc.alloc_semaphore("o_recip")
    S.o_normed = nc.alloc_semaphore("o_normed")
    S.o_T = nc.alloc_semaphore("o_T")
    S.o_copied = nc.alloc_semaphore("o_copied")
    S.wq_loaded = nc.alloc_semaphore("wq_loaded")
    S.g_loaded = nc.alloc_semaphore("g_loaded")
    S.x_in = nc.alloc_semaphore("x_in")
    S.mixed = nc.alloc_semaphore("mixed")
    S.h_done = nc.alloc_semaphore("h_done")
    S.h_squared = nc.alloc_semaphore("h_squared")
    S.h_meaned = nc.alloc_semaphore("h_meaned")
    S.h_rooted = nc.alloc_semaphore("h_rooted")
    S.h_recip = nc.alloc_semaphore("h_recip")
    S.h_normed = nc.alloc_semaphore("h_normed")
    S.h_T = nc.alloc_semaphore("h_T")
    S.h_copied = nc.alloc_semaphore("h_copied")
    S.queried = nc.alloc_semaphore("queried")
    S.queries_copied = nc.alloc_semaphore("queries_copied")
    S.scored = nc.alloc_semaphore("scored")
    S.top8 = nc.alloc_semaphore("top8")
    S.index8 = nc.alloc_semaphore("index8")
    S.replaced = nc.alloc_semaphore("replaced")
    S.top16 = nc.alloc_semaphore("top16")
    S.index16 = nc.alloc_semaphore("index16")
    S.top_floated = nc.alloc_semaphore("top_floated")
    S.cand_done = nc.alloc_semaphore("cand_done")
    S.best8 = nc.alloc_semaphore("best8")
    S.bindex8 = nc.alloc_semaphore("bindex8")
    S.breplaced = nc.alloc_semaphore("breplaced")
    S.best16 = nc.alloc_semaphore("best16")
    S.bindex16 = nc.alloc_semaphore("bindex16")
    S.split = nc.alloc_semaphore("split")
    S.split_f = nc.alloc_semaphore("split_f")
    S.matched = nc.alloc_semaphore("matched")
    S.picked = nc.alloc_semaphore("picked")
    S.looked = nc.alloc_semaphore("looked")
    S.experts_done = nc.alloc_semaphore("experts_done")
    S.g_shifted = nc.alloc_semaphore("g_shifted")
    S.g_exped = nc.alloc_semaphore("g_exped")
    S.g_summed = nc.alloc_semaphore("g_summed")
    S.g_recip = nc.alloc_semaphore("g_recip")
    S.gates_done = nc.alloc_semaphore("gates_done")
    S.taken = nc.alloc_semaphore("taken")
    S.experts_live = nc.alloc_semaphore("experts_live")
    S.gates_live = nc.alloc_semaphore("gates_live")
    S.dve_passed = nc.alloc_semaphore("dve_passed")

    phase0(nc, S, keep.at, psum, ident, ident_b, mask_band, kT, vals, keys_bd, w_kept, wo_sb, actT, qT,
           conv_in, acc, vec, iota16, taps, g_mix, g_attn, b_conv, g_ln, b_ln, g_q, g_k, qT_spill,
           hT_spill, x, norm_mix_g, w_in, q_norm_g, k_norm_g, attn_out_g, conv_w, conv_b, conv_ln_g,
           conv_ln_b, w_out, norm_ffn_g, peer_wq, peer_k1, peer_k2)
    phase1(nc, S, late.at, psum, ident, ident_b, mask_band, kT, vals, keys_bd, w_kept, wo_sb, actT, qT,
           conv_in, acc, iota16, taps, g_attn, b_conv, g_ln, b_ln, qT_spill, hT_spill, x,
           w_out, peer_u, peer_v, out)


def phase0(nc, S, base, psum, ident, ident_b, mask_band, kT, vals, keys_bd, w_kept, wo_sb, actT, qT,
           conv_in, acc, vec, iota16, taps, g_mix, g_attn, b_conv, g_ln, b_ln, g_q, g_k, qT_spill,
           hT_spill, x, norm_mix_g, w_in, q_norm_g, k_norm_g, attn_out_g, conv_w, conv_b, conv_ln_g,
           conv_ln_b, w_out, norm_ffn_g, peer_wq, peer_k1, peer_k2):
    m = Map(nc, base)
    GROUPS = COLS // BANK
    Q, K, V, A, G = range(GROUPS)
    ORDER = (Q, K, A, G, V)
    w_sb = m.tile("w_sb", [P, GROUPS, KT_D, BANK], F32)
    x_in = m.tile("x_in", [P, D], F32)
    xn = m.tile("xn", [P, D], F32)
    xnT = m.tile("xnT", [P, KT_D, P], F32)
    squares = m.tile("squares", [P, 2 * AW], F32)
    qn, kn = squares[:, 0:AW], squares[:, AW:]
    qT_out = m.tile("qT_out", [P, AW], F32)
    sig = m.tile("sig", [P, CW], F32)
    glu = m.tile("glu", [P, CW], F32)
    hT_out = m.tile("hT_out", [P, CB, P], F32)
    before = m.tile("before", [P, CB, HALO], F32)
    rows = m.tile("rows", [P, P], F32)
    taps_row = m.tile("taps_row", [TAPS, CW], F32)
    keys = S.h_res[:, :].rearrange("p (h a d) -> p h a d", h=PH, a=2)
    x_stat = m.tile("x_stat", [P, 4], F32)
    qk_stat = m.tile("qk_stat", [P, 4, 2 * HEADS], F32)
    soft = S.hn_next
    relu_attT = S.h_res
    bn = m.tile("first_bn", [P, 6], F32)
    ln_stat = m.tile("first_ln_stat", [P, 8], F32)
    assert m.at <= nc.sbuf_usable_end
    NVEC = vec.shape[1]

    ps = [psum[:, b, :] for b in (0, 1, 0, 4, 1)]
    z_ps = psum[:, 2:4, :].rearrange("p b n -> p (b n)")
    X, Y = psum[:, 2, :], psum[:, 3, :]
    tA, tB, tC = psum[:, 5, :], psum[:, 6, :], psum[:, 7, :]

    sem = nc.alloc_semaphore
    small_in, w_loaded = sem("small_in"), [sem(f"w_loaded{g}") for g in range(GROUPS)]
    x_loaded, consts, zeroed, setup_T, setup_copied = (
        sem("x_loaded"), sem("consts"), sem("zeroed"), sem("setup_T"), sem("setup_copied"))
    x_squared, x_meaned, x_rooted, x_recip, x_normed = (
        sem("x_squared"), sem("x_meaned"), sem("x_rooted"), sem("x_recip"), sem("x_normed"))
    xT_ready, xT_copied = sem("xT_ready"), sem("xT_copied")
    projected = [sem(f"projected{g}") for g in range(GROUPS)]
    qk_squared, qk_summed, qk_meaned, qk_rooted, qk_recip, q_normed, k_normed = (
        sem("qk_squared"), sem("qk_summed"), sem("qk_meaned"), sem("qk_rooted"), sem("qk_recip"),
        sem("q_normed"), sem("k_normed"))
    qT_ready, kT_ready, hT_ready = sem("qT_ready"), sem("kT_ready"), sem("hT_ready")
    qT_copied, kT_copied, hT_copied, v_copied = (
        sem("qT_copied"), sem("kT_copied"), sem("hT_copied"), sem("v_copied"))
    gated, glu_done = sem("gated"), sem("glu_done")
    qT_stored, hT_stored, zeros_stored = sem("qT_stored"), sem("hT_stored"), sem("zeros_stored")
    w_second = sem("w_second")
    keys_in, keys_T, keys_copied = sem("keys_in"), sem("keys_T"), sem("keys_copied")
    NSMALL = 8
    PENULT, LAST = CHUNKS - 2, CHUNKS - 1

    def xT(i):
        last = isinstance(i, int) and i == LAST
        return x_in[:, :].rearrange("p (k t) -> p k t", t=P) if last else xnT

    o_norm, cn = soft[:, 0:AW], soft[:, AW:]
    TAPS_EARLY = TAPS // 2

    def block_of(a):
        n = a % 2 * (HEADS // 2) + a // 2
        return slice(n * P, (n + 1) * P)

    with nc.Block() as block:

        @block.sync
        def _(sp):
            sp.dma_start(x_in[:, :], x[0, 0:P, :]).then_inc(x_loaded, 16)
            r = 0
            for v, n in ((norm_mix_g, KT_D), (attn_out_g, AB), (conv_b, CB), (conv_ln_g, CB),
                         (conv_ln_b, CB)):
                sp.dma_start(rows[r:r + n, :], v[0, :].rearrange("(n p) -> n p", p=P)).then_inc(small_in, 16)
                r += n
            for v in (q_norm_g, k_norm_g):
                sp.dma_start(rows[r:r + 1, :].rearrange("o (two d) -> o two d", two=2),
                             v[0:1, :].unsqueeze(1).to_broadcast([1, 2, HD])).then_inc(small_in, 16)
                r += 1
            sp.dma_start(taps_row[:, :], conv_w[0, :, :]).then_inc(small_in, 16)
            for g in ORDER:
                parts = 2 if g == Q else 1
                for n in range(parts):
                    k, rows_in = KT_D // parts, D // parts
                    sp.dma_start(w_sb[:, g, n * k:(n + 1) * k, :],
                                 w_in[0, n * rows_in:(n + 1) * rows_in, g * BANK:(g + 1) * BANK]
                                 .rearrange("(k p) n -> p k n", p=P)).then_inc(w_second if n else w_loaded[g], 16)
            for n, k in enumerate((peer_k1, peer_k2)):
                sp.dma_start(keys[:, :, n, :], k[0].rearrange("h n d -> n h d")).then_inc(keys_in, 16)

            def next_x(i):
                sp.wait_ge(x_normed, i + 1)
                sp.dma_start(x_in[:, :], x[0, bass.ds((i + 1) * P, P), :]).then_inc(x_loaded, 16)

            def store_q(i):
                sp.wait_ge(qT_copied, i + 1)
                sp.dma_start(qT_spill[bass.ds(i, 1), :, :].rearrange("o p n -> (o p) n"),
                             qT_out[:, :]).then_inc(qT_stored, 16)

            def store_h(i):
                sp.wait_ge(hT_copied, i + 1)
                sp.dma_start(hT_spill[:, :, bass.ds(i * P + HALO, P)], hT_out[:, :, :]).then_inc(hT_stored, 16)

            next_x(0)
            sp.wait_ge(zeroed, 6)
            sp.dma_start(hT_spill[:, :, 0:HALO], before[:, :, :]).then_inc(zeros_stored, 16)
            store_q(0)
            store_h(0)
            sp.wait_ge(qT_stored, 16)
            sp.dma_start(qT[:, :, :].rearrange("p b t -> p (b t)"), qT_spill[0]).then_inc(S.q_in, 16)
            sp.wait_ge(zeros_stored, 16)
            sp.wait_ge(hT_stored, 16)
            sp.dma_start(conv_in[:, :, :], hT_spill[:, :, 0:HALO + P]).then_inc(S.c_in, 16)
            sp.dma_start(w_kept[:, :, :], w_out[0].rearrange("(k p) n -> p k n", p=P)).then_inc(S.wo_loaded, 16)
            sp.dma_start(S.g_ffn[:, :], norm_ffn_g[0:1, :].to_broadcast([P, D])).then_inc(S.g_loaded, 16)
            with sp.Fori(1, CHUNKS - 3) as i:
                next_x(i)
                store_q(i)
                store_h(i)
            next_x(CHUNKS - 3)
            sp.wait_ge(S.attended, HEADS)
            sp.dma_start(S.h_res[:, :], x[0, 0:P, :]).then_inc(S.x_in, 16)
            store_q(CHUNKS - 3)
            store_h(CHUNKS - 3)
            next_x(PENULT)
            sp.wait_ge(S.mixed, 1)
            sp.dma_start(w_kept[:, :, :], peer_wq[0].rearrange("(k p) n -> p k n", p=P)).then_inc(S.wq_loaded, 16)
            store_q(PENULT)
            store_h(PENULT)
            store_q(LAST)
            sp.wait_ge(projected[V], CHUNKS)
            sp.dma_start(wo_sb[:, :, :], w_out[0].rearrange("(k p) n -> p k n", p=P)).then_inc(S.wo_loaded, 16)
            store_h(LAST)
            sp.wait_ge(qT_stored, 16 * CHUNKS)
            sp.wait_ge(hT_stored, 16 * CHUNKS)

        @block.gpsimd
        def _(pool):
            nc.gpsimd.memset(ident[:, :], 0.0).then_inc(zeroed, 1)
            nc.gpsimd.memset(mask_band[:, :], 0.0).then_inc(zeroed, 1)
            pool.wait_ge(zeroed, 2)
            nc.gpsimd.affine_select(out=ident[:, :], in_=ident[:, :], compare_op=ALU.not_equal, fill=1.0,
                                    base=0, pattern=[[-1, P]], channel_multiplier=1).then_inc(consts, 1)
            nc.gpsimd.affine_select(out=mask_band[:, :], in_=mask_band[:, :], compare_op=ALU.is_gt, fill=NEG,
                                    base=MASK_SPAN, pattern=[[-1, MASK_SPAN + SEQ]],
                                    channel_multiplier=1).then_inc(consts, 1)
            nc.gpsimd.iota(iota16[:, :], pattern=[[1, TOPK]], base=0, channel_multiplier=0,
                           allow_small_or_imprecise_dtypes=True).then_inc(consts, 1)
            pool.wait_ge(consts, 3)
            nc.gpsimd.tensor_copy(ident_b[:, :], ident[:, :]).then_inc(consts, 1)
            nc.gpsimd.memset(kT[:, :, :], 0.0).then_inc(zeroed, 1)
            nc.gpsimd.memset(vals[:, :, :], 0.0).then_inc(zeroed, 1)
            nc.gpsimd.memset(keys_bd[:, :, :], 0.0).then_inc(zeroed, 1)
            nc.gpsimd.memset(before[:, :, :], 0.0).then_inc(zeroed, 1)

        @block.tensor
        def _(pe):
            pe.wait_ge(consts, 4)
            pe.wait_ge(small_in, 16 * NSMALL)
            nc.tensor.transpose(tC[:, 0:NVEC], rows[0:NVEC, :], ident[0:NVEC, 0:NVEC])
            for c in range(CB):
                last = nc.tensor.transpose(tC[:, P + c * 32:P + c * 32 + TAPS],
                                           taps_row[:, c * P:(c + 1) * P], ident[0:TAPS, 0:TAPS])
            last.then_inc(setup_T, 1)

            def transpose_keys():
                pe.wait_ge(keys_in, 32)
                for h in range(PH):
                    last = nc.tensor.transpose((X, Y)[h // 4][:, (h % 4) * P:(h % 4 + 1) * P],
                                               keys[:, h, :, :].rearrange("p a d -> p (a d)"), ident[:, :])
                last.then_inc(keys_T, 1)

            def transpose_x(i):
                pe.wait_ge(x_normed, i + 1)
                if not isinstance(i, int) or i:
                    pe.wait_ge(qT_copied, i)
                    pe.wait_ge(kT_copied, i)
                for k in range(KT_D):
                    last = nc.tensor.transpose((tA, tB)[k // 4][:, (k % 4) * P:(k % 4 + 1) * P],
                                               xn[:, k * P:(k + 1) * P], ident[:, :])
                    if k % 4 == 3:
                        last.then_inc(xT_ready, 1)

            def project(i, g):
                if isinstance(i, int) and i == 0:
                    pe.wait_ge(w_loaded[g], 16)
                if isinstance(i, int) and i >= PENULT:
                    pe.wait_ge(*{Q: (q_normed, i) if i == LAST else (v_copied, i),
                                 K: (k_normed, i) if i == LAST else (gated, i),
                                 A: (glu_done, i),
                                 G: (gated, i) if i == LAST else (k_normed, LAST + 1),
                                 V: (v_copied, i) if i == LAST else (q_normed, LAST + 1)}[g])
                elif g == V:
                    pe.wait_ge(q_normed, i + 1)
                elif g == G:
                    pe.wait_ge(k_normed, i + 1)
                elif not isinstance(i, int) or i:
                    pe.wait_ge(*{Q: (v_copied, i), K: (gated, i), A: (glu_done, i)}[g])
                for k in range(KT_D):
                    if isinstance(i, int) and i == 0 and g == Q and k == KT_D // 2:
                        pe.wait_ge(w_second, 16)
                    if g == Q:
                        pe.wait_ge(xT_copied, KT_D * i + k + 1)
                    last = nc.tensor.matmul(ps[g], xT(i)[:, k, :], w_sb[:, g, k, :],
                                            start=k == 0, stop=k == KT_D - 1)
                last.then_inc(projected[g], 1)

            def transpose_qk(i):
                pe.wait_ge(xT_copied, KT_D * (i + 1))
                pe.wait_ge(q_normed, i + 1)
                for b in range(AB):
                    last = nc.tensor.transpose(tA[:, b * P:(b + 1) * P], qn[:, b * P:(b + 1) * P], ident[:, :])
                last.then_inc(qT_ready, 1)
                pe.wait_ge(k_normed, i + 1)
                for b in range(AB):
                    last = nc.tensor.transpose(tB[:, b * P:(b + 1) * P], kn[:, b * P:(b + 1) * P], ident[:, :])
                last.then_inc(kT_ready, 1)

            def transpose_glu(i):
                pe.wait_ge(setup_copied, 2)
                if not isinstance(i, int) or i:
                    pe.wait_ge(hT_copied, i)
                pe.wait_ge(glu_done, i + 1)
                for c in range(CB):
                    last = nc.tensor.transpose(tC[:, c * P:(c + 1) * P], glu[:, c * P:(c + 1) * P], ident[:, :])
                last.then_inc(hT_ready, 1)

            def first_scores():
                pe.wait_ge(S.q_in, 16)
                pe.wait_ge(keys_copied, 4)
                for a in range(HEADS):
                    lo = HD * (a % 2)
                    nc.tensor.matmul(z_ps[:, block_of(a)], qT[lo:lo + HD, a // 2, :],
                                     kT[lo:lo + HD, a // 2, 0:P], start=True, stop=False)
                    last = nc.tensor.matmul(z_ps[:, block_of(a)], ident_b[:, :],
                                            mask_band[:, MASK_SPAN:MASK_SPAN + P], start=False, stop=True)
                last.then_inc(S.z_ready, HEADS)

            def first_transpose_weights():
                pe.wait_ge(S.att_done, HEADS)
                for a in range(HEADS):
                    last = nc.tensor.transpose(z_ps[:, a * P:(a + 1) * P], soft[:, a * P:(a + 1) * P], ident[:, :])
                last.then_inc(S.att_T, 2 * HEADS)

            def first_attend():
                pe.wait_ge(S.att_copied, 2 * HEADS)
                pe.wait_ge(hT_copied, CHUNKS - 3)
                for a in range(HEADS):
                    last = nc.tensor.matmul(tC[:, a * HD:(a + 1) * HD], relu_attT[:, block_of(a)],
                                            vals[:, 0, a * HD:(a + 1) * HD], start=True, stop=True)
                last.then_inc(S.attended, HEADS)

            def first_transpose_conv():
                pe.wait_ge(S.tapped, TAPS * CB)
                for c in range(CB):
                    last = nc.tensor.transpose(X[:, c * P:(c + 1) * P], acc[:, c, :], ident[:, :])
                last.then_inc(S.conv_T, 1)

            def first_transpose_o():
                pe.wait_ge(S.o_normed, 1)
                for b in range(AB):
                    last = nc.tensor.transpose(Y[:, b * P:(b + 1) * P], o_norm[:, b * P:(b + 1) * P], ident[:, :])
                last.then_inc(S.o_T, 1)

            def first_transpose_conv_back():
                pe.wait_ge(S.cn_done, 1)
                for c in range(CB):
                    last = nc.tensor.transpose(tC[:, c * P:(c + 1) * P], cn[:, c * P:(c + 1) * P], ident[:, :])
                last.then_inc(S.cT_ready, 1)

            mix, transpose_h, query, score_keys = tensor_front(nc, pe, S, (z_ps, z_ps), w_kept, w_kept)

            def mix_first():
                for n in range(MIX_SLOTS):
                    mix(0, n)

            def query_first():
                for n in range(QUERY_SLOTS):
                    query(0, n)
                score_keys(0, 0)
                score_keys(0, 1)

            def score_first():
                score_keys(0, 2)
                score_keys(0, 3)

            def chunk(i, between={}):
                for g in ORDER:
                    project(i, g)
                    if g in between:
                        between[g]()
                    if g == G:
                        transpose_qk(i)
                if isinstance(i, int) and i == CHUNKS - 3:
                    pe.wait_ge(S.swished, CB)
                transpose_x(i + 1)
                transpose_glu(i)

            transpose_x(0)
            chunk(0)
            transpose_keys()
            with pe.Fori(1, CHUNKS - 4) as i:
                chunk(i)
            first_scores()
            chunk(CHUNKS - 4, {G: first_transpose_weights})
            chunk(CHUNKS - 3, {Q: first_attend, K: first_transpose_conv, A: first_transpose_o, G: first_transpose_conv_back})
            project(PENULT, Q)
            project(PENULT, K)
            mix_first()
            transpose_qk(PENULT)
            transpose_x(LAST)
            project(LAST, Q)
            transpose_h(0)
            project(LAST, K)
            query_first()
            project(PENULT, A)
            score_first()
            project(PENULT, G)
            project(PENULT, V)
            transpose_glu(PENULT)
            transpose_qk(LAST)
            for g in (A, V, G):
                project(LAST, g)
            transpose_glu(LAST)

        @block.scalar
        def _(act):
            def square_x(i):
                act.wait_ge(x_loaded, 16 * (i + 1))
                if not isinstance(i, int) or i:
                    act.wait_ge(xT_ready, 2 * i)
                    act.wait_ge(x_meaned, i)
                nc.scalar.activation(xn[:, :], x_in[:, :], ACT.Square, accum_out=x_stat[:, 0:1]).then_inc(x_squared, 1)

            def root_x(i):
                act.wait_ge(x_meaned, i + 1)
                if not isinstance(i, int) or i:
                    act.wait_ge(x_recip, i)
                nc.scalar.activation(x_stat[:, 2:3], x_stat[:, 1:2], ACT.Sqrt).then_inc(x_rooted, 1)

            def copy_xT(i):
                act.wait_ge(setup_copied, 2)
                if isinstance(i, int) and i == LAST:
                    act.wait_ge(x_normed, i + 1)
                elif not isinstance(i, int) or i:
                    act.wait_ge(projected[V], i)
                for k in range(KT_D):
                    if k % 4 == 0:
                        act.wait_ge(xT_ready, 2 * i + k // 4 + 1)
                    nc.scalar.activation(xT(i)[:, k, :], (tA, tB)[k // 4][:, (k % 4) * P:(k % 4 + 1) * P],
                                         ACT.Copy, scale=g_mix[:, k:k + 1]).then_inc(xT_copied, 1)

            def square_qk(i):
                if not isinstance(i, int) or i:
                    act.wait_ge(kT_ready, i)
                for n, g in enumerate((Q, K)):
                    act.wait_ge(projected[g], i + 1)
                    nc.scalar.activation(squares[:, n * AW:(n + 1) * AW], ps[g], ACT.Square).then_inc(qk_squared, 1)

            def gate(i):
                act.wait_ge(projected[G], i + 1)
                if not isinstance(i, int) or i:
                    act.wait_ge(glu_done, i)
                nc.scalar.activation(sig[:, :], ps[G], ACT.Sigmoid).then_inc(gated, 1)

            def root_qk(i):
                act.wait_ge(qk_meaned, 2 * (i + 1))
                if not isinstance(i, int) or i:
                    act.wait_ge(qk_recip, i)
                nc.scalar.activation(qk_stat[:, 2, :], qk_stat[:, 1, :], ACT.Sqrt).then_inc(qk_rooted, 1)

            def copy_v(i):
                act.wait_ge(projected[V], i + 1)
                act.wait_ge(zeroed, 6)
                nc.scalar.activation(vals[:, bass.ds(i, 1), :].rearrange("p o n -> p (o n)"), ps[V],
                                     ACT.Copy).then_inc(v_copied, 1)

            def copy_qk(i):
                act.wait_ge(qT_ready, i + 1)
                if not isinstance(i, int) or i:
                    act.wait_ge(qT_stored, 16 * i)
                nc.scalar.activation(qT_out[:, :], tA, ACT.Copy, scale=g_q).then_inc(qT_copied, 1)
                act.wait_ge(kT_ready, i + 1)
                act.wait_ge(zeroed, 6)
                nc.scalar.activation(kT[:, :, bass.ds(i * P, P)], tB.rearrange("p (b t) -> p b t", b=AB),
                                     ACT.Copy, scale=g_k).then_inc(kT_copied, 1)

            def copy_glu(i):
                act.wait_ge(hT_ready, i + 1)
                if not isinstance(i, int) or i:
                    act.wait_ge(hT_stored, 16 * i)
                nc.scalar.activation(hT_out[:, :, :], tC.rearrange("p (b t) -> p b t", b=CB),
                                     ACT.Copy).then_inc(hT_copied, 1)

            def first_soften():
                act.wait_ge(S.z_ready, HEADS)
                nc.scalar.activation(soft[:, :], z_ps, ACT.Abs).then_inc(S.abs_done, HEADS)
                nc.scalar.activation(relu_attT[:, :], z_ps, ACT.Relu).then_inc(S.relu_done, HEADS)
                act.wait_ge(S.abs_done, HEADS)
                nc.scalar.preload_act_table_set("natural_log_exp_and_others")
                nc.scalar.activation(soft[:, :], soft[:, :], ACT.Exp, scale=-1.0).then_inc(S.exp_done, HEADS)
                act.wait_ge(S.exp_done, HEADS)
                nc.scalar.activation(soft[:, :], soft[:, :], ACT.Ln, bias=1.0).then_inc(S.ln_done1, HEADS)

            def first_weigh():
                act.wait_ge(S.stick, HEADS)
                nc.scalar.activation(soft[:, :], soft[:, :], ACT.Exp).then_inc(S.att_done, HEADS)

            def first_copy_weights():
                act.wait_ge(S.att_T, 2 * HEADS)
                act.wait_ge(S.summed, HEADS)
                nc.scalar.activation(relu_attT[:, :], z_ps, ACT.Copy).then_inc(S.att_copied, 2 * HEADS)

            def first_rms():
                act.wait_ge(S.attended, HEADS)
                act.wait_ge(S.att_T, 2 * HEADS)
                nc.scalar.activation(o_norm, tC, ACT.Square, accum_out=S.stat[:, 0:1]).then_inc(S.o_squared, 1)
                act.wait_ge(S.o_meaned, 1)
                nc.scalar.activation(S.stat[:, 2:3], S.stat[:, 1:2], ACT.Sqrt).then_inc(S.o_rooted, 1)

            def first_copy_o():
                act.wait_ge(S.o_T, 1)
                for b in range(AB):
                    nc.scalar.activation(actT[:, b, :], Y[:, b * P:(b + 1) * P], ACT.Copy,
                                         scale=g_attn[:, b:b + 1]).then_inc(S.o_copied, 1)

            def first_root_ln():
                act.wait_ge(S.ln_eps, 1)
                nc.scalar.activation(ln_stat[:, 3:4], ln_stat[:, 2:3], ACT.Sqrt).then_inc(S.ln_rooted, 1)

            def first_swish():
                act.wait_ge(S.cT_ready, 1)
                for c in range(CB):
                    nc.scalar.activation(actT[:, AB + c, :], tC[:, c * P:(c + 1) * P], ACT.Silu,
                                         bias=b_ln[:, c:c + 1], scale=g_ln[:, c:c + 1]).then_inc(S.swished, 1)

            square_h, root_h, copy_h, copy_queries, exp_gates = scalar_front(nc, act, S, (z_ps, z_ps))

            def chunk(i, before_squares=(), before_gate=(), after_roots=()):
                for piece in before_squares:
                    piece()
                square_qk(i)
                root_qk(i)
                for piece in before_gate:
                    piece()
                gate(i)
                copy_qk(i)
                square_x(i + 1)
                root_x(i + 1)
                for piece in after_roots:
                    piece()
                copy_v(i)
                copy_xT(i + 1)
                copy_glu(i)

            nc.scalar.preload_act_table(ACT.Sqrt)
            square_x(0)
            root_x(0)
            copy_xT(0)
            chunk(0)
            with act.Fori(1, CHUNKS - 4) as i:
                chunk(i)
            chunk(CHUNKS - 4, before_squares=(first_soften,), before_gate=(first_weigh,),
                  after_roots=(first_copy_weights,))
            chunk(CHUNKS - 3, before_squares=(first_rms,), before_gate=(first_root_ln, first_copy_o),
                  after_roots=(first_swish,))
            square_x(LAST)
            root_x(LAST)
            square_qk(PENULT)
            root_qk(PENULT)
            copy_qk(PENULT)
            copy_xT(LAST)
            square_h(0)
            root_h(0)
            copy_h(0)
            square_qk(LAST)
            root_qk(LAST)
            copy_queries(0)
            gate(PENULT)
            copy_v(PENULT)
            copy_glu(PENULT)
            copy_qk(LAST)
            copy_v(LAST)
            gate(LAST)
            copy_glu(LAST)
            exp_gates(0)

        @block.vector
        def _(dve):
            def norm_x(i):
                dve.wait_ge(x_squared, i + 1)
                if not isinstance(i, int) or i:
                    dve.wait_ge(x_rooted, i)
                nc.vector.tensor_scalar(x_stat[:, 1:2], x_stat[:, 0:1], 1.0 / D, EPS, ALU.mult, ALU.add).then_inc(x_meaned, 1)
                dve.wait_ge(x_rooted, i + 1)
                if not isinstance(i, int) or i:
                    dve.wait_ge(x_normed, i)
                nc.vector.reciprocal(x_stat[:, 3:4], x_stat[:, 2:3]).then_inc(x_recip, 1)
                dve.wait_ge(x_recip, i + 1)
                nc.vector.tensor_scalar(xn[:, :], x_in[:, :], x_stat[:, 3:4], None, ALU.mult).then_inc(x_normed, 1)

            def norm_qk(i):
                dve.wait_ge(qk_squared, 2 * (i + 1))
                if not isinstance(i, int) or i:
                    dve.wait_ge(qk_meaned, 2 * i)
                nc.vector.reduce_sum(qk_stat[:, 0, :], squares[:, :].rearrange("p (h d) -> p h d", d=HD),
                                     AXX).then_inc(qk_summed, 1)
                dve.wait_ge(qk_summed, i + 1)
                if not isinstance(i, int) or i:
                    dve.wait_ge(qk_rooted, i)
                nc.vector.tensor_scalar(qk_stat[:, 1, 0:HEADS], qk_stat[:, 0, 0:HEADS], 1.0, HD * EPS,
                                        ALU.mult, ALU.add).then_inc(qk_meaned, 1)
                nc.vector.tensor_scalar(qk_stat[:, 1, HEADS:], qk_stat[:, 0, HEADS:], 1.0 / HD, EPS,
                                        ALU.mult, ALU.add).then_inc(qk_meaned, 1)

            def scale_qk(i):
                dve.wait_ge(qk_rooted, i + 1)
                if not isinstance(i, int) or i:
                    dve.wait_ge(k_normed, i)
                nc.vector.reciprocal(qk_stat[:, 3, :], qk_stat[:, 2, :]).then_inc(qk_recip, 1)
                dve.wait_ge(qk_recip, i + 1)
                for n, (g, to, done, used) in enumerate(((Q, qn, q_normed, qT_ready), (K, kn, k_normed, kT_ready))):
                    if not isinstance(i, int) or i:
                        dve.wait_ge(used, i)
                    nc.vector.tensor_tensor(to[:, :].rearrange("p (h d) -> p h d", d=HD),
                                            ps[g].rearrange("p (h d) -> p h d", d=HD),
                                            spread(qk_stat[:, 3, n * HEADS:], [[1, HEADS], [0, HD]]),
                                            ALU.mult).then_inc(done, 1)

            def glu_(i):
                dve.wait_ge(gated, i + 1)
                dve.wait_ge(projected[A], i + 1)
                if not isinstance(i, int) or i:
                    dve.wait_ge(hT_ready, i)
                nc.vector.tensor_tensor(glu[:, :], ps[A], sig[:, :], ALU.mult).then_inc(glu_done, 1)

            def first_accumulate():
                dve.wait_ge(S.ln_done1, HEADS)
                dve.wait_ge(S.relu_done, HEADS)
                for a in range(HEADS):
                    back = slice((a + 1) * P - 1, a * P - 1 if a else None, -1)
                    nc.vector.tensor_tensor_scan(soft[:, back], soft[:, back], relu_attT[:, back], 0.0,
                                                 ALU.add, ALU.add).then_inc(S.summed, 1)
                dve.wait_ge(S.summed, HEADS)
                nc.vector.tensor_tensor(soft[:, :], z_ps, soft[:, :], ALU.subtract).then_inc(S.stick, HEADS)

            def first_norm_o():
                dve.wait_ge(S.o_squared, 1)
                nc.vector.tensor_scalar(S.stat[:, 1:2], S.stat[:, 0:1], 1.0 / AW, EPS, ALU.mult, ALU.add).then_inc(S.o_meaned, 1)
                dve.wait_ge(S.o_rooted, 1)
                nc.vector.reciprocal(S.stat[:, 3:4], S.stat[:, 2:3]).then_inc(S.o_recip, 1)
                dve.wait_ge(S.o_recip, 1)
                nc.vector.tensor_scalar(o_norm, tC, S.stat[:, 3:4], None, ALU.mult).then_inc(S.o_normed, 1)

            def first_convolve(t):
                if t == 0:
                    dve.wait_ge(S.c_in, 16)
                else:
                    dve.wait_ge(S.tapped, t * CB)
                for c in range(CB):
                    if t == 0:
                        nc.vector.tensor_scalar(acc[:, c, :], conv_in[:, c, 0:P], taps[:, c, 0:1],
                                                b_conv[:, c:c + 1], ALU.mult, ALU.add).then_inc(S.tapped, 1)
                    else:
                        nc.vector.scalar_tensor_tensor(out=acc[:, c, :], in0=conv_in[:, c, t:t + P],
                                                       scalar=taps[:, c, t:t + 1], in1=acc[:, c, :],
                                                       op0=ALU.mult, op1=ALU.add).then_inc(S.tapped, 1)

            def first_ln():
                dve.wait_ge(S.conv_T, 1)
                nc.vector.bn_stats(bn[:, :], X).then_inc(S.bn_done, 1)
                hold(dve, S.bn_done, 1, S.dve_passed)
                nc.vector.bn_aggr(ln_stat[:, 0:2], bn[:, :]).then_inc(S.ln_done, 1)
                dve.wait_ge(S.ln_done, 1)
                nc.vector.tensor_scalar(ln_stat[:, 2:3], ln_stat[:, 1:2], 1.0, EPS, ALU.mult, ALU.add).then_inc(S.ln_eps, 1)
                dve.wait_ge(S.ln_rooted, 1)
                nc.vector.reciprocal(ln_stat[:, 4:5], ln_stat[:, 3:4]).then_inc(S.ln_recip, 1)
                dve.wait_ge(S.ln_recip, 1)
                nc.vector.tensor_scalar(cn, X, ln_stat[:, 0:1], ln_stat[:, 4:5],
                                        ALU.subtract, ALU.mult).then_inc(S.cn_done, 1)

            (add_residual, mean_h, norm_h, search_keys, add_candidates, search_candidates, shift_gates,
             split_positions, look_up, number_experts, _) = vector_front(nc, dve, S, (z_ps, z_ps))

            def search_first():
                for part in range(2):
                    for stage in range(5):
                        search_keys(0, 2 * stage + part)

            def chunk(i, after_scale=()):
                norm_qk(i)
                scale_qk(i)
                for piece in after_scale:
                    piece()
                glu_(i)
                norm_x(i + 1)

            norm_x(0)
            dve.wait_ge(setup_T, 1)
            nc.vector.tensor_copy(vec[:, :], tC[:, 0:NVEC]).then_inc(setup_copied, 1)
            nc.vector.tensor_copy(taps[:, :, :], tC[:, P:P + CB * 32].rearrange("p (c t) -> p c t", t=32)[:, :, 0:TAPS]).then_inc(setup_copied, 1)

            chunk(0)
            dve.wait_ge(keys_T, 1)
            dve.wait_ge(zeroed, 6)
            for half, (lo, hi) in enumerate(((0, HALF), (HALF, P))):
                for t, bank in enumerate((X, Y)):
                    nc.vector.tensor_copy(
                        keys_bd[lo:hi, 4 * t:4 * t + 4, half * NKEYS:(half + 1) * NKEYS],
                        bank[lo:hi, :].rearrange("p (h n) -> p h n", n=NKEYS)).then_inc(keys_copied, 1)
            dve.wait_ge(keys_copied, 4)
            with dve.Fori(1, CHUNKS - 4) as i:
                chunk(i)
            for t in range(TAPS_EARLY):
                first_convolve(t)
            first_accumulate()
            chunk(CHUNKS - 4)
            for t in range(TAPS_EARLY, TAPS):
                first_convolve(t)
            first_norm_o()
            chunk(CHUNKS - 3, after_scale=(first_ln,))
            norm_x(LAST)
            norm_qk(PENULT)
            scale_qk(PENULT)
            add_residual(0)
            mean_h(0)
            norm_h(0)
            norm_qk(LAST)
            scale_qk(LAST)
            search_first()
            glu_(PENULT)
            for n in range(3):
                add_candidates(0, n)
            for n in range(10):
                search_candidates(0, n)
            shift_gates(0)
            split_positions(0)
            look_up(0, 0)
            look_up(0, 1)
            look_up(0, 2)
            glu_(LAST)
            look_up(0, 3)
            number_experts(0)


def tensor_front(nc, pe, S, z, wo_sb, wq_sb):
    def mix(f, n):
        if n == 0:
            pe.wait_ge(S.stick, HEADS * (f + 1))
            pe.wait_ge(S.o_copied, AB * (f + 1))
            pe.wait_ge(S.swished, CB * (f + 1))
            pe.wait_ge(S.wo_loaded, 32 if later(f) else 16)
        total = 2 * KT_D
        for m in range(total * n // MIX_SLOTS, total * (n + 1) // MIX_SLOTS):
            j, k = m // KT_D, m % KT_D
            product = nc.tensor.matmul(z[0][:, j * BANK:(j + 1) * BANK], S.actT[:, k, :],
                                       wo_sb[:, k, j * BANK:(j + 1) * BANK], start=k == 0, stop=k == KT_D - 1)
            if m == total - 1:
                product.then_inc(S.mixed, 1)

    def transpose_h(f):
        pe.wait_ge(S.h_normed, f + 1)
        for k in range(KT_D):
            last = nc.tensor.transpose(z[1][:, k * P:(k + 1) * P], S.hn_next[:, k * P:(k + 1) * P], S.ident[:, :])
            if k % 4 == 3:
                last.then_inc(S.h_T, 1)

    def query(f, n):
        if n == 0:
            pe.wait_ge(S.h_copied, 2 * (f + 1))
            pe.wait_ge(S.h_done, f + 1)
            pe.wait_ge(S.wq_loaded, 16)
        total = PH * KT_D
        for m in range(total * n // QUERY_SLOTS, total * (n + 1) // QUERY_SLOTS):
            h, k = m // KT_D, m % KT_D
            product = nc.tensor.matmul(z[0][:, h * P:(h + 1) * P], wq_sb[:, k, h * P:(h + 1) * P],
                                       S.actT[:, k, :], start=k == 0, stop=k == KT_D - 1)
            if m == total - 1:
                product.then_inc(S.queried, 1)

    def score_keys(f, pair):
        pe.wait_ge(S.queries_copied, f + 1)
        if z[0] is z[1] and pair == 2:
            pe.wait_ge(S.replaced, KEY_HALVES * f + PH)
            pe.wait_ge(S.index8, KEY_HALVES * f + PH)
        for h in (2 * pair, 2 * pair + 1):
            last = nc.tensor.matmul(z[h // 4][:, (h % 4) * 2 * NKEYS:(h % 4 + 1) * 2 * NKEYS],
                                    S.qhT[:, h, :], S.keys_bd[:, h, :], start=True, stop=True)
        last.then_inc(S.scored, 1)

    return mix, transpose_h, query, score_keys


def scalar_front(nc, act, S, z):
    def square_h(f):
        act.wait_ge(S.h_done, f + 1)
        act.wait_ge(S.cT_ready, f + 1)
        if later(f):
            act.wait_ge(S.taken, f)
            act.wait_ge(S.h_meaned, f)
        nc.scalar.activation(S.hn_next[:, :], S.h_res[:, :], ACT.Square, accum_out=S.stat[:, 4:5]).then_inc(S.h_squared, 1)

    def root_h(f):
        act.wait_ge(S.h_meaned, f + 1)
        if later(f):
            act.wait_ge(S.h_recip, f)
        nc.scalar.activation(S.stat[:, 6:7], S.stat[:, 5:6], ACT.Sqrt).then_inc(S.h_rooted, 1)

    def copy_h(f):
        act.wait_ge(S.mixed, f + 1)
        for j in range(2):
            act.wait_ge(S.h_T, 2 * f + j + 1)
            nc.scalar.activation(S.actT[:, 4 * j:4 * j + 4, :],
                                 z[1][:, j * BANK:(j + 1) * BANK].rearrange("p (b t) -> p b t", t=P),
                                 ACT.Copy).then_inc(S.h_copied, 1)

    def copy_queries(f):
        act.wait_ge(S.queried, f + 1)
        nc.scalar.activation(S.qhT[:, :, :], z[0].rearrange("p (h t) -> p h t", t=P),
                             ACT.Copy).then_inc(S.queries_copied, 1)

    def exp_gates(f):
        act.wait_ge(S.g_shifted, f + 1)
        nc.scalar.activation(S.gates_next[:, :], S.gates_next[:, :], ACT.Exp).then_inc(S.g_exped, 1)

    return square_h, root_h, copy_h, copy_queries, exp_gates


def vector_front(nc, dve, S, z):
    def score(h, half):
        at = (h % 4) * 2 * NKEYS + half * NKEYS
        return z[h // 4][:, at:at + NKEYS]

    def left(h, half):
        n = 2 * h + half
        return S.relu_z[n // 8][:, (n % 8) * NKEYS:(n % 8 + 1) * NKEYS]

    cand = [S.log_keep[n][:, :].rearrange("p (h c) -> p h c", c=TOPK * TOPK) for n in range(2)]

    def add_residual(f):
        dve.wait_ge(S.mixed, f + 1)
        dve.wait_ge(S.x_in, 16 * (f + 1))
        nc.vector.tensor_tensor(S.h_res[:, :], z[0], S.h_res[:, :], ALU.add).then_inc(S.h_done, 1)

    def mean_h(f):
        dve.wait_ge(S.h_squared, f + 1)
        if later(f):
            dve.wait_ge(S.h_rooted, f)
        nc.vector.tensor_scalar(S.stat[:, 5:6], S.stat[:, 4:5], 1.0 / D, EPS, ALU.mult, ALU.add).then_inc(S.h_meaned, 1)

    def norm_h(f):
        dve.wait_ge(S.h_rooted, f + 1)
        if later(f):
            dve.wait_ge(S.h_normed, f)
        else:
            dve.wait_ge(S.g_loaded, 16)
        nc.vector.reciprocal(S.stat[:, 7:8], S.stat[:, 6:7]).then_inc(S.h_recip, 1)
        dve.wait_ge(S.h_recip, f + 1)
        nc.vector.scalar_tensor_tensor(out=S.hn_next[:, :], in0=S.h_res[:, :], scalar=S.stat[:, 7:8],
                                       in1=S.g_ffn[:, :], op0=ALU.mult, op1=ALU.mult).then_inc(S.h_normed, 1)

    def search_keys(f, n):
        stage, part = n // 2, n % 2
        halves = [(h, half) for h in range(4 * part, 4 * part + 4) for half in range(2)]
        ended = KEY_HALVES * f + PH * (part + 1)
        if stage == 0:
            if later(f):
                hold(dve, S.cand_done, 2 * f, S.dve_passed)
                hold(dve, S.top_floated, f, S.dve_passed)
            hold(dve, S.scored, 4 * f + 2 * part + 2, S.dve_passed)
            for h, half in halves:
                nc.vector.max(S.top_v[:, h, half, 0:8], score(h, half)).then_inc(S.top8, 1)
        elif stage == 1:
            hold(dve, S.top8, ended, S.dve_passed)
            for h, half in halves:
                nc.vector.max_index(S.top_i[:, h, half, 0:8], S.top_v[:, h, half, 0:8], score(h, half)).then_inc(S.index8, 1)
        elif stage == 2:
            for h, half in halves:
                nc.vector.match_replace(left(h, half), S.top_v[:, h, half, 0:8], score(h, half), LOWEST).then_inc(S.replaced, 1)
        elif stage == 3:
            hold(dve, S.replaced, ended, S.dve_passed)
            for h, half in halves:
                nc.vector.max(S.top_v[:, h, half, 8:16], left(h, half)).then_inc(S.top16, 1)
        else:
            hold(dve, S.top16, ended, S.dve_passed)
            for h, half in halves:
                nc.vector.max_index(S.top_i[:, h, half, 8:16], S.top_v[:, h, half, 8:16], left(h, half)).then_inc(S.index16, 1)

    tf = S.attT[:, 0:2, :].rearrange("p b t -> p (b t)").rearrange("p (h two k) -> p h two k", two=2, k=TOPK)
    parts_i = S.attT[:, 2:4, :].bitcast(U32).rearrange("p b t -> p (b t)")
    parts = S.attT[:, 4:6, :].rearrange("p b t -> p (b t)")
    looks = S.attT[:, 6:8, :].rearrange("p b t -> p (b t)")

    def add_candidates(f, n):
        if n == 0:
            dve.wait_ge(S.index16, KEY_HALVES * (f + 1))
            nc.vector.tensor_copy(tf, S.top_i[:, :, :, :]).then_inc(S.top_floated, 1)
            return
        j = n - 1
        dve.wait_ge(S.top16, KEY_HALVES * (f + 1))
        nc.vector.tensor_tensor(
            spread(cand[j], [[256, 4], [TOPK, TOPK], [1, TOPK]]),
            spread(S.top_v[:, 4 * j, 0, :], [[2 * TOPK, 4], [1, TOPK], [0, TOPK]]),
            spread(S.top_v[:, 4 * j, 1, :], [[2 * TOPK, 4], [0, TOPK], [1, TOPK]]), ALU.add).then_inc(S.cand_done, 1)

    def search_candidates(f, n):
        stage, part = n // 2, n % 2
        heads = range(4 * part, 4 * part + 4)
        ended = PH * f + 4 * (part + 1)
        if stage == 0:
            if part == 0 and later(f):
                hold(dve, S.split, 2 * f, S.dve_passed)
                hold(dve, S.g_shifted, f, S.dve_passed)
            hold(dve, S.cand_done, 2 * f + part + 1, S.dve_passed)
        else:
            hold(dve, (S.best8, S.bindex8, S.breplaced, S.best16)[stage - 1], ended, S.dve_passed)
        for h in heads:
            c = cand[h // 4][:, h % 4, :]
            if stage == 0:
                nc.vector.max(S.best_v[:, h, 0:8], c).then_inc(S.best8, 1)
            elif stage == 1:
                nc.vector.max_index(S.best_i[:, h, 0:8], S.best_v[:, h, 0:8], c).then_inc(S.bindex8, 1)
            elif stage == 2:
                nc.vector.match_replace(c, S.best_v[:, h, 0:8], c, LOWEST).then_inc(S.breplaced, 1)
            elif stage == 3:
                nc.vector.max(S.best_v[:, h, 8:16], c).then_inc(S.best16, 1)
            else:
                nc.vector.max_index(S.best_i[:, h, 8:16], S.best_v[:, h, 8:16], c).then_inc(S.bindex16, 1)

    def shift_gates(f):
        dve.wait_ge(S.best16, PH * (f + 1))
        if later(f):
            dve.wait_ge(S.gates_live, f)
        nc.vector.tensor_tensor(S.gates_next[:, :].rearrange("p (h k) -> p h k", k=TOPK), S.best_v[:, :, :],
                                spread(S.best_v[:, 0, 0:1], [[TOPK, PH], [0, TOPK]]), ALU.subtract).then_inc(S.g_shifted, 1)

    def split_positions(f):
        dve.wait_ge(S.bindex16, PH * (f + 1))
        pos = S.best_i[:, :, :].rearrange("p h k -> p (h k)")
        nc.vector.tensor_single_scalar(parts_i[:, 0:ROWS], pos, 4, ALU.logical_shift_right).then_inc(S.split, 1)
        nc.vector.tensor_single_scalar(parts_i[:, ROWS:], pos, TOPK - 1, ALU.bitwise_and).then_inc(S.split, 1)
        dve.wait_ge(S.split, 2 * (f + 1))
        nc.vector.tensor_copy(parts, parts_i).then_inc(S.split_f, 1)

    def look_up(f, n):
        half, j = n // 2, n % 2
        grid = spread(S.relu_z[j][:, :], [[256, 4], [TOPK, TOPK], [1, TOPK]])
        dve.wait_ge(S.split_f, f + 1)
        if half:
            dve.wait_ge(S.looked, 4 * f + j + 1)
        nc.vector.tensor_tensor(
            grid, spread(parts[:, half * ROWS + 4 * j * TOPK:], [[TOPK, 4], [1, TOPK], [0, TOPK]]),
            spread(S.iota16[:, :], [[0, 4], [0, TOPK], [1, TOPK]]), ALU.is_equal).then_inc(S.matched, 1)
        dve.wait_ge(S.matched, 4 * f + n + 1)
        nc.vector.tensor_tensor(
            grid, grid, spread(tf[:, 4 * j, half, :], [[2 * TOPK, 4], [0, TOPK], [1, TOPK]]),
            ALU.mult).then_inc(S.picked, 1)
        dve.wait_ge(S.picked, 4 * f + n + 1)
        at = half * ROWS + 4 * j * TOPK
        nc.vector.reduce_sum(looks[:, at:at + 4 * TOPK],
                             S.relu_z[j][:, :].rearrange("p (r s) -> p r s", s=TOPK), AXX).then_inc(S.looked, 1)

    def number_experts(f):
        dve.wait_ge(S.looked, 4 * (f + 1))
        if later(f):
            dve.wait_ge(S.experts_live, 2 * f)
        nc.vector.scalar_tensor_tensor(out=S.experts_next[:, :], in0=looks[:, 0:ROWS], scalar=float(NKEYS),
                                       in1=looks[:, ROWS:], op0=ALU.mult, op1=ALU.add).then_inc(S.experts_done, 1)

    def finish_gates(f):
        g = S.gates_next[:, :].rearrange("p (h k) -> p h k", k=TOPK)
        dve.wait_ge(S.g_exped, f + 1)
        nc.vector.reduce_sum(S.gate_sum[:, 0, :], g, AXX).then_inc(S.g_summed, 1)
        dve.wait_ge(S.g_summed, f + 1)
        nc.vector.reciprocal(S.gate_sum[:, 1, :], S.gate_sum[:, 0, :]).then_inc(S.g_recip, 1)
        dve.wait_ge(S.g_recip, f + 1)
        nc.vector.tensor_tensor(g, g, spread(S.gate_sum[:, 1, :], [[1, PH], [0, TOPK]]), ALU.mult).then_inc(S.gates_done, 1)

    return (add_residual, mean_h, norm_h, search_keys, add_candidates, search_candidates, shift_gates,
            split_positions, look_up, number_experts, finish_gates)


def phase1(nc, S, base, psum, ident, ident_b, mask_band, kT, vals, keys_bd, w_kept, wo_sb, actT, qT,
           conv_in, acc, iota16, taps, g_attn, b_conv, g_ln, b_ln, qT_spill, hT_spill, x,
           w_out, peer_u, peer_v, out):
    m = Map(nc, base)
    ring = {kind: m.tile(f"ring_{kind}", [P, RING, D], F32) for kind in "uv"}
    hn = m.tile("hn", [P, D], F32)
    y_out = m.tile("y_out", [P, D], F32)
    diag = m.tile("diag", [P, TOPK, P], F32)
    small = Map(nc, m.at)
    bn = small.tile("bn", [P, 6], F32)
    ln_stat = small.tile("ln_stat", [P, 8], F32)
    experts = small.tile("experts", [P, ROWS], I32)
    gates = small.tile("gates", [P, ROWS], F32)
    dots = small.tile("dots", [P, ROWS], F32)
    geld = small.tile("geld", [P, ROWS], F32)
    weights = small.tile("weights", [P, ROWS], F32)
    assert small.at <= nc.sbuf_usable_end

    o_norm = S.log_keep[0][:, 0:AW]
    cn = S.hn_next[:, 0:CW]

    y_ps = psum[:, 0:2, :].rearrange("p b n -> p (b n)")
    z_ps = [psum[:, 2 + 2 * n:4 + 2 * n, :].rearrange("p b n -> p (b n)") for n in range(2)]
    t_ps, o_ps = psum[:, 6, :], psum[:, 7, :]

    sem = nc.alloc_semaphore
    y_stored = sem("y_stored")
    TAP_OPS = TAPS * CB
    row_in = {kind: [sem(f"{kind}_in{n}") for n in range(RING)] for kind in "uv"}
    dotted, gelued, weighted, diagonal, y_begun, row_added, y_copied = (
        sem("dotted"), sem("gelued"), sem("weighted"), sem("diagonal"), sem("y_begun"),
        sem("row_added"), sem("y_copied"))

    pool_passed = sem("pool_passed")
    HALF_ROWS = TOPK // 2
    side_added = sem("side_added")
    SIDE = [e for e in range(ROWS - LAG, ROWS) if e % RING == RING - 1]
    y_side = S.hn_next

    def pe_rows(e):
        return ROWS * (CHUNKS - 1) + e + 1 - len([t for t in SIDE if t <= e])


    SPANS = ((0, 1, P), (1, 2, 2 * P), (2, 3, 4 * P), (3, CHUNKS, SEQ))

    def over_chunks(eng, step):
        step(None, 0, SPANS[0][2])
        for lo, hi, keys in SPANS[1:]:
            if hi - lo == 1:
                step(lo - 1, lo, keys)
            else:
                with eng.Fori(lo, hi) as f:
                    step(f - 1, f, keys)
        step(CHUNKS - 1, None, 0)

    with nc.Block() as block:

        @block.sync
        def _(sp):
            def load_front(f):
                if later(f):
                    sp.wait_ge(S.z_ready, HEADS * f)
                    sp.dma_start(qT[:, :, :].rearrange("p b t -> p (b t)"),
                                 qT_spill[bass.ds(f, 1), :, :].rearrange("o p n -> (o p) n")).then_inc(S.q_in, 16)
                    sp.wait_ge(S.tapped, TAP_OPS * f)
                    sp.dma_start(conv_in[:, :, :], hT_spill[:, :, bass.ds(f * P, HALO + P)]).then_inc(S.c_in, 16)
                    sp.wait_ge(y_begun, f)
                    sp.dma_start(S.h_res[:, :], x[0, bass.ds(f * P, P), :]).then_inc(S.x_in, 16)

            def store(c):
                sp.wait_ge(y_copied, c + 1)
                sp.dma_start(out[0, bass.ds(c * P, P), :], y_out[:, :]).then_inc(y_stored, 16)

            def step(c, f, keys):
                if f is not None:
                    load_front(f)
                if c is not None and later(c):
                    store(c - 1)

            over_chunks(sp, step)
            store(CHUNKS - 1)
            sp.wait_ge(y_stored, 16 * CHUNKS)

        @block.gpsimd
        def _(pool):
            def step(c, f, keys):
                if c is None:
                    return
                hold(pool, S.experts_live, 2 * c + 1, pool_passed)
                for s in range(SLOTS):
                    if s == TABLE_PART:
                        hold(pool, S.experts_live, 2 * c + 2, pool_passed)
                    gather("u", c, s)
                    if s >= LAG:
                        gather("v", c, s - LAG)
                    elif later(c):
                        gather("v", c - 1, s - LAG + ROWS)

            def gather(kind, c, e):
                if kind == "v" and isinstance(c, int) and c == CHUNKS - 1 and e >= ROWS - LAG:
                    if e - RING in SIDE:
                        hold(pool, side_added, SIDE.index(e - RING) + 1, pool_passed)
                    else:
                        hold(pool, row_added, pe_rows(e - RING), pool_passed)
                elif e >= RING or later(c):
                    hold(pool, dotted if kind == "u" else row_added, ROWS * c + e - RING + 1, pool_passed)
                nc.gpsimd.indirect_dma_start(
                    ring[kind][:, e % RING, :], None, peer_u[0] if kind == "u" else peer_v[0],
                    bass.IndirectOffsetOnAxis(experts[:, e:e + 1], 0)).then_inc(row_in[kind][e % RING], 16)

            def tail():
                for e in range(ROWS - LAG, ROWS):
                    gather("v", CHUNKS - 1, e)

            over_chunks(pool, step)
            tail()

        @block.tensor
        def _(pe):
            mix, transpose_h, query, score_keys = tensor_front(nc, pe, S, z_ps, wo_sb, w_kept)

            def scores(f, a, keys):
                z = z_ps[a % 2]
                if a == 0:
                    pe.wait_ge(S.q_in, 16 * (f + 1))
                if a < 2:
                    if later(f):
                        pe.wait_ge(S.replaced, KEY_HALVES * f)
                        pe.wait_ge(S.index8, KEY_HALVES * f)
                else:
                    pe.wait_ge(S.stick, HEADS * f + a - 1)
                lo = HD * (a % 2)
                for s in range(0, keys, BANK):
                    n = min(BANK, keys - s)
                    nc.tensor.matmul(z[:, s:s + n], qT[lo:lo + HD, a // 2, :], kT[lo:lo + HD, a // 2, s:s + n],
                                     start=True, stop=False)
                    last = nc.tensor.matmul(z[:, s:s + n], ident_b[:, :],
                                            mask_band[:, bass.ds(s + MASK_SPAN - f * P, n)],
                                            start=False, stop=True)
                last.then_inc(S.z_ready, 1)

            def transpose_weights(f, a, half, keys):
                blocks = keys // P
                pe.wait_ge(S.att_done, HEADS * f + a + 1)
                if a or half:
                    pe.wait_ge(S.att_copied, 2 * HEADS * f + 2 * a + half)
                elif later(f):
                    pe.wait_ge(S.o_copied, AB * f)
                for b in range(blocks // 2):
                    s = (half * blocks // 2 + b) * P
                    last = nc.tensor.transpose(t_ps[:, b * P:(b + 1) * P],
                                               S.log_keep[a % 2][:, s:s + P], ident[:, :])
                last.then_inc(S.att_T, 1)

            def attend(f, a, keys):
                blocks = keys // P
                if a == 0 and later(f):
                    pe.wait_ge(S.o_normed, f)
                for b in range(blocks):
                    if b in (0, blocks // 2):
                        pe.wait_ge(S.att_copied, 2 * HEADS * f + 2 * a + 1 + (b > 0))
                    last = nc.tensor.matmul(o_ps[:, a * HD:(a + 1) * HD], S.attT[:, b, :],
                                            vals[:, b, a * HD:(a + 1) * HD], start=b == 0, stop=b == blocks - 1)
                last.then_inc(S.attended, 1)

            def transpose_conv(f):
                pe.wait_ge(S.tapped, TAP_OPS * (f + 1))
                pe.wait_ge(S.stick, HEADS * (f + 1))
                for c in range(CB):
                    last = nc.tensor.transpose(z_ps[1][:, c * P:(c + 1) * P], acc[:, c, :], ident[:, :])
                last.then_inc(S.conv_T, 1)

            def transpose_conv_back(f):
                pe.wait_ge(S.cn_done, f + 1)
                for c in range(CB):
                    last = nc.tensor.transpose(z_ps[1][:, BANK + c * P:BANK + (c + 1) * P], cn[:, c * P:(c + 1) * P],
                                               ident[:, :])
                last.then_inc(S.cT_ready, 1)

            def transpose_o(f):
                pe.wait_ge(S.o_normed, f + 1)
                pe.wait_ge(S.att_copied, 2 * HEADS * (f + 1))
                for b in range(AB):
                    last = nc.tensor.transpose(t_ps[:, b * P:(b + 1) * P], o_norm[:, b * P:(b + 1) * P], ident[:, :])
                last.then_inc(S.o_T, 1)

            def begin_y(c):
                pe.wait_ge(S.h_done, c + 1)
                if later(c):
                    pe.wait_ge(y_copied, c)
                for j in range(2):
                    last = nc.tensor.matmul(y_ps[:, j * BANK:(j + 1) * BANK], ident[:, :],
                                            S.h_res[:, j * BANK:(j + 1) * BANK], start=True, stop=False)
                last.then_inc(y_begun, 1)

            def add_row(c, e):
                if e % HALF_ROWS == 0:
                    pe.wait_ge(diagonal, 2 * PH * c + e // HALF_ROWS + 1)
                pe.wait_ge(row_in["v"][e % RING], 16 * (FILLS * c + e // RING + 1))
                is_last = isinstance(c, int) and c == CHUNKS - 1
                for j in range(2):
                    last = nc.tensor.matmul(y_ps[:, j * BANK:(j + 1) * BANK], diag[:, e % TOPK, :],
                                            ring["v"][:, e % RING, j * BANK:(j + 1) * BANK], start=False,
                                            stop=e == ROWS - 1 or is_last and e == ROWS - 2)
                last.then_inc(row_added, 1)

            def front(f, s, keys):
                for a in heads_at(s, 0):
                    scores(f, a, keys)
                for a in heads_at(s, ATT_T0):
                    transpose_weights(f, a, 0, keys)
                for a in heads_at(s, ATT_T1):
                    transpose_weights(f, a, 1, keys)
                for a in heads_at(s, ATT_USE):
                    attend(f, a, keys)
                if s == CONV_T:
                    transpose_conv(f)
                if s == O_T:
                    transpose_o(f)
                if s == CONV_BACK:
                    transpose_conv_back(f)
                if MIX <= s < MIX + MIX_SLOTS:
                    mix(f, s - MIX)
                if s == H_T:
                    transpose_h(f)
                if QUERY <= s < QUERY + QUERY_SLOTS:
                    query(f, s - QUERY)
                if SCORE <= s < SCORE + 4:
                    score_keys(f, s - SCORE)

            def step(c, f, keys):
                for s in range(SLOTS):
                    if c is not None:
                        if s < LAG and later(c):
                            add_row(c - 1, s - LAG + ROWS)
                        if s == LAG:
                            begin_y(c)
                        if s >= LAG:
                            add_row(c, s - LAG)
                    if f is not None and later(f):
                        front(f, s, keys)

            over_chunks(pe, step)
            for e in range(ROWS - LAG, ROWS):
                if e not in SIDE:
                    add_row(CHUNKS - 1, e)

        @block.scalar
        def _(act):
            square_h, root_h, copy_h, copy_queries, exp_gates = scalar_front(nc, act, S, z_ps)

            def soften(f, a, keys):
                z, l, r = z_ps[a % 2][:, 0:keys], S.log_keep[a % 2][:, 0:keys], S.relu_z[a % 2][:, 0:keys]
                act.wait_ge(S.z_ready, HEADS * f + a + 1)
                if a >= 2:
                    act.wait_ge(S.att_T, 2 * (HEADS * f + a - 1))
                    act.wait_ge(S.summed, HEADS * f + a - 1)
                elif later(f):
                    act.wait_ge(S.looked, 4 * f)
                    act.wait_ge(S.bindex16, PH * f)
                nc.scalar.activation(l, z, ACT.Abs).then_inc(S.abs_done, 1)
                nc.scalar.activation(r, z, ACT.Relu).then_inc(S.relu_done, 1)
                act.wait_ge(S.abs_done, HEADS * f + a + 1)
                nc.scalar.activation(l, l, ACT.Exp, scale=-1.0).then_inc(S.exp_done, 1)
                act.wait_ge(S.exp_done, HEADS * f + a + 1)
                nc.scalar.activation(l, l, ACT.Ln, bias=1.0).then_inc(S.ln_done1, 1)

            def weigh(f, a, keys):
                act.wait_ge(S.stick, HEADS * f + a + 1)
                l = S.log_keep[a % 2][:, 0:keys]
                nc.scalar.activation(l, l, ACT.Exp).then_inc(S.att_done, 1)

            def copy_weights(f, a, half, keys):
                blocks = keys // P // 2
                if half == 0 and (a or later(f)):
                    act.wait_ge(S.attended, HEADS * f + a)
                if half == 0 and a == 0 and later(f):
                    act.wait_ge(S.experts_done, f)
                act.wait_ge(S.att_T, 2 * (HEADS * f + a) + half + 1)
                nc.scalar.activation(S.attT[:, half * blocks:(half + 1) * blocks, :],
                                     t_ps[:, 0:blocks * P].rearrange("p (b t) -> p b t", t=P),
                                     ACT.Copy).then_inc(S.att_copied, 1)

            def square_o(f):
                act.wait_ge(S.attended, HEADS * (f + 1))
                act.wait_ge(S.att_T, 2 * HEADS * (f + 1))
                if later(f):
                    act.wait_ge(S.o_meaned, f)
                nc.scalar.activation(o_norm, o_ps, ACT.Square, accum_out=S.stat[:, 0:1]).then_inc(S.o_squared, 1)

            def root_o(f):
                act.wait_ge(S.o_meaned, f + 1)
                if later(f):
                    act.wait_ge(S.o_recip, f)
                nc.scalar.activation(S.stat[:, 2:3], S.stat[:, 1:2], ACT.Sqrt).then_inc(S.o_rooted, 1)

            def copy_o(f):
                act.wait_ge(S.o_T, f + 1)
                if later(f):
                    act.wait_ge(S.queried, f)
                for b in range(AB):
                    nc.scalar.activation(actT[:, b, :], t_ps[:, b * P:(b + 1) * P], ACT.Copy,
                                         scale=g_attn[:, b:b + 1]).then_inc(S.o_copied, 1)

            def root_ln(f):
                act.wait_ge(S.ln_eps, f + 1)
                if later(f):
                    act.wait_ge(S.ln_recip, f)
                nc.scalar.activation(ln_stat[:, 3:4], ln_stat[:, 2:3], ACT.Sqrt).then_inc(S.ln_rooted, 1)

            def swish(f):
                act.wait_ge(S.cT_ready, f + 1)
                if later(f):
                    act.wait_ge(S.queried, f)
                for c in range(CB):
                    nc.scalar.activation(actT[:, AB + c, :], z_ps[1][:, BANK + c * P:BANK + (c + 1) * P], ACT.Silu,
                                         bias=b_ln[:, c:c + 1], scale=g_ln[:, c:c + 1]).then_inc(S.swished, 1)

            def gelu(c, w):
                act.wait_ge(dotted, ROWS * c + TOPK * (w + 1))
                if w or later(c):
                    act.wait_ge(weighted, PH * c + w)
                nc.scalar.activation(geld[:, w * TOPK:(w + 1) * TOPK], dots[:, w * TOPK:(w + 1) * TOPK],
                                     ACT.Gelu).then_inc(gelued, 1)

            def copy_y(c):
                act.wait_ge(row_added, ROWS * (c + 1))
                if later(c):
                    act.wait_ge(y_stored, 16 * c)
                nc.scalar.activation(y_out[:, :], y_ps, ACT.Copy).then_inc(y_copied, 1)

            def front(f, s, keys):
                for a in heads_at(s, ATT_T0):
                    copy_weights(f, a, 0, keys)
                for a in heads_at(s, ATT_T1):
                    copy_weights(f, a, 1, keys)
                for a in heads_at(s, ATT_SOFT):
                    soften(f, a, keys)
                for a in heads_at(s, ATT_EXP):
                    weigh(f, a, keys)
                if s == ATT_END:
                    square_o(f)
                if s == O_MEAN:
                    root_o(f)
                if s == LN_STAT + 1:
                    root_ln(f)
                if s == O_T:
                    copy_o(f)
                if s == CONV_BACK:
                    swish(f)
                if s == H_ADD:
                    square_h(f)
                if s == H_MEAN:
                    root_h(f)
                if s == H_T:
                    copy_h(f)
                if s == QUERY + QUERY_SLOTS:
                    copy_queries(f)
                if s == SHIFT:
                    exp_gates(f)

            def step(c, f, keys):
                for s in range(SLOTS):
                    if c is not None:
                        if s == 0 and later(c):
                            gelu(c - 1, PH - 1)
                        if s % TOPK == 0 and s > 0:
                            gelu(c, s // TOPK - 1)
                        if s == LAG and later(c):
                            copy_y(c - 1)
                    if f is not None and later(f):
                        if s % TOPK == 0 and s < ATT_END:
                            nc.scalar.preload_act_table_set("natural_log_exp_and_others")
                        front(f, s, keys)

            over_chunks(act, step)
            gelu(CHUNKS - 1, PH - 1)

        @block.vector
        def _(dve):
            (add_residual, mean_h, norm_h, search_keys, add_candidates, search_candidates, shift_gates,
             split_positions, look_up, number_experts, finish_gates) = vector_front(nc, dve, S, z_ps)

            def accumulate(f, a, keys):
                l, r = S.log_keep[a % 2], S.relu_z[a % 2]
                dve.wait_ge(S.ln_done1, HEADS * f + a + 1)
                dve.wait_ge(S.relu_done, HEADS * f + a + 1)
                back = slice(keys - 1, None, -1)
                nc.vector.tensor_tensor_scan(l[:, back], l[:, back], r[:, back], 0.0, ALU.add, ALU.add).then_inc(S.summed, 1)
                dve.wait_ge(S.summed, HEADS * f + a + 1)
                nc.vector.tensor_tensor(l[:, 0:keys], z_ps[a % 2][:, 0:keys], l[:, 0:keys], ALU.subtract).then_inc(S.stick, 1)

            def mean_o(f):
                dve.wait_ge(S.o_squared, f + 1)
                if later(f):
                    dve.wait_ge(S.o_rooted, f)
                nc.vector.tensor_scalar(S.stat[:, 1:2], S.stat[:, 0:1], 1.0 / AW, EPS, ALU.mult, ALU.add).then_inc(S.o_meaned, 1)

            def norm_o(f):
                dve.wait_ge(S.o_rooted, f + 1)
                if later(f):
                    dve.wait_ge(S.o_normed, f)
                nc.vector.reciprocal(S.stat[:, 3:4], S.stat[:, 2:3]).then_inc(S.o_recip, 1)
                dve.wait_ge(S.o_recip, f + 1)
                nc.vector.tensor_scalar(o_norm, o_ps, S.stat[:, 3:4], None, ALU.mult).then_inc(S.o_normed, 1)

            def convolve(f, t):
                if t == 0:
                    dve.wait_ge(S.c_in, 16 * (f + 1))
                    if later(f):
                        dve.wait_ge(S.conv_T, f)
                else:
                    dve.wait_ge(S.tapped, TAP_OPS * f + t * CB)
                for c in range(CB):
                    if t == 0:
                        nc.vector.tensor_scalar(acc[:, c, :], conv_in[:, c, 0:P], taps[:, c, 0:1],
                                                b_conv[:, c:c + 1], ALU.mult, ALU.add).then_inc(S.tapped, 1)
                    else:
                        nc.vector.scalar_tensor_tensor(out=acc[:, c, :], in0=conv_in[:, c, t:t + P],
                                                       scalar=taps[:, c, t:t + 1], in1=acc[:, c, :],
                                                       op0=ALU.mult, op1=ALU.add).then_inc(S.tapped, 1)

            def ln_stats(f):
                dve.wait_ge(S.conv_T, f + 1)
                if later(f):
                    dve.wait_ge(S.ln_done, f)
                nc.vector.bn_stats(bn[:, :], z_ps[1][:, 0:CW]).then_inc(S.bn_done, 1)
                if later(f):
                    hold(dve, S.cn_done, f, S.dve_passed)
                hold(dve, S.bn_done, f + 1, S.dve_passed)
                nc.vector.bn_aggr(ln_stat[:, 0:2], bn[:, :]).then_inc(S.ln_done, 1)
                dve.wait_ge(S.ln_done, f + 1)
                if later(f):
                    dve.wait_ge(S.ln_rooted, f)
                nc.vector.tensor_scalar(ln_stat[:, 2:3], ln_stat[:, 1:2], 1.0, EPS, ALU.mult, ALU.add).then_inc(S.ln_eps, 1)

            def ln_scale(f):
                dve.wait_ge(S.ln_rooted, f + 1)
                nc.vector.reciprocal(ln_stat[:, 4:5], ln_stat[:, 3:4]).then_inc(S.ln_recip, 1)
                dve.wait_ge(S.ln_recip, f + 1)
                if later(f):
                    dve.wait_ge(S.taken, f)
                    dve.wait_ge(S.h_T, 2 * f)
                nc.vector.tensor_scalar(cn, z_ps[1][:, 0:CW], ln_stat[:, 0:1], ln_stat[:, 4:5],
                                        ALU.subtract, ALU.mult).then_inc(S.cn_done, 1)

            def table_go_live(c):
                dve.wait_ge(S.experts_done, c + 1)
                if later(c):
                    dve.wait_ge(dotted, ROWS * (c - 1) + TABLE_PART)
                    dve.wait_ge(row_added, ROWS * (c - 1) + TABLE_PART)
                nc.vector.tensor_copy(experts[:, 0:TABLE_PART], S.experts_next[:, 0:TABLE_PART]).then_inc(S.experts_live, 1)

            def hn_go_live(c):
                dve.wait_ge(S.h_normed, c + 1)
                if later(c):
                    dve.wait_ge(dotted, ROWS * c)
                nc.vector.tensor_copy(hn[:, :], S.hn_next[:, :]).then_inc(S.taken, 1)

            def gates_go_live(c):
                dve.wait_ge(S.gates_done, c + 1)
                if later(c):
                    dve.wait_ge(weighted, PH * c)
                nc.vector.tensor_copy(gates[:, :], S.gates_next[:, :]).then_inc(S.gates_live, 1)

            def rest_go_live(c):
                if later(c):
                    dve.wait_ge(row_added, ROWS * c)
                nc.vector.tensor_copy(experts[:, TABLE_PART:], S.experts_next[:, TABLE_PART:]).then_inc(S.experts_live, 1)

            def dot_row(c, e):
                if e == 0:
                    dve.wait_ge(S.taken, c + 1)
                if e % TOPK == 0 and later(c):
                    dve.wait_ge(gelued, PH * (c - 1) + e // TOPK + 1)
                dve.wait_ge(row_in["u"][e % RING], 16 * (FILLS * c + e // RING + 1))
                row = ring["u"][:, e % RING, :]
                nc.vector.tensor_tensor_reduce(out=row, in0=row, in1=hn[:, :],
                                               scale=1.0, scalar=0.0, op0=ALU.mult, op1=ALU.add,
                                               accum_out=dots[:, e:e + 1]).then_inc(dotted, 1)

            def weigh_rows(c, h):
                dve.wait_ge(gelued, PH * c + h + 1)
                if h == 0:
                    dve.wait_ge(S.gates_live, c + 1)
                if h or later(c):
                    dve.wait_ge(diagonal, 2 * (PH * c + h))
                at = slice(h * TOPK, (h + 1) * TOPK)
                nc.vector.tensor_tensor(weights[:, at], geld[:, at], gates[:, at], ALU.mult).then_inc(weighted, 1)

            def spread_weights(c, e):
                dve.wait_ge(weighted, PH * c + e // TOPK + 1)
                if isinstance(c, int) and c == CHUNKS - 1 and e == ROWS - HALF_ROWS:
                    dve.wait_ge(row_added, pe_rows(e - TOPK + HALF_ROWS - 1))
                elif e >= TOPK or later(c):
                    dve.wait_ge(row_added, ROWS * c + e - TOPK + HALF_ROWS)
                at = e % TOPK
                nc.vector.tensor_tensor(diag[:, at:at + HALF_ROWS, :], spread(ident[:, :], [[0, HALF_ROWS], [1, P]]),
                                        spread(weights[:, e:e + HALF_ROWS], [[1, HALF_ROWS], [0, P]]),
                                        ALU.mult).then_inc(diagonal, 1)

            def add_row_aside(n, e):
                row = ring["v"][:, e % RING, :]
                dve.wait_ge(row_in["v"][e % RING], 16 * (FILLS * (CHUNKS - 1) + e // RING + 1))
                if n == 0:
                    nc.vector.tensor_scalar(y_side[:, :], row, weights[:, e:e + 1], None, ALU.mult).then_inc(side_added, 1)
                else:
                    dve.wait_ge(side_added, n)
                    nc.vector.scalar_tensor_tensor(out=y_side[:, :], in0=row, scalar=weights[:, e:e + 1],
                                                   in1=y_side[:, :], op0=ALU.mult, op1=ALU.add).then_inc(side_added, 1)

            def end_y():
                dve.wait_ge(row_added, pe_rows(ROWS - 1))
                dve.wait_ge(side_added, len(SIDE))
                dve.wait_ge(y_stored, 16 * (CHUNKS - 1))
                nc.vector.tensor_tensor(y_out[:, :], y_ps, y_side[:, :], ALU.add).then_inc(y_copied, 1)

            def front(f, s, keys):
                for a in heads_at(s, ATT_SUM):
                    accumulate(f, a, keys)
                for t, at in enumerate(FIRST_TAP_SLOTS if isinstance(f, int) and f == 1 else TAP_SLOTS):
                    if s == at:
                        convolve(f, t)
                if s == O_MEAN:
                    mean_o(f)
                if s == O_NORM:
                    norm_o(f)
                if s == LN_STAT:
                    ln_stats(f)
                if s == LN_SCALE:
                    ln_scale(f)
                if s == H_ADD:
                    add_residual(f)
                if s == H_MEAN:
                    mean_h(f)
                if s == H_NORM:
                    norm_h(f)
                if SEARCH <= s < SEARCH + 10:
                    search_keys(f, s - SEARCH)
                if CAND <= s < CAND + 3:
                    add_candidates(f, s - CAND)
                if BEST <= s < BEST + 10:
                    search_candidates(f, s - BEST)
                if s == SHIFT:
                    shift_gates(f)
                if s == SPLIT:
                    split_positions(f)
                if LOOK <= s < EXPERTS and (s - LOOK) % 2 == 0:
                    look_up(f, (s - LOOK) // 2)
                if s == EXPERTS:
                    number_experts(f)
                if s == GATES:
                    finish_gates(f)
            def step(c, f, keys):
                if c is not None:
                    hn_go_live(c)
                for s in range(SLOTS):
                    if c is not None:
                        dot_row(c, s)
                        h, after = divmod(s, TOPK)
                        h -= 1
                        if h >= 0 or later(c):
                            ch, h = (c, h) if h >= 0 else (c - 1, PH - 1)
                            if after == 1:
                                weigh_rows(ch, h)
                                spread_weights(ch, h * TOPK)
                            if after == HALF_ROWS:
                                spread_weights(ch, h * TOPK + HALF_ROWS)
                        if s == TOPK // 2 + 2:
                            gates_go_live(c)
                        if s == TABLE_SLOT:
                            rest_go_live(c)
                    if f is not None and later(f):
                        front(f, s, keys)
                    if f is not None and s == TABLE_NEXT:
                        table_go_live(f)
                        if not later(f):
                            finish_gates(f)

            over_chunks(dve, step)
            weigh_rows(CHUNKS - 1, PH - 1)
            spread_weights(CHUNKS - 1, ROWS - TOPK)
            for n, e in enumerate(SIDE):
                add_row_aside(n, e)
                if n == 0:
                    spread_weights(CHUNKS - 1, ROWS - HALF_ROWS)
            end_y()


_INS = ["x", "norm_mix_g", "w_in", "q_norm_g", "k_norm_g", "attn_out_g", "conv_w", "conv_b", "conv_ln_g",
        "conv_ln_b", "w_out", "norm_ffn_g", "peer_wq", "peer_k1", "peer_k2", "peer_u", "peer_v"]


def kernel(**inputs):
    import concourse.bacc as _bacc
    from concourse.bass_utils import run_bass_kernel_spmd as _run

    nc = _bacc.Bacc("TRN2", target_bir_lowering=False, num_devices=1)
    arrays, args = {}, []
    for name in _INS:
        a = np.ascontiguousarray(inputs[name])
        arrays[f"in_{name}"] = a
        args.append(nc.dram_tensor(f"in_{name}", a.shape, mybir.dt.from_np(a.dtype), kind="ExternalInput").ap())
    args.append(nc.dram_tensor("out_0", [1, SEQ, D], F32, kind="ExternalOutput").ap())
    build(nc, *args)
    r = _run(nc, [arrays], core_ids=[0])
    return r.results[0]["out_0"]
```
